# Optimizing a Trainium2 kernel written in Bass

```python
import jax, jax.numpy as jnp
from jax import lax
import numpy as np

D_MODEL = 1024
BATCH = 1
SEQ = 2048
DEPTH = 1
DEC_BATCH = 8
DEC_SEQ = 1
PAST_LEN = 2048
PAGE_SIZE = 128

N_MEM = 256
FOX_HEADS = 8
FOX_HEAD_DIM = 64
FOX_WIDTH = FOX_HEADS * FOX_HEAD_DIM
HG_HEADS = 4
HG_HEAD_DIM = 128
HG_WIDTH = HG_HEADS * HG_HEAD_DIM
MEM_HEADS = 4
MEM_HEAD_DIM = 128
MEM_WIDTH = MEM_HEADS * MEM_HEAD_DIM
N_BRANCH = 3
Q_BLOCK = 128
HG_CHUNK = 64
FGATE_BIAS_LO = 2.0
FGATE_BIAS_HI = 10.0
RMS_EPS = 1e-6
IN_SIZES = (FOX_WIDTH, FOX_WIDTH, FOX_WIDTH, FOX_HEADS, FOX_WIDTH,
            HG_WIDTH, HG_WIDTH, HG_WIDTH, HG_WIDTH,
            MEM_WIDTH, MEM_WIDTH,
            D_MODEL, D_MODEL, D_MODEL)
N_IN = sum(IN_SIZES)

kernel_name = 'fox_hgrn2_memxattn_gated_hybrid_step'

F32 = jnp.float32

def rmsnorm(x, g):
    xf = x.astype(F32)
    y = xf * lax.rsqrt(jnp.mean(xf * xf, axis=-1, keepdims=True) + RMS_EPS)
    return (y * g.astype(F32)).astype(x.dtype)

def in_proj(xn, w_in, b_fgate, lb):
    B, T, _ = xn.shape
    h = xn @ w_in
    idx = np.cumsum(IN_SIZES)[:-1].tolist()
    fq, fk, fv, ff, fz, hq, hf, hi, hz, mq, mz, ga, gb, gm = jnp.split(h, idx, axis=-1)
    fox_logf = jax.nn.log_sigmoid(ff.astype(F32) + b_fgate.astype(F32))
    f = lb + (1.0 - lb) * jax.nn.sigmoid(hf.astype(F32))
    hg = lambda t: t.reshape(B, T, HG_HEADS, HG_HEAD_DIM)
    fx = lambda t: t.reshape(B, T, FOX_HEADS, FOX_HEAD_DIM)
    return dict(
        fox_q=fx(fq), fox_k=fx(fk), fox_v=fx(fv), fox_logf=fox_logf, fox_z=fz,
        hg_q=hg(jax.nn.silu(hq.astype(F32))), hg_k=hg(1.0 - f), hg_logf=hg(jnp.log(f)), hg_v=hg(hi), hg_z=hz,
        mem_q=mq.reshape(B, T, MEM_HEADS, MEM_HEAD_DIM), mem_z=mz,
        ga=ga, gb=gb, gm=gm)

def fox_prompt(q, k, v, logf):
    B, T, H, Dh = q.shape
    scale = Dh ** -0.5
    c = jnp.cumsum(logf, axis=1).transpose(0, 2, 1)
    kpos = jnp.arange(T)

    def block(i):
        start = i * Q_BLOCK
        qb = lax.dynamic_slice_in_dim(q, start, Q_BLOCK, axis=1)
        cq = lax.dynamic_slice_in_dim(c, start, Q_BLOCK, axis=2)
        sc = (jnp.einsum('bqhd,bkhd->bhqk', qb, k).astype(F32) * scale
              + cq[..., None] - c[:, :, None, :])
        qpos = start + jnp.arange(Q_BLOCK)
        sc = jnp.where(kpos[None, :] <= qpos[:, None], sc, -jnp.inf)
        p = jax.nn.softmax(sc, axis=-1).astype(v.dtype)
        return jnp.einsum('bhqk,bkhd->bqhd', p, v)

    o = lax.map(block, jnp.arange(T // Q_BLOCK))
    return o.transpose(1, 0, 2, 3, 4).reshape(B, T, H, Dh)

def fox_sample(q, k_new, v_new, logf_new, k_past, v_past, logf_past):
    Dh = q.shape[-1]
    P = k_past.shape[1]
    Tn = q.shape[1]
    scale = Dh ** -0.5
    rev = lax.cumsum(logf_past.astype(F32), axis=1, reverse=True)
    r_excl = jnp.concatenate([rev[:, 1:], jnp.zeros_like(rev[:, :1])], axis=1)
    r_excl = r_excl.transpose(0, 2, 1)
    cn = jnp.cumsum(logf_new.astype(F32), axis=1).transpose(0, 2, 1)
    sp = (jnp.einsum('bqhd,bkhd->bhqk', q, k_past).astype(F32) * scale
          + cn[..., None] + r_excl[:, :, None, :])
    sn = (jnp.einsum('bqhd,bkhd->bhqk', q, k_new).astype(F32) * scale
          + cn[..., None] - cn[:, :, None, :])
    tri = jnp.tril(jnp.ones((Tn, Tn), bool))
    sn = jnp.where(tri, sn, -jnp.inf)
    p = jax.nn.softmax(jnp.concatenate([sp, sn], axis=-1), axis=-1).astype(v_new.dtype)
    return (jnp.einsum('bhqk,bkhd->bqhd', p[..., :P], v_past)
            + jnp.einsum('bhqk,bkhd->bqhd', p[..., P:], v_new))

def hgrn2(q, k, v, logf, s0, chunk):
    B, L, H, DK = q.shape
    DV = v.shape[-1]
    n = L // chunk

    def blocks(t):
        return t.astype(F32).reshape(B, n, chunk, H, t.shape[-1]).swapaxes(0, 1)

    tri = jnp.tril(jnp.ones((chunk, chunk), bool))[None, :, :, None, None]

    def step(S, inp):
        qc, kc, vc, lc = inp
        b = jnp.cumsum(lc, axis=1)
        decay = jnp.exp(jnp.where(tri, b[:, :, None] - b[:, None, :], -jnp.inf))
        att = jnp.einsum('bthk,btshk,bshk->bhts', qc, decay, kc)
        o = (jnp.einsum('bhts,bshv->bthv', att, vc)
             + jnp.einsum('bthk,bhkv->bthv', qc * jnp.exp(b), S))
        bl = b[:, -1]
        S = (jnp.exp(bl)[..., None] * S
             + jnp.einsum('bshk,bshv->bhkv', kc * jnp.exp(bl[:, None] - b), vc))
        return S, o

    S, o = lax.scan(step, s0.astype(F32), (blocks(q), blocks(k), blocks(v), blocks(logf)))
    return o.swapaxes(0, 1).reshape(B, L, H, DV), S

def mem_kv(mem, g, w_mk, w_mv):
    B = mem.shape[0]
    mn = rmsnorm(mem, g)
    mk = (mn @ w_mk).reshape(B, N_MEM, MEM_HEADS, MEM_HEAD_DIM)
    mv = (mn @ w_mv).reshape(B, N_MEM, MEM_HEADS, MEM_HEAD_DIM)
    return mk, mv

def mem_attn(q, mk, mv):
    scale = q.shape[-1] ** -0.5
    sc = jnp.einsum('bqhd,bkhd->bhqk', q, mk).astype(F32) * scale
    p = jax.nn.softmax(sc, axis=-1).astype(mv.dtype)
    return jnp.einsum('bhqk,bkhd->bqhd', p, mv)

def merge_branches(x, p, o_fox, o_hg, o_mem, hg_norm_g, w_pa, w_pb, w_pm, w_o):
    B, T, _ = x.shape
    o_hg = rmsnorm(o_hg.astype(x.dtype), hg_norm_g.reshape(HG_HEADS, HG_HEAD_DIM)).reshape(B, T, HG_WIDTH)
    ya = (o_fox.reshape(B, T, FOX_WIDTH) * jax.nn.silu(p['fox_z'])) @ w_pa
    yb = (o_hg * jax.nn.silu(p['hg_z'])) @ w_pb
    ym = (o_mem.reshape(B, T, MEM_WIDTH) * jax.nn.silu(p['mem_z'])) @ w_pm
    mixed = jax.nn.sigmoid(p['ga']) * ya + jax.nn.sigmoid(p['gb']) * yb + jax.nn.sigmoid(p['gm']) * ym
    return x + mixed @ w_o

def setup_inputs(seed: int = 0) -> dict:
    key = jax.random.key(seed)
    ks = jax.random.split(key, 24)
    n_pages = PAST_LEN // PAGE_SIZE
    n_phys = (DEC_BATCH * n_pages * 5) // 4
    nrm = lambda k, shape, s=1.0: jax.random.normal(k, shape, F32) * s
    head_bias = jnp.linspace(FGATE_BIAS_LO, FGATE_BIAS_HI, FOX_HEADS, dtype=F32)
    page_table = jax.random.permutation(ks[0], n_phys)[:DEC_BATCH * n_pages].reshape(DEC_BATCH, n_pages).astype(jnp.int32)
    return {
        'x_prompt': nrm(ks[1], (BATCH, SEQ, D_MODEL)),
        'x_sample': nrm(ks[2], (DEC_BATCH, DEC_SEQ, D_MODEL)),
        'mem_prompt': nrm(ks[3], (BATCH, N_MEM, D_MODEL)),
        'cache_fox_k': nrm(ks[4], (DEPTH, n_phys, PAGE_SIZE, FOX_HEADS, FOX_HEAD_DIM)),
        'cache_fox_v': nrm(ks[5], (DEPTH, n_phys, PAGE_SIZE, FOX_HEADS, FOX_HEAD_DIM)),
        'cache_fox_logf': jax.nn.log_sigmoid(head_bias + nrm(ks[6], (DEPTH, n_phys, PAGE_SIZE, FOX_HEADS), 0.5)),
        'page_table': page_table,
        'state_hgrn': nrm(ks[7], (DEPTH, DEC_BATCH, HG_HEADS, HG_HEAD_DIM, HG_HEAD_DIM), 0.5),
        'cache_mem_k': nrm(ks[8], (DEPTH, DEC_BATCH, N_MEM, MEM_HEADS, MEM_HEAD_DIM)),
        'cache_mem_v': nrm(ks[9], (DEPTH, DEC_BATCH, N_MEM, MEM_HEADS, MEM_HEAD_DIM)),
        'norm_g': 1.0 + nrm(ks[10], (DEPTH, D_MODEL), 0.02),
        'w_in': nrm(ks[11], (DEPTH, D_MODEL, N_IN), D_MODEL ** -0.5),
        'b_fgate': head_bias + nrm(ks[12], (DEPTH, FOX_HEADS), 0.1),
        'hg_norm_g': 1.0 + nrm(ks[13], (DEPTH, HG_WIDTH), 0.02),
        'lb_param': 1.0 + nrm(ks[14], (DEPTH + 1, HG_WIDTH), 0.1),
        'mem_norm_g': 1.0 + nrm(ks[15], (DEPTH, D_MODEL), 0.02),
        'w_mk': nrm(ks[16], (DEPTH, D_MODEL, MEM_WIDTH), D_MODEL ** -0.5),
        'w_mv': nrm(ks[17], (DEPTH, D_MODEL, MEM_WIDTH), D_MODEL ** -0.5),
        'w_pa': nrm(ks[18], (DEPTH, FOX_WIDTH, D_MODEL), FOX_WIDTH ** -0.5),
        'w_pb': nrm(ks[19], (DEPTH, HG_WIDTH, D_MODEL), HG_WIDTH ** -0.5),
        'w_pm': nrm(ks[20], (DEPTH, MEM_WIDTH, D_MODEL), MEM_WIDTH ** -0.5),
        'w_o': nrm(ks[21], (DEPTH, D_MODEL, D_MODEL), D_MODEL ** -0.5),
        'final_norm_g': 1.0 + nrm(ks[22], (D_MODEL,), 0.02),
    }

def reference(x_prompt, x_sample, mem_prompt, cache_fox_k, cache_fox_v, cache_fox_logf, page_table,
              state_hgrn, cache_mem_k, cache_mem_v, norm_g, w_in, b_fgate, hg_norm_g, lb_param,
              mem_norm_g, w_mk, w_mv, w_pa, w_pb, w_pm, w_o, final_norm_g):
    lb_all = jnp.cumsum(jax.nn.softmax(lb_param.astype(F32), axis=0), axis=0)
    xp, xs = x_prompt, x_sample
    fkp, fvp, flp, hsp, mkp, mvp = [], [], [], [], [], []
    fks, fvs, fls, hss = [], [], [], []
    for l in range(DEPTH):
        pp = in_proj(rmsnorm(xp, norm_g[l]), w_in[l], b_fgate[l], lb_all[l])
        o_fox = fox_prompt(pp['fox_q'], pp['fox_k'], pp['fox_v'], pp['fox_logf'])
        s0 = jnp.zeros((xp.shape[0], HG_HEADS, HG_HEAD_DIM, HG_HEAD_DIM), F32)
        o_hg, s_p = hgrn2(pp['hg_q'], pp['hg_k'], pp['hg_v'], pp['hg_logf'], s0, HG_CHUNK)
        mk, mv = mem_kv(mem_prompt, mem_norm_g[l], w_mk[l], w_mv[l])
        o_mem = mem_attn(pp['mem_q'], mk, mv)
        xp = merge_branches(xp, pp, o_fox, o_hg, o_mem, hg_norm_g[l], w_pa[l], w_pb[l], w_pm[l], w_o[l])
        fkp.append(pp['fox_k'])
        fvp.append(pp['fox_v'])
        flp.append(pp['fox_logf'].astype(cache_fox_logf.dtype))
        hsp.append(s_p.astype(state_hgrn.dtype))
        mkp.append(mk)
        mvp.append(mv)
        ps = in_proj(rmsnorm(xs, norm_g[l]), w_in[l], b_fgate[l], lb_all[l])
        db = xs.shape[0]
        k_past = cache_fox_k[l][page_table].reshape(db, -1, FOX_HEADS, FOX_HEAD_DIM)
        v_past = cache_fox_v[l][page_table].reshape(db, -1, FOX_HEADS, FOX_HEAD_DIM)
        lf_past = cache_fox_logf[l][page_table].reshape(db, -1, FOX_HEADS)
        o_fox_s = fox_sample(ps['fox_q'], ps['fox_k'], ps['fox_v'], ps['fox_logf'], k_past, v_past, lf_past)
        o_hg_s, s_s = hgrn2(ps['hg_q'], ps['hg_k'], ps['hg_v'], ps['hg_logf'], state_hgrn[l], xs.shape[1])
        o_mem_s = mem_attn(ps['mem_q'], cache_mem_k[l], cache_mem_v[l])
        xs = merge_branches(xs, ps, o_fox_s, o_hg_s, o_mem_s, hg_norm_g[l], w_pa[l], w_pb[l], w_pm[l], w_o[l])
        fks.append(ps['fox_k'])
        fvs.append(ps['fox_v'])
        fls.append(ps['fox_logf'].astype(cache_fox_logf.dtype))
        hss.append(s_s.astype(state_hgrn.dtype))
    y_prompt = rmsnorm(xp, final_norm_g)
    y_sample = rmsnorm(xs, final_norm_g)
    return (y_prompt, y_sample,
            jnp.stack(fkp), jnp.stack(fvp), jnp.stack(flp), jnp.stack(hsp), jnp.stack(mkp), jnp.stack(mvp),
            jnp.stack(fks), jnp.stack(fvs), jnp.stack(fls), jnp.stack(hss))


_drawn_inputs = setup_inputs


def setup_inputs(seed=0):
    import zlib

    import numpy as np

    out = dict(_drawn_inputs(seed))
    spreads = {}
    factors = {'hg_norm_g': 74.346,
     'mem_norm_g': 23.438,
     'final_norm_g': 22.52,
     'cache_fox_k': 4.83,
     'cache_fox_v': 3.586,
     'cache_fox_logf': 3.309,
     'cache_mem_k': 5.959,
     'cache_mem_v': 5.034}
    for name, (base, spread) in spreads.items():
        noise = np.random.default_rng([zlib.crc32(name.encode()), seed]).standard_normal(out[name].shape)
        drawn = base * np.exp(spread * noise) if base else spread * noise
        out[name] = __import__('jax').numpy.asarray(drawn.astype(out[name].dtype))
    for name, factor in factors.items():
        out[name] = (out[name] * factor).astype(out[name].dtype)
    return out
```

```python
from contextlib import ExitStack

import numpy as np

import concourse.bass as bass
from concourse import mybir

F32 = mybir.dt.float32
F32R = mybir.dt.float32r
I32 = mybir.dt.int32
ALU = mybir.AluOpType
ACT = mybir.ActivationFunctionType
AX = mybir.AxisListType

P = 128
D = 1024
KT = D // P
T = 2048
NT = T // P
B = 8
NM = 256
W = 512
FH, FD = 8, 64
HH, HD = 4, 128
EPS = 1e-6
PAGE = 128
BANK = 512
NEG = -1e30

COL = {}
at = 0
for name, width in (("fq", W), ("fk", W), ("fv", W), ("ff", FH), ("fz", W), ("hq", W), ("hf", W), ("hi", W),
                    ("hz", W), ("mq", W), ("mz", W), ("ga", D), ("gb", D), ("gm", D)):
    COL[name] = at
    at += width
N_IN = at

TURNED = ["fq", "mq", "hf", "hq"]
PLAIN = ["fk", "fv", "hi", "fz", "hz", "mz"]
KIND = {"fq": "scale", "mq": "copy", "hf": "sigmoid", "hq": "silu", "fk": "copy", "fv": "copy", "hi": "copy",
        "fz": "silu", "hz": "silu", "mz": "silu"}
NGATE = 3 * D // W
FIRST_GATE = len(TURNED) + len(PLAIN)
NGROUP = FIRST_GATE + NGATE
PT = {"fq": 0, "mq": 1, "hf": 2, "hq": 3}
PN = {"hi": 0, "fz": 1, "hz": 2, "mz": 3, "gate": 4}
SAMPLE_COLUMNS = 66
UNITS = 16


class Core:

    def __init__(self, nc, ctx):
        self.nc, self.ctx = nc, ctx
        self.ident = ctx.enter_context(nc.sbuf_tensor("ident", [P, P], F32))

    def sem(self, name):
        return self.nc.alloc_semaphore(name=name)


def linker(eng, sem, base=0):
    done = [0]

    def link(ins):
        done[0] += 1
        ins.then_inc(sem, 1)
        eng.wait_ge(sem, base + done[0])
    link.done = done
    return link


def rows_of(dram, start, count):
    return dram[bass.ds(start, count), :]


def constants(nc, core):
    cleared = core.sem("cleared")
    with nc.Block() as block:
        @block.gpsimd
        def _(pool):
            pool.memset(core.ident[:], 0.0).then_inc(cleared, 1)
            pool.wait_ge(cleared, 1)
            pool.affine_select(out=core.ident[:], in_=core.ident[:], compare_op=ALU.not_equal, fill=1.0, base=0,
                               pattern=[[-1, P]], channel_multiplier=1)


def clear(nc, core, tile):
    with nc.Block() as block:
        @block.gpsimd
        def _(pool):
            pool.memset(tile[:].bitcast(F32), 0.0)


def normalise_rows(nc, core, tag, src, gain, hi, lo, tiles, rows, slots):
    with ExitStack() as ctx:
        def sb(name, shape, dt=F32):
            return ctx.enter_context(nc.sbuf_tensor(f"{tag}_{name}", shape, dt))

        x = [sb(f"x{r}", [rows, D]) for r in range(slots)]
        square = sb("square", [rows, D])
        normed = [sb(f"normed{r}", [rows, D]) for r in range(slots)]
        gains = sb("gains", [rows, D])
        stat = sb("stat", [rows, 3])
        turned = [ctx.enter_context(nc.psum_tensor(f"{tag}_turned{r}", [P, KT, P], F32)) for r in range(slots)]
        x_loaded = [core.sem(f"{tag}_x_loaded{r}") for r in range(slots)]
        gains_loaded = core.sem(f"{tag}_gains_loaded")
        x_used = core.sem(f"{tag}_x_used")
        stat_step = core.sem(f"{tag}_stat_step")
        normed_ready = core.sem(f"{tag}_normed_ready")
        turned_ready = core.sem(f"{tag}_turned_ready")
        turned_used = core.sem(f"{tag}_turned_used")
        hi_ready = core.sem(f"{tag}_hi_ready")
        mean_ready = core.sem(f"{tag}_mean_ready")
        root_ready = core.sem(f"{tag}_root_ready")

        with nc.Block() as block:
            @block.sync
            def _(sp):
                sp.dma_start(gains[:], gain.partition_broadcast(rows)).then_inc(gains_loaded, 16)
                with sp.Fori(0, tiles // slots) as i:
                    for r in range(slots):
                        sp.wait_ge(x_used, i * slots + r + 1)
                        sp.dma_start(x[r][:], rows_of(src, (i * slots + r) * rows, rows)).then_inc(x_loaded[r], 16)

            @block.vector
            def _(dve):
                dve.sem_inc(x_used, slots)
                dve.wait_ge(gains_loaded, 16)
                with dve.Fori(0, tiles // slots) as i:
                    for r in range(slots):
                        link = linker(dve, stat_step, (i * slots + r) * 2)
                        dve.wait_ge(x_loaded[r], (i + 1) * 16)
                        link(dve.tensor_tensor_reduce(square[:], x[r][:], x[r][:], 1.0, 0.0, ALU.mult, ALU.add,
                                                      stat[:, 0:1]))
                        dve.tensor_scalar(stat[:, 1:2], stat[:, 0:1], 1.0 / D, EPS, ALU.mult,
                                          ALU.add).then_inc(mean_ready, 1)
                        dve.wait_ge(root_ready, i * slots + r + 1)
                        link(dve.reciprocal(stat[:, 2:3], stat[:, 1:2]))
                        dve.scalar_tensor_tensor(out=normed[r][:], in0=x[r][:], scalar=stat[:, 2:3], in1=gains[:],
                                                 op0=ALU.mult, op1=ALU.mult).then_inc(normed_ready, 1)
                        dve.wait_ge(normed_ready, i * slots + r + 1)
                        dve.sem_inc(x_used, 1)
                    for r in range(slots):
                        dve.wait_ge(turned_ready, i * slots + r + 1)
                        dve.wait_ge(hi_ready, i * slots + r + 1)
                        at = bass.ds((i * slots + r) * rows, rows)
                        dve.tensor_tensor(lo[:, :, at], turned[r][:, :, 0:rows], hi[:, :, at].bitcast(F32),
                                          ALU.subtract).then_inc(turned_used, 1)

            @block.tensor
            def _(pe):
                pe.sem_inc(turned_used, slots)
                with pe.Fori(0, tiles // slots) as i:
                    for r in range(slots):
                        pe.wait_ge(turned_used, i * slots + r + 1)
                        pe.wait_ge(normed_ready, i * slots + r + 1)
                        for k in range(KT):
                            last = pe.transpose(turned[r][:, k, 0:rows], normed[r][:, k * P:(k + 1) * P],
                                                core.ident[0:rows, 0:rows])
                        last.then_inc(turned_ready, 1)

            @block.scalar
            def _(act):
                with act.Fori(0, tiles // slots) as i:
                    for r in range(slots):
                        act.wait_ge(mean_ready, i * slots + r + 1)
                        act.activation(stat[:, 1:2], stat[:, 1:2], ACT.Sqrt).then_inc(root_ready, 1)
                    for r in range(slots):
                        act.wait_ge(turned_ready, i * slots + r + 1)
                        act.activation(hi[:, :, bass.ds((i * slots + r) * rows, rows)], turned[r][:, :, 0:rows],
                                       ACT.Copy).then_inc(hi_ready, 1)


def product(pe, out, a, b, first, last):
    pe.matmul(out, a[0], b[0], start=first, stop=False)
    pe.matmul(out, a[1], b[0], start=False, stop=False)
    return pe.matmul(out, a[0], b[1], start=False, stop=last)


def project_memory(nc, core, mem_hi, mem_lo, weights, outputs):
    tiles = NM // P
    with ExitStack() as ctx:
        def sb(name, shape, dt=F32):
            return ctx.enter_context(nc.sbuf_tensor(f"mkv_{name}", shape, dt))

        raw = [sb(f"raw{g}", [P, KT, W]) for g in range(2)]
        whi = [sb(f"whi{g}", [P, KT, W], F32R) for g in range(2)]
        wlo = [sb(f"wlo{g}", [P, KT, W], F32R) for g in range(2)]
        stage = sb("stage", [P, 2, tiles, W])
        out = ctx.enter_context(nc.psum_tensor("mkv_out", [P, 2, tiles, W], F32))
        raw_loaded = [core.sem(f"mkv_raw_loaded{g}") for g in range(2)]
        hi_ready = core.sem("mkv_hi_ready")
        lo_ready = core.sem("mkv_lo_ready")
        out_ready = core.sem("mkv_out_ready")
        staged = core.sem("mkv_staged")
        stored = core.sem("mkv_stored")

        with nc.Block() as block:
            @block.sync
            def _(sp):
                for g in range(2):
                    sp.dma_start(raw[g][:], weights[g].rearrange("(k p) n -> p k n", p=P)).then_inc(raw_loaded[g], 16)
                for g in range(2):
                    for t in range(tiles):
                        sp.wait_ge(staged, g * tiles + t + 1)
                        sp.dma_start(outputs[g][t * P:(t + 1) * P, :], stage[:, g, t, :]).then_inc(stored, 16)
                sp.wait_ge(stored, 16 * 2 * tiles)

            @block.scalar
            def _(act):
                for g in range(2):
                    act.wait_ge(raw_loaded[g], 16)
                    act.activation(whi[g][:], raw[g][:], ACT.Copy).then_inc(hi_ready, 1)
                for n in range(2 * tiles):
                    act.wait_ge(out_ready, n + 1)
                    act.activation(stage[:, n // tiles, n % tiles, :], out[:, n // tiles, n % tiles, :],
                                   ACT.Copy).then_inc(staged, 1)

            @block.vector
            def _(dve):
                for g in range(2):
                    dve.wait_ge(hi_ready, g + 1)
                    dve.tensor_tensor(wlo[g][:], raw[g][:], whi[g][:].bitcast(F32), ALU.subtract).then_inc(lo_ready, 1)

            @block.tensor
            def _(pe):
                for g in range(2):
                    pe.wait_ge(lo_ready, g + 1)
                    for t in range(tiles):
                        for k in range(KT):
                            m = product(pe, out[:, g, t, :],
                                        (mem_hi[:, k, t * P:(t + 1) * P], mem_lo[:, k, t * P:(t + 1) * P]),
                                        (whi[g][:, k, :], wlo[g][:, k, :]), k == 0, k == KT - 1)
                        m.then_inc(out_ready, 1)


def forget_gates(nc, core, x_hi, x_lo, xs_hi, xs_lo, w_ff, bias, logf_p, logf_s, neg_c):
    N = NT * FH + FH
    with ExitStack() as ctx:
        def sb(name, shape, dt=F32):
            return ctx.enter_context(nc.sbuf_tensor(f"ff_{name}", shape, dt))

        raw, whi, wlo = sb("raw", [P, KT, FH]), sb("whi", [P, KT, FH], F32R), sb("wlo", [P, KT, FH], F32R)
        biases = sb("biases", [P, FH])
        z, e, u, r, low = (sb(n, [P, NT + 1, FH]) for n in ("z", "e", "u", "r", "low"))
        logf = sb("logf", [P, NT + 1, FH])
        turned = sb("turned", [FH, T])
        summed = sb("summed", [FH, T])
        one_row = sb("one_row", [FH, T])
        out = ctx.enter_context(nc.psum_tensor("ff_out", [P, NT + 1, FH], F32))
        flipped = ctx.enter_context(nc.psum_tensor("ff_flipped", [FH, T], F32))
        loaded, split, out_ready, step = (core.sem(f"ff_{n}") for n in ("loaded", "split", "out_ready", "step"))
        exp_ready, exp_asked, ln_asked, ln_ready = (core.sem(f"ff_{n}") for n in
                                                    ("exp_ready", "exp_asked", "ln_asked", "ln_ready"))
        logf_ready, flipped_ready, sum_ready, stored = (core.sem(f"ff_{n}") for n in
                                                        ("logf_ready", "flipped_ready", "sum_ready", "stored"))

        with nc.Block() as block:
            @block.sync
            def _(sp):
                with nc.allow_non_contiguous_dma(reason="eight columns of the weights, eight gates of a row"):
                    sp.dma_start(raw[:], w_ff.rearrange("(k p) n -> p k n", p=P)).then_inc(loaded, 16)
                    sp.dma_start(biases[:], bias.partition_broadcast(P)).then_inc(loaded, 16)
                    sp.wait_ge(logf_ready, 1)
                    sp.dma_start(logf_p.rearrange("(t p) h -> p t h", p=P), logf[:, 0:NT, :]).then_inc(stored, 16)
                    sp.dma_start(logf_s, logf[0:B, NT, :]).then_inc(stored, 16)
                sp.wait_ge(sum_ready, 1)
                sp.dma_start(neg_c, summed[:]).then_inc(stored, 16)
                sp.wait_ge(stored, 48)

            @block.vector
            def _(dve):
                link = linker(dve, step)
                dve.wait_ge(loaded, 32)
                link(dve.tensor_copy(whi[:], raw[:]))
                dve.tensor_tensor(wlo[:], raw[:], whi[:].bitcast(F32), ALU.subtract).then_inc(split, 1)
                link(dve.memset(z[:], 0.0))
                link(dve.memset(one_row[:], 1.0))
                dve.wait_ge(out_ready, 1)
                link(dve.tensor_tensor(z[:, 0:NT, :], out[:, 0:NT, :],
                                       biases[:].unsqueeze(1).to_broadcast([P, NT, FH]), ALU.add))
                link(dve.tensor_tensor(z[0:B, NT, :], out[0:B, NT, :], biases[0:B, :], ALU.add))
                dve.scalar_tensor_tensor(out=u[:], in0=z[:], scalar=-1.0, in1=z[:], op0=ALU.mult,
                                         op1=ALU.max).then_inc(exp_asked, 1)
                link(dve.tensor_scalar(low[:], z[:], 0.0, None, ALU.min))
                dve.wait_ge(exp_ready, 1)
                dve.tensor_scalar(u[:], e[:], 1.0, None, ALU.add).then_inc(ln_asked, 1)
                dve.wait_ge(ln_asked, 1)
                link(dve.scalar_tensor_tensor(out=r[:], in0=u[:], scalar=-1.0, in1=e[:], op0=ALU.add,
                                              op1=ALU.subtract))
                dve.wait_ge(ln_ready, 1)
                link(dve.reciprocal(u[:], u[:]))
                link(dve.tensor_tensor(r[:], r[:], u[:], ALU.mult))
                link(dve.tensor_tensor(z[:], z[:], r[:], ALU.subtract))
                dve.tensor_tensor(logf[:], low[:], z[:], ALU.subtract).then_inc(logf_ready, 1)
                dve.wait_ge(flipped_ready, 1)
                link(dve.tensor_scalar(turned[:], flipped[:], -1.0, None, ALU.mult))
                dve.tensor_tensor_scan(summed[:], one_row[:], turned[:], 0.0, ALU.mult, ALU.add).then_inc(sum_ready, 1)

            @block.scalar
            def _(act):
                act.wait_ge(exp_asked, 1)
                act.activation(e[:], u[:], ACT.Exp, scale=-1.0).then_inc(exp_ready, 1)
                act.wait_ge(ln_asked, 1)
                act.activation(z[:], u[:], ACT.Ln).then_inc(ln_ready, 1)

            @block.tensor
            def _(pe):
                pe.wait_ge(split, 1)
                for t in range(NT + 1):
                    for k in range(KT):
                        if t < NT:
                            product(pe, out[:, t, :], (x_hi[:, k, t * P:(t + 1) * P], x_lo[:, k, t * P:(t + 1) * P]),
                                    (whi[:, k, :], wlo[:, k, :]), k == 0, k == KT - 1)
                        else:
                            pe.matmul(out[0:B, t, :], xs_hi[:, k, :].bitcast(F32), raw[:, k, :], start=(k == 0),
                                      stop=False)
                            m = pe.matmul(out[0:B, t, :], xs_lo[:, k, :].bitcast(F32), raw[:, k, :], start=False,
                                          stop=(k == KT - 1))
                m.then_inc(out_ready, 1)
                pe.wait_ge(logf_ready, 1)
                for t in range(NT):
                    m = pe.transpose(flipped[:, t * P:(t + 1) * P], logf[:, t, :], core.ident[:])
                m.then_inc(flipped_ready, 1)


def project_inputs(nc, core, x_hi, x_lo, xs_both, w_in, turned, plain, fox_k, fox_v, sample):
    STAGES = 4
    ROUNDS = UNITS // STAGES
    USES = ROUNDS + 1
    with ExitStack() as ctx:
        def sb(name, shape, dt=F32):
            return ctx.enter_context(nc.sbuf_tensor(f"in_{name}", shape, dt))

        raw = [sb(f"raw{r}", [P, W]) for r in range(2)]
        whi = [sb(f"whi{r}", [P, KT, W], F32R) for r in range(2)]
        wlo = [sb(f"wlo{r}", [P, KT, W], F32R) for r in range(2)]
        stage = [sb(f"stage{s}", [P, W]) for s in range(STAGES)]
        out = [ctx.enter_context(nc.psum_tensor(f"in_out{s}", [P, BANK], F32)) for s in range(STAGES)]
        out_s = ctx.enter_context(nc.psum_tensor("in_out_s", [P, BANK], F32))
        primer = nc.dram_tensor("in_primer", (STAGES, P), F32, kind="Internal").ap()

        raw_loaded = [core.sem(f"in_raw_loaded{r}") for r in range(2)]
        split = core.sem("in_split")
        multiplied = core.sem("in_multiplied")
        out_ready = core.sem("in_out_ready")
        sigmoid_ready = core.sem("in_sigmoid_ready")
        taken = core.sem("in_taken")
        stored = [core.sem(f"in_stored{s}") for s in range(STAGES)]
        taken_s = core.sem("in_taken_s")
        paced = core.sem("in_paced")

        names = TURNED + PLAIN
        silus_before = [sum(KIND[n] == "silu" for n in names[:g]) for g in range(len(names))]

        with nc.Block() as block:
            @block.sync
            def _(sp):
                def load(g, column, k, slot):
                    sp.wait_ge(split, 2 * (g * KT + k) + 2)
                    sp.dma_start(raw[slot][:], w_in[bass.ds(k * P, P), bass.ds(column, W)]).then_inc(raw_loaded[slot], 16)

                def store_group(g, place, following):
                    with sp.Fori(0, ROUNDS) as q:
                        if following is not None:
                            for r in range(2):
                                load(g + 1, following, q * 2 + r, r)
                        for s in range(STAGES):
                            sp.wait_ge(taken, STAGES + g * UNITS + q * STAGES + s + 1)
                            sp.dma_start(place(q, s), stage[s][:]).then_inc(stored[s], 16)
                    sp.wait_ge(taken_s, g + 2)
                    sp.dma_start(sample[bass.ds(g, 1)].rearrange("o p n -> (o p) n"), stage[0][0:2 * B, :]).then_inc(stored[0], 16)

                for s in range(STAGES):
                    sp.dma_start(primer[s:s + 1, :], core.ident[0:1, :]).then_inc(stored[s], 16)
                with sp.Fori(0, KT // 2) as q:
                    for r in range(2):
                        load(0, COL[names[0]], q * 2 + r, r)
                for g, name in enumerate(names):
                    following = COL[names[g + 1]] if g + 1 < FIRST_GATE else COL["ga"]
                    if name in PT:
                        dst = turned[PT[name]]
                        store_group(g, lambda q, s, dst=dst: dst[bass.ds(q * P, P), s * W:(s + 1) * W], following)
                    else:
                        dst = fox_k if name == "fk" else fox_v if name == "fv" else plain[PN[name]]
                        store_group(g, lambda q, s, dst=dst: dst[bass.ds((q * STAGES + s) * P, P), :], following)

                def gate_place(j):
                    return lambda q, s: plain[bass.ds(j + PN["gate"], 1), bass.ds((q * STAGES + s) * P, P), :] \
                        .rearrange("o t n -> (o t) n")

                with sp.Fori(0, NGATE - 1) as j:
                    store_group(j + FIRST_GATE, gate_place(j), j * W + COL["ga"] + W)
                store_group(NGROUP - 1, gate_place(NGATE - 1), None)
                for s in range(STAGES):
                    sp.wait_ge(stored[s], 16 * (1 + NGROUP * (USES if s == 0 else ROUNDS)))

            @block.gpsimd
            def _(pool):
                pool.sem_inc(split, 4)
                with pool.Fori(0, NGROUP // 2) as pair:
                    for r in range(2):
                        pool.wait_ge(multiplied, pair * 2 + r + 1)
                        for k in range(KT):
                            n = (pair * 2 + r) * KT + k
                            pool.wait_ge(raw_loaded[k % 2], ((pair * 2 + r) * (KT // 2) + k // 2 + 1) * 16)
                            pool.sem_inc(paced, 1)
                            pool.tensor_copy(whi[r][:, k, :], raw[k % 2][:]).then_inc(split, 1)
                            pool.wait_ge(split, n * 2 + 5)
                            pool.tensor_tensor(wlo[r][:, k, :], raw[k % 2][:], whi[r][:, k, :].bitcast(F32),
                                               ALU.subtract).then_inc(split, 1)

            @block.tensor
            def _(pe):
                pe.sem_inc(multiplied, 2)
                pe.sem_inc(taken, STAGES)
                pe.sem_inc(taken_s, 1)

                def group(g, r, is_turned):
                    for u in range(UNITS):
                        pe.wait_ge(taken, g * UNITS + u + 1)
                        c, b = u // STAGES, u % STAGES
                        for k in range(KT):
                            if u == 0:
                                pe.wait_ge(split, (g * KT + k) * 2 + 6)
                            w = (whi[r], wlo[r])
                            x = (x_hi, x_lo)
                            if is_turned:
                                m = product(pe, out[u % STAGES][:], [a[:, k, c * P:(c + 1) * P] for a in w],
                                            [a[:, k, b * W:(b + 1) * W] for a in x], k == 0, k == KT - 1)
                            else:
                                m = product(pe, out[u % STAGES][:], [a[:, k, u * P:(u + 1) * P] for a in x],
                                            [a[:, k, :] for a in w], k == 0, k == KT - 1)
                        m.then_inc(out_ready, 1)
                    pe.wait_ge(taken_s, g + 1)
                    for k in range(KT):
                        pe.matmul(out_s[0:SAMPLE_COLUMNS, :], xs_both[:, k, :], whi[r][:, k, :], start=(k == 0),
                                  stop=False)
                        m = pe.matmul(out_s[0:SAMPLE_COLUMNS, :], xs_both[:, k, :], wlo[r][:, k, :], start=False,
                                      stop=(k == KT - 1))
                    m.then_inc(multiplied, 1)

                with pe.Fori(0, len(TURNED) // 2) as pair:
                    for r in range(2):
                        group(pair * 2 + r, r, True)
                with pe.Fori(len(TURNED) // 2, NGROUP // 2) as pair:
                    for r in range(2):
                        group(pair * 2 + r, r, False)

            @block.scalar
            def _(act):
                def group(g, kind):
                    how = {"copy": (ACT.Copy, 1.0), "scale": (ACT.Copy, FD ** -0.5)}.get(kind, (ACT.Sigmoid, 1.0))
                    signal = sigmoid_ready if kind == "silu" else taken
                    act.wait_ge(taken, STAGES + g * UNITS)
                    with act.Fori(0, ROUNDS) as q:
                        for s in range(STAGES):
                            act.wait_ge(out_ready, g * UNITS + q * STAGES + s + 1)
                            act.wait_ge(stored[s], (g * (USES if s == 0 else ROUNDS) + q + 1) * 16)
                            act.activation(stage[s][:], out[s][:], how[0], scale=how[1]).then_inc(signal, 1)
                    act.wait_ge(multiplied, g + 3)
                    act.wait_ge(taken, STAGES + (g + 1) * UNITS)
                    act.wait_ge(stored[0], (g * USES + ROUNDS + 1) * 16)
                    act.activation(stage[0][0:2 * B, :], out_s[0:2 * B, :], ACT.Copy).then_inc(taken_s, 1)

                for g, name in enumerate(names):
                    group(g, KIND[name])
                with act.Fori(FIRST_GATE, NGROUP) as g:
                    group(g, "sigmoid")

            @block.vector
            def _(dve):
                for g, name in enumerate(names):
                    if KIND[name] == "silu":
                        n = silus_before[g]
                        with dve.Fori(0, ROUNDS) as q:
                            for s in range(STAGES):
                                dve.wait_ge(sigmoid_ready, q * STAGES + s + 1 + n * UNITS)
                                dve.tensor_tensor(stage[s][:], stage[s][:], out[s][:], ALU.mult).then_inc(taken, 1)


def attend_prompt(nc, core, queries, fox_k, fox_v, z_fox, neg_c, gated):
    QUADS = NT // 4
    HEADS = 2
    S_BANKS = 3
    CHUNKS = [i // 4 + 1 for i in range(NT)]
    S_HEAD = sum(CHUNKS)
    J_HEAD = sum(4 * (q + 1) for q in range(QUADS))
    J_AT = [sum(4 * (p + 1) for p in range(q)) for q in range(QUADS)]
    S_AT = [sum(CHUNKS[:i]) for i in range(NT)]
    TURN_BANKS = 3
    PT_SLOTS = 4
    SPREAD = 0.8
    DEPTH = 2
    quads = [(h, q) for h in range(HEADS) for q in range(QUADS)]

    def chunks_of(h, q):
        return [("score", h, i, c) for i in range(4 * q, 4 * q + 4) for c in range(CHUNKS[i])]

    steps = [("set", 0)] + [("keys", 0, b) for b in range(QUADS)]
    for i in range(4):
        steps += [("score", 0, i, 0), ("exp", 0, i)]
    for n, (h, q) in enumerate(quads):
        ahead = [("score", quads[n + 1][0], i, c) for i in range(4 * quads[n + 1][1], 4 * quads[n + 1][1] + 4)
                 for c in range(CHUNKS[i])] if n + 1 < len(quads) else []
        keys = 4 * (q + 1)
        spread = max(1, round(keys * SPREAD))
        late = []
        for j in range(keys):
            some = ahead[len(ahead) * min(j, spread) // spread:len(ahead) * min(j + 1, spread) // spread]
            steps += some
            if h == 0 and q == 1 and j == keys - 2:
                steps += [("set", 1)]
            if h == 0 and q == 2 and j % 3 == 0:
                steps += [("keys", 1, j // 3)]
            steps += [("key", h, q, j)]
            steps += late
            late = [("exp", st[1], st[2]) for st in some if st[3] == CHUNKS[st[2]] - 1]
            if j == DEPTH - 1 and n > 0:
                steps += [("out", *quads[n - 1])]
            if j == DEPTH + 1 and n > 0:
                steps += [("back", *quads[n - 1])]
        steps += late
    steps += [("out", *quads[-1]), ("back", *quads[-1])]
    turn_at = {st: n for n, st in enumerate(s for s in steps if s[0] in ("keys", "key", "back"))}
    TURNS = len(turn_at)
    assert TURNS % TURN_BANKS == 0 and J_HEAD % PT_SLOTS == 0

    with ExitStack() as ctx:
        def sb(name, shape, dt=F32):
            return ctx.enter_context(nc.sbuf_tensor(f"fox_{name}", shape, dt))

        def pair(name, shape, dt=F32):
            return [sb(f"{name}{h}", shape, dt) for h in range(HEADS)]

        q_both = pair("q_both", [P, T], F32R)
        k_hi, k_lo = pair("k_hi", [P, T], F32R), pair("k_lo", [P, T], F32R)
        v_both = pair("v_both", [P, NT, 2 * FD], F32R)
        q_raw = sb("q_raw", [P, T])
        k_raw = sb("k_raw", [P, NT, 2 * FD])
        v_raw = sb("v_raw", [P, NT, FD])
        z = pair("z", [P, NT, FD])
        bias = pair("bias", [P, T])
        mask = sb("mask", [P, P])
        mask_r, ident_r = sb("mask_r", [P, P], F32R), sb("ident_r", [P, P], F32R)
        halves = sb("halves", [P, P])
        probs = sb("probs", [P, 8, T])
        most = sb("most", [P, 8, CHUNKS[-1]])
        neg_most = sb("neg_most", [P, 8])
        row_sum = sb("row_sum", [P, HEADS * NT])
        inverse = sb("inverse", [P, 4])
        pt_hi, pt_lo = sb("pt_hi", [P, PT_SLOTS, BANK], F32R), sb("pt_lo", [P, PT_SLOTS, BANK], F32R)
        o_turned = sb("o_turned", [P, BANK])
        o_rows = pair("o_rows", [P, NT, FD])

        def psum(name, n):
            return [ctx.enter_context(nc.psum_tensor(f"fox_{name}{i}", [P, BANK], F32)) for i in range(n)]

        scores, turned, o_sum = psum("scores", S_BANKS), psum("turned", TURN_BANKS), psum("o_sum", 2)

        def bank_of(st):
            return turned[turn_at[st] % TURN_BANKS]

        def sem(name):
            return core.sem(f"fox_{name}")

        raw_loaded, z_loaded, bias_loaded = sem("raw_loaded"), [sem(f"z_loaded{h}") for h in range(HEADS)], \
            [sem(f"bias_loaded{h}") for h in range(HEADS)]
        raw_free = sem("raw_free")
        consts_ready = sem("consts_ready")
        q_hi_ready, q_ready, v_ready = sem("q_hi_ready"), sem("q_ready"), sem("v_ready")
        turned_ready, turned_used = sem("turned_ready"), sem("turned_used")
        keys_hi = sem("keys_hi")
        scored, scores_used = sem("scored"), sem("scores_used")
        most_ready, exp_ready = sem("most_ready"), sem("exp_ready")
        hi_ready = sem("hi_ready")
        multiplied = sem("multiplied")
        o_copied = sem("o_copied")
        rows_ready, rows_stored = sem("rows_ready"), sem("rows_stored")
        started, inverse_ready = sem("started"), sem("inverse_ready")
        paced = sem("paced")

        with nc.Block() as block:
            @block.gpsimd
            def _(pool):
                link = linker(pool, started)
                link(pool.memset(mask[:], 0.0))
                link(pool.memset(halves[:], 0.0))
                pool.affine_select(out=mask[:], in_=mask[:], compare_op=ALU.is_ge, fill=NEG, base=0,
                                   pattern=[[-1, P]], channel_multiplier=1)
                for n, base in enumerate((0, -FD, FD)):
                    link(pool.affine_select(out=halves[:], in_=halves[:], compare_op=ALU.not_equal, fill=1.0,
                                            base=base, pattern=[[-1, P]], channel_multiplier=1))
                link(pool.tensor_copy(mask_r[:], mask[:]))
                link(pool.tensor_copy(ident_r[:], core.ident[:]))
                pool.sem_inc(consts_ready, 1)

            @block.sync
            def _(sp):
                def rows(dram, head):
                    return dram.rearrange("(t p) c -> p t c", p=P)[:, :, bass.ds(head * FD, FD)]

                def load(head, h):
                    sp.wait_ge(raw_free, head + 1)
                    for half in range(2):
                        sp.dma_start(q_raw[half * FD:(half + 1) * FD, :],
                                     rows_of(queries, head * FD, FD)).then_inc(raw_loaded, 16)
                        sp.dma_start(k_raw[:, :, half * FD:(half + 1) * FD], rows(fox_k, head)).then_inc(raw_loaded, 16)
                    sp.dma_start(v_raw[:], rows(fox_v, head)).then_inc(raw_loaded, 16)
                    sp.dma_start(bias[h][:], neg_c[bass.ds(head, 1), :].to_broadcast([P, T])).then_inc(bias_loaded[h], 16)
                    sp.dma_start(z[h][:], rows(z_fox, head)).then_inc(z_loaded[h], 16)

                def store(head, h):
                    sp.wait_ge(rows_ready, (head + 3) * QUADS)
                    sp.dma_start(rows(gated, head), o_rows[h][:]).then_inc(rows_stored, 16)

                sp.sem_inc(raw_free, 1)
                with nc.allow_non_contiguous_dma(reason="a head's 64 columns of a row"):
                    for h in range(HEADS):
                        load(h, h)
                    with sp.Fori(1, FH // HEADS) as it:
                        for h in range(HEADS):
                            head = it * HEADS + h
                            store(head - HEADS, h)
                            sp.wait_ge(rows_stored, (head - 1) * 16)
                            load(head, h)
                    for h in range(HEADS):
                        store(FH - HEADS + h, h)
                    sp.wait_ge(rows_stored, FH * 16)

            @block.tensor
            def _(pe):
                pe.sem_inc(scores_used, S_BANKS)
                pe.sem_inc(turned_used, TURN_BANKS)
                pe.sem_inc(multiplied, PT_SLOTS)
                pe.sem_inc(o_copied, 2)
                pe.wait_ge(consts_ready, 1)
                with pe.Fori(0, FH // HEADS) as it:
                    pending = []

                    def values(h, q, j):
                        n, skip = h * QUADS + q, max(0, j - 4 * q) * P
                        pe.wait_ge(turned_used, it * TURNS + turn_at["key", h, q, j] + TURN_BANKS + 1)
                        if j == 0:
                            pe.wait_ge(v_ready, it * HEADS + h + 1)
                            pe.wait_ge(o_copied, it * len(quads) + n + 1)
                        for m, p in enumerate((pt_hi, pt_lo)):
                            last = pe.matmul(o_sum[n % 2][:, skip:BANK], v_both[h][:, j, :],
                                             p[:, (J_AT[q] + j) % PT_SLOTS, skip:BANK], start=(j == 0 and m == 0),
                                             stop=(j == 4 * q + 3 and m == 1))
                        last.then_inc(multiplied, 1)

                    for st in steps:
                        kind, h, *rest = st
                        head = it * HEADS + h
                        if kind == "keys":
                            b = rest[0]
                            pe.wait_ge(raw_loaded, (head + 1) * 80)
                            pe.wait_ge(turned_used, it * TURNS + turn_at[st] + 1)
                            for t in range(4):
                                last = pe.transpose(bank_of(st)[:, t * P:(t + 1) * P], k_raw[:, 4 * b + t, :], core.ident[:])
                            last.then_inc(turned_ready, 1)
                        if kind == "score":
                            i, c = rest
                            if i == 0:
                                pe.wait_ge(q_ready, head + 1)
                                pe.wait_ge(turned_used, it * TURNS + turn_at["keys", h, QUADS - 1] + TURN_BANKS + 1)
                            s = h * S_HEAD + S_AT[i] + c
                            pe.wait_ge(scores_used, it * HEADS * S_HEAD + S_BANKS + max(0, s - S_BANKS + 1))
                            width = min(BANK, (i + 1) * P - c * BANK)
                            out, keys = scores[s % S_BANKS][:, 0:width], slice(c * BANK, c * BANK + width)
                            pe.matmul(out, q_both[h][:, i * P:(i + 1) * P], k_hi[h][:, keys], start=True, stop=False)
                            last = pe.matmul(out, q_both[h][:, i * P:(i + 1) * P], k_lo[h][:, keys], start=False,
                                             stop=c < CHUNKS[i] - 1)
                            if c == CHUNKS[i] - 1:
                                last = pe.matmul(out[:, width - P:width], ident_r[:], mask_r[:], start=False, stop=True)
                            last.then_inc(scored, 1)
                        if kind == "key":
                            q, j = rest
                            if j == 0:
                                pe.wait_ge(exp_ready, head * NT + 4 * q + 4)
                            pe.wait_ge(turned_used, it * TURNS + turn_at[st] + 1)
                            for t in range(max(0, j - 4 * q), 4):
                                last = pe.transpose(bank_of(st)[:, t * P:(t + 1) * P],
                                                    probs[:, q % 2 * 4 + t, j * P:(j + 1) * P], core.ident[:])
                            last.then_inc(turned_ready, 1)
                            if len(pending) == DEPTH:
                                values(*pending.pop(0))
                            pending.append((h, q, j))
                        if kind == "out" and st is steps[-2]:
                            while pending:
                                values(*pending.pop(0))
                        if kind == "back":
                            n = h * QUADS + rest[0]
                            pe.wait_ge(o_copied, it * len(quads) + n + 3)
                            pe.wait_ge(turned_used, it * TURNS + turn_at[st] + 1)
                            for t in range(4):
                                last = pe.matmul(bank_of(st)[:, t * P:(t + 1) * P], o_turned[:, t * P:(t + 1) * P], halves[:],
                                                 start=True, stop=True)
                            last.then_inc(turned_ready, 1)

            @block.scalar
            def _(act):
                with act.Fori(0, FH // HEADS) as it:
                    for st in steps:
                        kind, h, *rest = st
                        head = it * HEADS + h
                        if kind == "set":
                            act.wait_ge(raw_loaded, (head + 1) * 80)
                            act.activation(q_both[h][:], q_raw[:], ACT.Copy).then_inc(q_hi_ready, 1)
                            act.activation(v_both[h][:, :, 0:FD], v_raw[:], ACT.Copy).then_inc(q_hi_ready, 1)
                        if kind == "keys":
                            b = rest[0]
                            act.wait_ge(turned_ready, it * TURNS + turn_at[st] + 1)
                            act.activation(k_hi[h][:, b * BANK:(b + 1) * BANK], bank_of(st)[:],
                                           ACT.Copy).then_inc(keys_hi, 1)
                        if kind == "exp":
                            i = rest[0]
                            slot = i // 4 % 2 * 4 + i % 4
                            act.wait_ge(most_ready, (head + 2) * NT + i + 1)
                            act.activation(probs[:, slot, 0:(i + 1) * P], probs[:, slot, 0:(i + 1) * P], ACT.Exp,
                                           bias=neg_most[:, slot:slot + 1],
                                           accum_out=row_sum[:, h * NT + i:h * NT + i + 1]).then_inc(exp_ready, 1)
                        if kind == "key":
                            q, j = rest
                            zeta = head * J_HEAD + J_AT[q] + j
                            skip = max(0, j - 4 * q) * P
                            act.wait_ge(turned_ready, it * TURNS + turn_at[st] + 1)
                            act.wait_ge(multiplied, zeta + 1)
                            act.activation(pt_hi[:, (J_AT[q] + j) % PT_SLOTS, skip:BANK],
                                           bank_of(st)[:, skip:BANK], ACT.Copy).then_inc(hi_ready, 1)
                        if kind == "out":
                            q = rest[0]
                            n = h * QUADS + q
                            act.wait_ge(multiplied, head * J_HEAD + J_AT[q] + 4 * (q + 1) + PT_SLOTS)
                            act.wait_ge(rows_ready, it * len(quads) + n + 2 * QUADS)
                            act.activation(o_turned[:], o_sum[n % 2][:], ACT.Copy).then_inc(o_copied, 1)

            @block.vector
            def _(dve):
                dve.sem_inc(most_ready, 2 * NT)
                dve.sem_inc(rows_ready, 2 * QUADS)
                with dve.Fori(0, FH // HEADS) as it:
                    for st in steps:
                        kind, h, *rest = st
                        head = it * HEADS + h
                        if kind == "set":
                            dve.wait_ge(q_hi_ready, head * 2 + 1)
                            dve.tensor_tensor(q_both[h][FD:P, :], q_raw[FD:P, :], q_both[h][FD:P, :].bitcast(F32),
                                              ALU.subtract).then_inc(q_ready, 1)
                            dve.wait_ge(q_hi_ready, head * 2 + 2)
                            dve.tensor_tensor(v_both[h][:, :, FD:2 * FD], v_raw[:], v_both[h][:, :, 0:FD].bitcast(F32),
                                              ALU.subtract).then_inc(v_ready, 1)
                        if kind == "keys":
                            b = rest[0]
                            dve.wait_ge(keys_hi, head * QUADS + b + 1)
                            keys = slice(b * BANK, (b + 1) * BANK)
                            dve.tensor_tensor(k_lo[h][:, keys], bank_of(st)[:], k_hi[h][:, keys].bitcast(F32),
                                              ALU.subtract).then_inc(turned_used, 1)
                            if b == QUADS - 1:
                                dve.wait_ge(v_ready, head + 1)
                                dve.sem_inc(raw_free, 1)
                        if kind == "score":
                            i, c = rest
                            slot = i // 4 % 2 * 4 + i % 4
                            if i == 0:
                                dve.wait_ge(bias_loaded[h], (it + 1) * 16)
                            s = h * S_HEAD + S_AT[i] + c
                            bank = scores[s % S_BANKS]
                            dve.wait_ge(scored, it * HEADS * S_HEAD + s + 1)
                            dve.sem_inc(paced, 1)
                            width = min(BANK, (i + 1) * P - c * BANK)
                            keys = slice(c * BANK, c * BANK + width)
                            dve.tensor_tensor_reduce(probs[:, slot, keys], bank[:, 0:width], bias[h][:, keys], 1.0,
                                                     NEG, ALU.add, ALU.max, most[:, slot, c:c + 1]
                                                     ).then_inc(scores_used, 1)
                            if c < CHUNKS[i] - 1:
                                continue
                            dve.wait_ge(scores_used, it * HEADS * S_HEAD + S_BANKS + s + 1)
                            dve.tensor_reduce(neg_most[:, slot:slot + 1], most[:, slot, 0:CHUNKS[i]], AX.X, ALU.max,
                                              negate=True).then_inc(most_ready, 1)
                        if kind == "key":
                            q, j = rest
                            skip = max(0, j - 4 * q) * P
                            dve.wait_ge(hi_ready, head * J_HEAD + J_AT[q] + j + 1)
                            b = (J_AT[q] + j) % PT_SLOTS
                            dve.tensor_tensor(pt_lo[:, b, skip:BANK], bank_of(st)[:, skip:BANK],
                                              pt_hi[:, b, skip:BANK].bitcast(F32), ALU.subtract).then_inc(turned_used, 1)
                        if kind == "back":
                            q = rest[0]
                            n = it * len(quads) + h * QUADS + q
                            dve.wait_ge(exp_ready, head * NT + 4 * q + 4)
                            dve.reciprocal(inverse[:], row_sum[:, h * NT + 4 * q:h * NT + 4 * q + 4]
                                           ).then_inc(inverse_ready, 1)
                            dve.wait_ge(inverse_ready, n + 1)
                            if q == 0:
                                dve.wait_ge(z_loaded[h], (it + 1) * 16)
                            dve.wait_ge(turned_ready, it * TURNS + turn_at[st] + 1)
                            for t in range(4):
                                last = dve.scalar_tensor_tensor(out=o_rows[h][:, 4 * q + t, :],
                                                                in0=bank_of(st)[:, t * P:t * P + FD],
                                                                scalar=inverse[:, t:t + 1], in1=z[h][:, 4 * q + t, :],
                                                                op0=ALU.mult, op1=ALU.mult)
                            last.then_inc(rows_ready, 1)
                            dve.wait_ge(rows_ready, n + 2 * QUADS + 1)
                            dve.sem_inc(turned_used, 1)


def lower_bound(nc, core, lb_param):
    core.bound = core.ctx.enter_context(nc.sbuf_tensor("bound", [P, HH], F32))
    core.rest = core.ctx.enter_context(nc.sbuf_tensor("rest", [P, HH], F32))
    with ExitStack() as ctx:
        def sb(name, shape):
            return ctx.enter_context(nc.sbuf_tensor(f"lb_{name}", shape, F32))

        layers, shifted, most, total = sb("layers", [P, 2, HH]), sb("shifted", [P, 2, HH]), sb("most", [P, HH]), \
            sb("total", [P, HH])
        loaded, step, asked, exp_ready = (core.sem(f"lb_{n}") for n in ("loaded", "step", "asked", "exp_ready"))
        with nc.Block() as block:
            @block.sync
            def _(sp):
                with nc.allow_non_contiguous_dma(reason="1024 parameters, turned"):
                    for layer in range(2):
                        sp.dma_start(layers[:, layer, :],
                                     lb_param[layer].rearrange("(h p) -> p h", p=P)).then_inc(loaded, 16)

            @block.vector
            def _(dve):
                link = linker(dve, step)
                dve.wait_ge(loaded, 32)
                link(dve.tensor_tensor(most[:], layers[:, 0, :], layers[:, 1, :], ALU.max))
                link(dve.tensor_tensor(shifted[:], layers[:], most[:].unsqueeze(1).to_broadcast([P, 2, HH]),
                                       ALU.subtract))
                dve.sem_inc(asked, 1)
                dve.wait_ge(exp_ready, 1)
                link(dve.tensor_tensor(total[:], shifted[:, 0, :], shifted[:, 1, :], ALU.add))
                link(dve.reciprocal(total[:], total[:]))
                link(dve.tensor_tensor(core.bound[:], shifted[:, 0, :], total[:], ALU.mult))
                link(dve.tensor_scalar(core.rest[:], core.bound[:], -1.0, 1.0, ALU.mult, ALU.add))

            @block.scalar
            def _(act):
                act.wait_ge(asked, 1)
                act.activation(shifted[:], shifted[:], ACT.Exp).then_inc(exp_ready, 1)


def recur_prompt(nc, core, queries, gates, values, z_hg, gain, gated, state_out):
    CH = 4
    BLOCKS = T // (CH * P)
    LEVELS = [P // 2, P // 4, P // 8]
    LEAF = P // 8
    CLAMP = 85.0
    NL = len(LEVELS)
    UNITS_, CHUNKS_ = HH, HH * CH
    DS = NL + 2
    ES = NL + 4

    with ExitStack() as ctx:
        def sb(name, shape, dt=F32):
            return ctx.enter_context(nc.sbuf_tensor(f"hg_{name}", shape, dt))

        def per_head(name, shape):
            return [sb(f"{name}{h}", shape) for h in range(HH)]

        def psum(name):
            return [ctx.enter_context(nc.psum_tensor(f"hg_{name}{i}", [P, BANK], F32)) for i in range(2)]

        q, f = per_head("q", [P, BANK]), per_head("f", [P, BANK])
        k, b = per_head("k", [P, BANK]), per_head("b", [P, BANK])
        level = [per_head(f"level{n}_", [P, BANK]) for n in range(NL)]
        leaf_q, leaf_k = per_head("leaf_q", [P, BANK]), per_head("leaf_k", [P, BANK])
        q_run, k_rest = per_head("q_run", [P, BANK]), per_head("k_rest", [P, BANK])
        decay = per_head("decay", [P, CH])
        log_f = sb("log_f", [P, BANK])
        ones = sb("ones", [P, P])
        v, z = sb("v", [P, CH, W]), sb("z", [P, CH, W])
        gains = sb("gains", [P, W])
        masks = sb("masks", [P, NL + 1, P])
        masked = [sb(f"masked{i}", [P, NL + 1, P]) for i in range(2)]
        weights = [sb(f"weights{i}", [P, P]) for i in range(2)]
        k_rows = [sb(f"k_rows{i}", [P, P]) for i in range(2)]
        state = sb("state", [P, HH, P])
        o_rows, square = sb("o_rows", [P, CH, W]), sb("square", [P, CH, W])
        stat = sb("stat", [P, CH * HH])
        root = sb("root", [P, CH * HH])
        primer = nc.dram_tensor("hg_primer", (1, P), F32, kind="Internal").ap()
        att, turned, o_sum, kv = psum("att"), psum("turned"), psum("o_sum"), psum("kv")

        def sem(name):
            return core.sem(f"hg_{name}")

        raw_loaded = [sem(f"raw_loaded{h}") for h in range(HH)]
        v_loaded, z_loaded, gains_loaded = sem("v_loaded"), sem("z_loaded"), sem("gains_loaded")
        unit_ready = sem("unit_ready")
        consts, consts_step = sem("consts"), sem("consts_step")
        f_ready, k_ready, log_ready, b_ready = sem("f_ready"), sem("k_ready"), sem("log_ready"), sem("b_ready")
        diff_ready, exp_ready = sem("diff_ready"), sem("exp_ready")
        diff_step = sem("diff_step")
        att_ready, att_used, weights_ready = sem("att_ready"), sem("att_used"), sem("weights_ready")
        turned_ready, k_rows_ready = sem("turned_ready"), sem("k_rows_ready")
        o_ready, o_taken = sem("o_ready"), sem("o_taken")
        kv_ready, state_ready = sem("kv_ready"), sem("state_ready")
        masked_ready, post_step, mean_ready, root_ready = sem("masked_ready"), sem("post_step"), \
            sem("mean_ready"), sem("root_ready")
        rows_ready, stored = sem("rows_ready"), sem("stored")
        paced = sem("paced")
        POST = 5

        with nc.Block() as block:
            @block.sync
            def _(sp):
                sp.dma_start(primer, core.ident[0:1, :]).then_inc(stored, 16)
                sp.dma_start(gains[:], gain.partition_broadcast(P)).then_inc(gains_loaded, 16)
                with sp.Fori(0, BLOCKS) as blk:
                    columns, rows = bass.ds(blk * BANK, BANK), bass.ds(blk * BANK, BANK)
                    for h in range(HH):
                        sp.wait_ge(unit_ready, blk * HH + h + 1)
                        sp.dma_start(q[h][:], queries[h * P:(h + 1) * P, columns]).then_inc(raw_loaded[h], 16)
                        sp.dma_start(f[h][:], gates[h * P:(h + 1) * P, columns]).then_inc(raw_loaded[h], 16)
                        if h == 0:
                            sp.wait_ge(state_ready, (blk + 1) * CHUNKS_)
                            sp.dma_start(v[:], values[rows, :].rearrange("(c p) n -> p c n", p=P)).then_inc(v_loaded, 16)
                    sp.wait_ge(rows_ready, blk + 1)
                    sp.dma_start(z[:], z_hg[rows, :].rearrange("(c p) n -> p c n", p=P)).then_inc(z_loaded, 16)
                    sp.wait_ge(rows_ready, blk + 2)
                    sp.dma_start(gated[rows, :].rearrange("(c p) n -> p c n", p=P), o_rows[:]).then_inc(stored, 16)
                sp.wait_ge(state_ready, (BLOCKS + 1) * CHUNKS_)
                sp.dma_start(state_out.rearrange("h k v -> k h v"), state[:]).then_inc(stored, 16)
                sp.wait_ge(stored, 16 * (BLOCKS + 2))

            @block.gpsimd
            def _(pool):
                link = linker(pool, consts_step)
                link(pool.memset(masks[:], 1.0))
                for n, width in enumerate([2 * half for half in LEVELS] + [LEAF]):
                    tile = masks[:, n, :].rearrange("s (g t) -> s g t", t=width)
                    groups = P // width
                    link(pool.affine_select(out=tile, in_=tile, compare_op=ALU.is_ge, fill=0.0, base=0,
                                            pattern=[[-width, groups], [0, width]], channel_multiplier=1))
                    link(pool.affine_select(out=tile, in_=tile, compare_op=ALU.is_ge, fill=0.0, base=width - 1,
                                            pattern=[[width, groups], [0, width]], channel_multiplier=-1))
                for n in range(NL):
                    link(pool.tensor_tensor(masks[:, n, :], masks[:, n, :], masks[:, n + 1, :], ALU.subtract))
                for n in range(NL + 1):
                    link(pool.affine_select(out=masks[:, n, :], in_=masks[:, n, :], compare_op=ALU.is_ge, fill=0.0,
                                            base=0, pattern=[[1, P]], channel_multiplier=-1))
                link(pool.memset(ones[:], 1.0))
                link(pool.memset(state[:], 0.0))
                pool.sem_inc(consts, 1)
                with pool.Fori(0, BLOCKS) as blk:
                    for h in range(HH):
                        unit = blk * HH + h
                        pool.wait_ge(state_ready, blk * CHUNKS_ + (h + 1) * CH)
                        pool.wait_ge(raw_loaded[h], (blk + 1) * 32)
                        pool.sem_inc(paced, 1)
                        pool.tensor_scalar(f[h][:], f[h][:], core.rest[:, h:h + 1], core.bound[:, h:h + 1], ALU.mult,
                                           ALU.add).then_inc(f_ready, 1)
                        pool.wait_ge(f_ready, unit + 1)
                        pool.sem_inc(paced, 1)
                        pool.tensor_scalar(k[h][:], f[h][:], -1.0, 1.0, ALU.mult, ALU.add).then_inc(k_ready, 1)
                        pool.wait_ge(b_ready, unit + 1)

                        def difference(out, height, row):
                            blocks = b[h][:].rearrange("p (g t) -> p g t", t=height)
                            return pool.tensor_tensor(
                                out[:].rearrange("p (g t) -> p g t", t=height), blocks,
                                blocks[:, :, row:row + 1].to_broadcast([P, BANK // height, height]), ALU.subtract)

                        for n, half in enumerate(LEVELS):
                            difference(level[n][h], 2 * half, half - 1).then_inc(diff_ready, 1)
                        difference(k_rest[h], P, P - 1).then_inc(diff_ready, 1)
                        difference(leaf_k[h], LEAF, LEAF // 2 - 1).then_inc(diff_step, 1)
                        pool.wait_ge(diff_step, unit + 1)
                        pool.sem_inc(paced, 1)
                        pool.tensor_scalar(leaf_k[h][:], leaf_k[h][:], CLAMP, -CLAMP, ALU.min,
                                           ALU.max).then_inc(diff_ready, 1)

            @block.scalar
            def _(act):
                def prepare(blk, h):
                    unit = blk * HH + h
                    act.wait_ge(f_ready, unit + 1)
                    act.activation(log_f[:], f[h][:], ACT.Ln).then_inc(log_ready, 1)
                    act.wait_ge(b_ready, unit + 1)
                    ends = b[h][:].rearrange("p (c t) -> p c t", t=P)[:, :, P - 1]
                    act.wait_ge(state_ready, blk * CHUNKS_ + (h + 1) * CH)
                    act.activation(decay[h][:], ends, ACT.Exp)
                    act.activation(q_run[h][:], b[h][:], ACT.Exp).then_inc(exp_ready, 1)
                    for n, half in enumerate(LEVELS):
                        act.wait_ge(diff_ready, unit * DS + n + 1)
                        halves = level[n][h][:].rearrange("p (g u t) -> p g u t", u=2, t=half)
                        act.activation(halves[:, :, 1, :], halves[:, :, 1, :], ACT.Exp)
                        act.activation(halves[:, :, 0, :], halves[:, :, 0, :], ACT.Exp, scale=-1.0).then_inc(exp_ready, 1)
                    act.wait_ge(diff_ready, unit * DS + NL + 1)
                    act.activation(k_rest[h][:], k_rest[h][:], ACT.Exp, scale=-1.0).then_inc(exp_ready, 1)
                    act.wait_ge(diff_ready, unit * DS + NL + 2)
                    act.activation(leaf_q[h][:], leaf_k[h][:], ACT.Exp).then_inc(exp_ready, 1)
                    act.wait_ge(exp_ready, unit * ES + NL + 3)
                    act.activation(leaf_k[h][:], leaf_k[h][:], ACT.Exp, scale=-1.0).then_inc(exp_ready, 1)

                def rows_of_keys(blk, h, c):
                    n = h * CH + c
                    act.wait_ge(turned_ready, blk * CHUNKS_ + n + 1)
                    act.wait_ge(kv_ready, blk * CHUNKS_ + n + 1)
                    act.activation(k_rows[n % 2][:], turned[n % 2][:, 0:P], ACT.Copy).then_inc(k_rows_ready, 1)

                def take(blk, h, c):
                    n = h * CH + c
                    if n == 0:
                        act.wait_ge(stored, (blk + 1) * 16)
                    act.wait_ge(o_ready, blk * CHUNKS_ + n + 1)
                    act.activation(o_rows[:, c, h * P:(h + 1) * P], o_sum[n % 2][:, 0:P], ACT.Copy).then_inc(o_taken, 1)

                with act.Fori(0, BLOCKS) as blk:
                    in_order(lambda h: prepare(blk, h), lambda h, c: rows_of_keys(blk, h, c),
                             lambda h, c: take(blk, h, c))
                    act.wait_ge(mean_ready, blk + 1)
                    act.activation(root[:], stat[:], ACT.Sqrt).then_inc(root_ready, 1)

            @block.vector
            def _(dve):
                dve.sem_inc(unit_ready, UNITS_)
                dve.sem_inc(att_used, 2)
                dve.sem_inc(state_ready, CHUNKS_)
                dve.sem_inc(rows_ready, 1)
                dve.wait_ge(consts, 1)

                def prepare(blk, h):
                    unit = blk * HH + h
                    dve.wait_ge(log_ready, unit + 1)
                    for c in range(CH):
                        at = slice(c * P, (c + 1) * P)
                        last = dve.tensor_tensor_scan(b[h][:, at], ones[:], log_f[:, at], 0.0, ALU.mult, ALU.add)
                    last.then_inc(b_ready, 1)
                    dve.wait_ge(k_ready, unit + 1)
                    dve.wait_ge(exp_ready, unit * ES + 1)
                    dve.tensor_tensor(q_run[h][:], q_run[h][:], q[h][:], ALU.mult)
                    for n, half in enumerate(LEVELS):
                        dve.wait_ge(exp_ready, unit * ES + n + 2)
                        for u, factor in enumerate((k[h], q[h])):
                            at = [t[:].rearrange("p (g u t) -> p g u t", u=2, t=half)[:, :, u, :]
                                  for t in (level[n][h], factor)]
                            dve.tensor_tensor(at[0], at[0], at[1], ALU.mult)
                    dve.wait_ge(exp_ready, unit * ES + NL + 2)
                    dve.tensor_tensor(k_rest[h][:], k_rest[h][:], k[h][:], ALU.mult)
                    dve.wait_ge(exp_ready, unit * ES + NL + 4)
                    dve.tensor_tensor(leaf_q[h][:], leaf_q[h][:], q[h][:], ALU.mult)
                    dve.tensor_tensor(leaf_k[h][:], leaf_k[h][:], k[h][:], ALU.mult).then_inc(unit_ready, 1)

                def weigh(blk, h, c):
                    n = h * CH + c
                    dve.wait_ge(att_ready, blk * CHUNKS_ + n + 1)
                    dve.tensor_tensor(masked[n % 2][:], att[n % 2][:].rearrange("s (n t) -> s n t", t=P), masks[:],
                                      ALU.mult).then_inc(att_used, 1)
                    dve.wait_ge(att_used, blk * CHUNKS_ + n + 3)
                    dve.tensor_reduce(weights[n % 2][:], masked[n % 2][:].rearrange("s n t -> s t n"), AX.X,
                                      ALU.add).then_inc(weights_ready, 1)

                def advance(blk, h, c):
                    n = h * CH + c
                    dve.wait_ge(weights_ready, blk * CHUNKS_ + n + 1)
                    dve.wait_ge(kv_ready, blk * CHUNKS_ + n + 3)
                    dve.wait_ge(o_ready, blk * CHUNKS_ + n + 1)
                    dve.scalar_tensor_tensor(out=state[:, h, :], in0=state[:, h, :], scalar=decay[h][:, c:c + 1],
                                             in1=kv[n % 2][:, 0:P], op0=ALU.mult, op1=ALU.add).then_inc(state_ready, 1)

                with dve.Fori(0, BLOCKS) as blk:
                    in_order(lambda h: prepare(blk, h), lambda h, c: weigh(blk, h, c), lambda h, c: advance(blk, h, c))
                    link = linker(dve, post_step, blk * POST)
                    dve.wait_ge(o_taken, blk * CHUNKS_ + CHUNKS_ + 2)
                    link(dve.tensor_tensor(square[:], o_rows[:], o_rows[:], ALU.mult))
                    heads = [t[:].rearrange("p c (h d) -> p (c h) d", d=HD) for t in (square, o_rows)]
                    link(dve.tensor_reduce(stat[:], heads[0], AX.X, ALU.add))
                    dve.tensor_scalar(stat[:], stat[:], 1.0 / HD, EPS, ALU.mult, ALU.add).then_inc(mean_ready, 1)
                    dve.wait_ge(root_ready, blk + 1)
                    link(dve.reciprocal(root[:], root[:]))
                    link(dve.tensor_tensor(heads[1], heads[1],
                                           root[:].unsqueeze(2).to_broadcast([P, CH * HH, HD]), ALU.mult))
                    dve.wait_ge(gains_loaded, 16)
                    link(dve.tensor_tensor(o_rows[:], o_rows[:], gains[:].unsqueeze(1).to_broadcast([P, CH, W]),
                                           ALU.mult))
                    dve.wait_ge(z_loaded, (blk + 1) * 16)
                    dve.tensor_tensor(o_rows[:], o_rows[:], z[:], ALU.mult).then_inc(rows_ready, 1)

            @block.tensor
            def _(pe):
                pe.sem_inc(k_rows_ready, 2)
                pe.sem_inc(kv_ready, 2)
                pe.sem_inc(o_taken, 2)

                def pairs(blk, h, c):
                    n = h * CH + c
                    at = slice(c * P, (c + 1) * P)
                    if c == 0:
                        pe.wait_ge(unit_ready, blk * HH + h + 1 + UNITS_)
                    pe.wait_ge(att_used, blk * CHUNKS_ + n + 1)
                    for m in range(NL):
                        pe.matmul(att[n % 2][:, m * P:(m + 1) * P], level[m][h][:, at], level[m][h][:, at],
                                  start=True, stop=True)
                    pe.matmul(att[n % 2][:, NL * P:(NL + 1) * P], leaf_k[h][:, at], leaf_q[h][:, at], start=True,
                              stop=True).then_inc(att_ready, 1)
                    pe.wait_ge(k_rows_ready, blk * CHUNKS_ + n + 1)
                    pe.transpose(turned[n % 2][:, 0:P], k_rest[h][:, at], core.ident[:]).then_inc(turned_ready, 1)

                def sums(blk, h, c):
                    n = h * CH + c
                    at = slice(c * P, (c + 1) * P)
                    if n == 0:
                        pe.wait_ge(v_loaded, (blk + 1) * 16)
                    pe.wait_ge(o_taken, blk * CHUNKS_ + n + 1)
                    pe.wait_ge(weights_ready, blk * CHUNKS_ + n + 1)
                    pe.matmul(o_sum[n % 2][:, 0:P], weights[n % 2][:], v[:, c, h * P:(h + 1) * P], start=True,
                              stop=False)
                    pe.wait_ge(state_ready, (blk + 1) * CHUNKS_ + n)
                    pe.matmul(o_sum[n % 2][:, 0:P], q_run[h][:, at], state[:, h, :], start=False,
                              stop=True).then_inc(o_ready, 1)
                    pe.wait_ge(k_rows_ready, blk * CHUNKS_ + n + 3)
                    pe.matmul(kv[n % 2][:, 0:P], k_rows[n % 2][:], v[:, c, h * P:(h + 1) * P], start=True,
                              stop=True).then_inc(kv_ready, 1)

                pe.wait_ge(consts, 1)
                with pe.Fori(0, BLOCKS) as blk:
                    in_order(lambda h: None, lambda h, c: pairs(blk, h, c), lambda h, c: sums(blk, h, c))


def in_order(prepare, early, late):
    chunks = [(h, c) for h in range(HH) for c in range(HH)]
    for n, (h, c) in enumerate(chunks):
        if n == 0:
            prepare(0)
        if c == 0 and h + 1 < HH:
            prepare(h + 1)
        early(h, c)
        if n > 0:
            late(*chunks[n - 1])
    late(*chunks[-1])


def attend_memory(nc, core, queries, mem_k, mem_v, z_mem, gated):
    ST = NM // P
    BLK = 4
    TILES = 2 * BLK
    PAIRS = HH // 2
    SCALE = HD ** -0.5
    PASSES = NT // TILES

    with ExitStack() as ctx:
        def sb(name, shape, dt=F32):
            return ctx.enter_context(nc.sbuf_tensor(f"mem_{name}", shape, dt))

        def psum(name):
            return [ctx.enter_context(nc.psum_tensor(f"mem_{name}{i}", [P, BANK], F32)) for i in range(2)]

        k_rows, v = sb("k_rows", [P, ST, W]), sb("v", [P, ST, W])
        keys = sb("keys", [P, HH, NM])
        q = [sb(f"q{i}", [P, HH, BLK * P]) for i in range(2)]
        z = [sb(f"z{i}", [P, BLK, W]) for i in range(2)]
        o_rows = [sb(f"o_rows{i}", [P, BLK, W]) for i in range(2)]
        probs = [sb(f"probs{i}", [P, HH, NM]) for i in range(2)]
        neg_most = sb("neg_most", [P, 4, HH])
        bias = sb("bias", [P, 4, HH])
        row_sum, inverse = sb("row_sum", [P, 4, HH]), sb("inverse", [P, HH])
        pt = [sb(f"pt{i}", [P, BANK]) for i in range(4)]
        primer = nc.dram_tensor("mem_primer", (2, P), F32, kind="Internal").ap()
        scores, turned, o_sum = psum("scores"), psum("turned"), psum("o_sum")

        def sem(name):
            return core.sem(f"mem_{name}")

        kv_loaded, k_flipped, keys_ready = sem("kv_loaded"), sem("k_flipped"), sem("keys_ready")
        q_loaded, z_loaded = [sem(f"q_loaded{i}") for i in range(2)], [sem(f"z_loaded{i}") for i in range(2)]
        scored, exp_ready = sem("scored"), sem("exp_ready")
        most_step, bias_ready = sem("most_step"), sem("bias_ready")
        pt_ready, pt_copied = sem("pt_ready"), sem("pt_copied")
        o_ready = sem("o_ready")
        inverse_ready, rows_ready = sem("inverse_ready"), sem("rows_ready")
        stored = [sem(f"stored{i}") for i in range(2)]

        with nc.Block() as block:
            @block.sync
            def _(sp):
                def rows(dram, blk):
                    return dram[bass.ds(blk * BLK * P, BLK * P), :].rearrange("(t p) c -> p t c", p=P)

                sp.dma_start(k_rows[:], mem_k.rearrange("(t p) c -> p t c", p=P)).then_inc(kv_loaded, 16)
                sp.dma_start(v[:], mem_v.rearrange("(t p) c -> p t c", p=P)).then_inc(kv_loaded, 16)
                for i in range(2):
                    sp.dma_start(primer[i:i + 1, :], core.ident[0:1, :]).then_inc(stored[i], 16)
                with sp.Fori(0, PASSES) as it:
                    for i in range(2):
                        blk = it * 2 + i
                        sp.wait_ge(rows_ready, (blk + 1) * BLK)
                        sp.dma_start(q[i][:], queries[:, bass.ds(blk * BLK * P, BLK * P)]
                                     .rearrange("(h p) t -> p h t", p=P)).then_inc(q_loaded[i], 16)
                        sp.dma_start(z[i][:], rows(z_mem, blk)).then_inc(z_loaded[i], 16)
                    for i in range(2):
                        blk = it * 2 + i
                        sp.wait_ge(rows_ready, (blk + 3) * BLK)
                        sp.dma_start(rows(gated, blk), o_rows[i][:]).then_inc(stored[i], 16)
                for i in range(2):
                    sp.wait_ge(stored[i], 16 * (PASSES + 1))

            def in_step(score, turn, value):
                for u in range(TILES + 2):
                    if u < TILES:
                        score(u)
                    if 0 <= u - 1 < TILES:
                        turn(u - 1)
                    if u >= 2:
                        value(u - 2)

            @block.tensor
            def _(pe):
                pe.sem_inc(exp_ready, 2)
                pe.wait_ge(kv_loaded, 32)
                for t in range(ST):
                    for h in range(HH):
                        m = pe.transpose(turned[t][:, h * P:(h + 1) * P], k_rows[:, t, h * P:(h + 1) * P], core.ident[:])
                m.then_inc(k_flipped, 1)
                pe.wait_ge(keys_ready, 1)
                with pe.Fori(0, PASSES) as it:
                    def score(u):
                        for p in range(PAIRS):
                            n = (it * TILES + u) * PAIRS + p
                            if u % BLK == 0:
                                pe.wait_ge(q_loaded[u // BLK], (it + 1) * 16)
                            pe.wait_ge(exp_ready, n + 1)
                            for e in range(2):
                                h = 2 * p + e
                                m = pe.matmul(scores[p][:, e * NM:(e + 1) * NM],
                                              q[u // BLK][:, h, u % BLK * P:(u % BLK + 1) * P], keys[:, h, :],
                                              start=True, stop=True)
                            m.then_inc(scored, 1)

                    def turn(u):
                        for p in range(PAIRS):
                            n = (it * TILES + u) * PAIRS + p
                            pe.wait_ge(exp_ready, n + 3)
                            pe.wait_ge(pt_copied, n + 1)
                            for e in range(2):
                                for t in range(ST):
                                    m = pe.transpose(turned[p][:, (e * ST + t) * P:(e * ST + t + 1) * P],
                                                     probs[u % 2][:, 2 * p + e, t * P:(t + 1) * P], core.ident[:])
                            m.then_inc(pt_ready, 1)

                    def value(u):
                        tile = it * TILES + u
                        pe.wait_ge(pt_copied, (tile + 1) * PAIRS + 2)
                        pe.wait_ge(rows_ready, tile + 2 * BLK - 1)
                        for h in range(HH):
                            for t in range(ST):
                                m = pe.matmul(o_sum[u % 2][:, h * P:(h + 1) * P],
                                              pt[u % 2 * 2 + h // 2][:, (h % 2 * ST + t) * P:(h % 2 * ST + t + 1) * P],
                                              v[:, t, h * P:(h + 1) * P], start=(t == 0), stop=(t == ST - 1))
                        m.then_inc(o_ready, 1)

                    in_step(score, turn, value)

            @block.vector
            def _(dve):
                dve.sem_inc(pt_copied, 2)
                dve.sem_inc(rows_ready, 2 * BLK)
                dve.wait_ge(k_flipped, 1)
                for t in range(ST):
                    m = dve.tensor_copy(keys[:, :, t * P:(t + 1) * P], turned[t][:].rearrange("d (h s) -> d h s", s=P))
                m.then_inc(keys_ready, 1)
                with dve.Fori(0, PASSES) as it:
                    def score(u):
                        for p in range(PAIRS):
                            n = (it * TILES + u) * PAIRS + p
                            two = slice(2 * p, 2 * p + 2)
                            dve.wait_ge(scored, n + 1)
                            dve.tensor_reduce(neg_most[:, u % 4, two],
                                              scores[p][:].rearrange("p (e s) -> p e s", s=NM), AX.X, ALU.max,
                                              negate=True).then_inc(most_step, 1)
                            dve.wait_ge(most_step, n + 1)
                            dve.tensor_scalar(bias[:, u % 4, two], neg_most[:, u % 4, two], SCALE, None,
                                              ALU.mult).then_inc(bias_ready, 1)

                    def turn(u):
                        for p in range(PAIRS):
                            n = (it * TILES + u) * PAIRS + p
                            dve.wait_ge(pt_ready, n + 1)
                            dve.tensor_copy(pt[u % 2 * 2 + p][:], turned[p][:]).then_inc(pt_copied, 1)

                    def value(u):
                        tile = it * TILES + u
                        dve.wait_ge(exp_ready, (tile + 1) * PAIRS + 2)
                        dve.reciprocal(inverse[:], row_sum[:, u % 4, :]).then_inc(inverse_ready, 1)
                        if u % BLK == 0:
                            dve.wait_ge(z_loaded[u // BLK], (it + 1) * 16)
                            dve.wait_ge(stored[u // BLK], (it + 1) * 16)
                        dve.wait_ge(o_ready, tile + 1)
                        dve.wait_ge(inverse_ready, tile + 1)
                        for h in range(HH):
                            at = slice(h * P, (h + 1) * P)
                            m = dve.scalar_tensor_tensor(out=o_rows[u // BLK][:, u % BLK, at], in0=o_sum[u % 2][:, at],
                                                         scalar=inverse[:, h:h + 1], in1=z[u // BLK][:, u % BLK, at],
                                                         op0=ALU.mult, op1=ALU.mult)
                        m.then_inc(rows_ready, 1)
                        dve.wait_ge(rows_ready, tile + 2 * BLK + 1)

                    in_step(score, turn, value)

            @block.scalar
            def _(act):
                with act.Fori(0, PASSES) as it:
                    for u in range(TILES):
                        for p in range(PAIRS):
                            n = (it * TILES + u) * PAIRS + p
                            act.wait_ge(bias_ready, n + 1)
                            for h in (2 * p, 2 * p + 1):
                                m = act.activation(probs[u % 2][:, h, :], scores[p][:, h % 2 * NM:(h % 2 + 1) * NM],
                                                   ACT.Exp, scale=SCALE, bias=bias[:, u % 4, h:h + 1],
                                                   accum_out=row_sum[:, u % 4, h:h + 1])
                            m.then_inc(exp_ready, 1)


def weights_split(nc, core, tag, ctx, loads):
    tiles = sum(w.shape[0] // P for w in loads)
    hi = ctx.enter_context(nc.sbuf_tensor(f"{tag}_w_hi", [P, tiles, D], F32R))
    lo = ctx.enter_context(nc.sbuf_tensor(f"{tag}_w_lo", [P, tiles, D], F32R))
    with ExitStack() as inner:
        raw = [inner.enter_context(nc.sbuf_tensor(f"{tag}_w_raw{r}", [P, 2, D], F32)) for r in range(3)]
        loaded = [core.sem(f"{tag}_w_loaded{r}") for r in range(3)]
        hi_ready, lo_ready = core.sem(f"{tag}_w_hi_ready"), core.sem(f"{tag}_w_lo_ready")
        sources = [w.rearrange("(t p) n -> p t n", p=P)[:, t:t + 2, :] for w in loads for t in range(0, w.shape[0] // P, 2)]
        with nc.Block() as block:
            @block.sync
            def _(sp):
                for n, src in enumerate(sources):
                    if n >= 3:
                        sp.wait_ge(lo_ready, n - 2)
                    sp.dma_start(raw[n % 3][:], src).then_inc(loaded[n % 3], 16)

            @block.scalar
            def _(act):
                for n in range(len(sources)):
                    act.wait_ge(loaded[n % 3], 16 * (n // 3 + 1))
                    act.activation(hi[:, 2 * n:2 * n + 2, :], raw[n % 3][:], ACT.Copy).then_inc(hi_ready, 1)

            @block.vector
            def _(dve):
                for n in range(len(sources)):
                    dve.wait_ge(hi_ready, n + 1)
                    dve.tensor_tensor(lo[:, 2 * n:2 * n + 2, :], raw[n % 3][:], hi[:, 2 * n:2 * n + 2, :].bitcast(F32),
                                      ALU.subtract).then_inc(lo_ready, 1)
    return hi, lo


def merge_branches(nc, core, gated, gates, w_branches, mixed):
    TILES = NT + 1
    BT = W // P
    NB = 3
    KTILES = NB * BT
    HALVES = D // BANK
    with ExitStack() as ctx:
        def sb(name, shape, dt=F32):
            return [ctx.enter_context(nc.sbuf_tensor(f"mb_{name}{i}", shape, dt)) for i in range(2)]

        w_hi, w_lo = weights_split(nc, core, "mb", ctx, w_branches)
        g_in = sb("g_in", [P, KTILES * P])
        gate = sb("gate", [P, NB * HALVES, BANK])
        t_hi, t_lo = sb("t_hi", [P, KTILES, P], F32R), sb("t_lo", [P, KTILES, P], F32R)
        total = sb("total", [P, HALVES, BANK])
        term = ctx.enter_context(nc.sbuf_tensor("mb_term", [P, 2, BANK], F32))
        turned = [ctx.enter_context(nc.psum_tensor(f"mb_turned{i}", [P, BANK], F32)) for i in range(2)]
        out = [ctx.enter_context(nc.psum_tensor(f"mb_out{i}", [P, BANK], F32)) for i in range(NB * HALVES)]
        primer = nc.dram_tensor("mb_primer", (2, P), F32, kind="Internal").ap()

        def sem(name):
            return core.sem(f"mb_{name}")

        loaded = [sem(f"loaded{i}") for i in range(2)]
        stored = [sem(f"stored{i}") for i in range(2)]
        turned_ready, hi_ready, split = sem("turned_ready"), sem("hi_ready"), sem("split")
        multiplied = sem("multiplied")
        term_ready = sem("term_ready")
        total_ready = sem("total_ready")
        summed = sem("summed")
        PER = NB * HALVES

        def tiles(eng, body):
            with eng.Fori(0, TILES // 2) as it:
                for i in range(2):
                    body(it * 2 + i, i)
            body(TILES - 1, 0)

        with nc.Block() as block:
            @block.sync
            def _(sp):
                def load(tile, i):
                    sp.wait_ge(total_ready, tile + 1)
                    rows = bass.ds(tile * P, P)
                    sp.dma_start(g_in[i][:], gated[rows, :]).then_inc(loaded[i], 16)
                    sp.dma_start(gate[i][:], gates[:, rows, :].rearrange("g p n -> p g n")).then_inc(loaded[i], 16)

                def store(tile, i):
                    sp.wait_ge(total_ready, tile + 3)
                    sp.dma_start(mixed[bass.ds(tile * P, P), :], total[i][:].rearrange("p h n -> p (h n)")
                                 ).then_inc(stored[i], 16)

                for i in range(2):
                    sp.dma_start(primer[i:i + 1, :], core.ident[0:1, :]).then_inc(stored[i], 16)
                    load(i, i)
                with sp.Fori(0, (TILES - 3) // 2) as it:
                    for i in range(2):
                        store(it * 2 + i, i)
                        load(it * 2 + i + 2, i)
                store(TILES - 3, 0)
                load(TILES - 1, 0)
                store(TILES - 2, 1)
                store(TILES - 1, 0)
                sp.wait_ge(stored[0], 16 * (TILES // 2 + 2))
                sp.wait_ge(stored[1], 16 * (TILES // 2 + 1))

            @block.tensor
            def _(pe):
                pe.sem_inc(split, 2)
                pe.sem_inc(term_ready, PER)

                def turn(tile, i):
                    pe.wait_ge(loaded[i], (tile // 2 + 1) * 32 if isinstance(tile, int) else tile * 16 + (32 - 16 * i))
                    for b in range(NB):
                        pe.wait_ge(split, tile * NB + b + 1)
                        for t in range(BT):
                            m = pe.transpose(turned[b % 2 if i == 0 else (b + 1) % 2][:, t * P:(t + 1) * P],
                                             g_in[i][:, (b * BT + t) * P:(b * BT + t + 1) * P], core.ident[:])
                        m.then_inc(turned_ready, 1)

                def body(tile, i):
                    turn(tile, i)
                    for b in range(NB):
                        pe.wait_ge(split, tile * NB + b + 3)
                        for n in range(HALVES):
                            u = b * HALVES + n
                            pe.wait_ge(term_ready, tile * PER + u + 1)
                            for k in range(BT):
                                kk = b * BT + k
                                m = product(pe, out[u][:], (t_hi[i][:, kk, :], t_lo[i][:, kk, :]),
                                            [w[:, kk, n * BANK:(n + 1) * BANK] for w in (w_hi, w_lo)], k == 0,
                                            k == BT - 1)
                            m.then_inc(multiplied, 1)

                tiles(pe, body)

            @block.scalar
            def _(act):
                def body(tile, i):
                    for b in range(NB):
                        act.wait_ge(turned_ready, tile * NB + b + 1)
                        act.activation(t_hi[i][:, b * BT:(b + 1) * BT, :],
                                       turned[b % 2 if i == 0 else (b + 1) % 2][:].rearrange("p (t q) -> p t q", q=P),
                                       ACT.Copy).then_inc(hi_ready, 1)

                tiles(act, body)

            @block.vector
            def _(dve):
                dve.sem_inc(total_ready, 2)

                def body(tile, i):
                    for b in range(NB):
                        at = slice(b * BT, (b + 1) * BT)
                        dve.wait_ge(hi_ready, tile * NB + b + 1)
                        dve.tensor_tensor(t_lo[i][:, at, :],
                                          turned[b % 2 if i == 0 else (b + 1) % 2][:].rearrange("p (t q) -> p t q", q=P),
                                          t_hi[i][:, at, :].bitcast(F32), ALU.subtract).then_inc(split, 1)
                    for b in range(NB):
                        for n in range(HALVES):
                            u = b * HALVES + n
                            if b == 0 and n == 0:
                                dve.wait_ge(stored[i], (tile // 2 + 1) * 16 if isinstance(tile, int) else tile * 8 + (16 - 8 * i))
                            dve.wait_ge(multiplied, tile * PER + u + 1)
                            to = total[i][:, n, :] if b == 0 else term[:, n, :]
                            dve.tensor_tensor(to, out[u][:], gate[i][:, u, :], ALU.mult).then_inc(term_ready, 1)
                            dve.wait_ge(term_ready, tile * PER + u + 1 + PER)
                            if b:
                                m = dve.tensor_tensor(total[i][:, n, :], total[i][:, n, :], term[:, n, :], ALU.add)
                                if b < NB - 1 or n < HALVES - 1:
                                    m.then_inc(summed, 1)
                                else:
                                    m.then_inc(total_ready, 1)
                        if b:
                            dve.wait_ge(summed, tile * 3 + (2 if b == 1 else 3))

                tiles(dve, body)


def finish_rows(nc, core, mixed, w_o, x, x_s, gain, y, y_s):
    TILES = NT + 1
    HALVES = D // BANK
    with ExitStack() as ctx:
        def one(name, shape, dt=F32):
            return ctx.enter_context(nc.sbuf_tensor(f"fin_{name}", shape, dt))

        def sb(name, shape, dt=F32):
            return [one(f"{name}{i}", shape, dt) for i in range(2)]

        w_hi, w_lo = weights_split(nc, core, "fin", ctx, [w_o])
        m_in, x_in = sb("m_in", [P, D]), sb("x_in", [P, D])
        t_hi, t_lo = sb("t_hi", [P, KT, P], F32R), sb("t_lo", [P, KT, P], F32R)
        res, square = sb("res", [P, D]), one("square", [P, D])
        gains = one("gains", [P, D])
        stat = one("stat", [P, 4])
        turned = [ctx.enter_context(nc.psum_tensor(f"fin_turned{i}", [P, BANK], F32)) for i in range(2)]
        out = [ctx.enter_context(nc.psum_tensor(f"fin_out{i}", [P, BANK], F32)) for i in range(4)]
        primer = nc.dram_tensor("fin_primer", (2, P), F32, kind="Internal").ap()

        def sem(name):
            return core.sem(f"fin_{name}")

        loaded = [sem(f"loaded{i}") for i in range(2)]
        stored = [sem(f"stored{i}") for i in range(2)]
        gains_loaded, cleared = sem("gains_loaded"), sem("cleared")
        turned_ready, hi_ready, split = sem("turned_ready"), sem("hi_ready"), sem("split")
        multiplied, added = sem("multiplied"), sem("added")
        step, mean_ready, root_ready = sem("step"), sem("mean_ready"), sem("root_ready")
        normed = sem("normed")

        def tiles(eng, body):
            with eng.Fori(0, TILES // 2) as it:
                for i in range(2):
                    body(it * 2 + i, i, it)
            body(TILES - 1, 0, TILES // 2)

        with nc.Block() as block:
            @block.sync
            def _(sp):
                def load(tile, i, sample=False):
                    sp.wait_ge(normed, tile + 1)
                    sp.dma_start(m_in[i][:], mixed[bass.ds(tile * P, P), :]).then_inc(loaded[i], 16)
                    if sample:
                        sp.dma_start(x_in[i][0:B, :], x_s).then_inc(loaded[i], 16)
                    else:
                        sp.dma_start(x_in[i][:], x[bass.ds(tile * P, P), :]).then_inc(loaded[i], 16)

                def store(tile, i, sample=False):
                    sp.wait_ge(normed, tile + 3)
                    if sample:
                        sp.dma_start(y_s, res[i][0:B, :]).then_inc(stored[i], 16)
                    else:
                        sp.dma_start(y[bass.ds(tile * P, P), :], res[i][:]).then_inc(stored[i], 16)

                sp.dma_start(gains[:], gain.partition_broadcast(P)).then_inc(gains_loaded, 16)
                for i in range(2):
                    sp.dma_start(primer[i:i + 1, :], core.ident[0:1, :]).then_inc(stored[i], 16)
                    load(i, i)
                with sp.Fori(0, (TILES - 3) // 2) as it:
                    for i in range(2):
                        store(it * 2 + i, i)
                        load(it * 2 + i + 2, i)
                store(TILES - 3, 0)
                load(TILES - 1, 0, True)
                store(TILES - 2, 1)
                store(TILES - 1, 0, True)
                sp.wait_ge(stored[0], 16 * (TILES // 2 + 2))
                sp.wait_ge(stored[1], 16 * (TILES // 2 + 1))

            @block.tensor
            def _(pe):
                pe.sem_inc(split, 2)
                pe.sem_inc(added, 4)

                def body(tile, i, it):
                    pe.wait_ge(loaded[i], (it + 1) * 32)
                    for b in range(2):
                        pe.wait_ge(split, tile * 2 + b + 1)
                        for t in range(4):
                            m = pe.transpose(turned[b][:, t * P:(t + 1) * P],
                                             m_in[i][:, (b * 4 + t) * P:(b * 4 + t + 1) * P], core.ident[:])
                        m.then_inc(turned_ready, 1)
                    for n in range(HALVES):
                        pe.wait_ge(added, tile * 2 + n + 1)
                        for k in range(KT):
                            if n == 0 and k % 4 == 0:
                                pe.wait_ge(split, tile * 2 + k // 4 + 3)
                            m = product(pe, out[i * 2 + n][:], (t_hi[i][:, k, :], t_lo[i][:, k, :]),
                                        [w[:, k, n * BANK:(n + 1) * BANK] for w in (w_hi, w_lo)], k == 0, k == KT - 1)
                        m.then_inc(multiplied, 1)

                tiles(pe, body)

            @block.scalar
            def _(act):
                def body(tile, i, it):
                    for b in range(2):
                        act.wait_ge(turned_ready, tile * 2 + b + 1)
                        act.activation(t_hi[i][:, b * 4:b * 4 + 4, :], turned[b][:].rearrange("p (t q) -> p t q", q=P),
                                       ACT.Copy).then_inc(hi_ready, 1)
                    act.wait_ge(mean_ready, tile + 1)
                    act.activation(stat[:, 2:3], stat[:, 1:2], ACT.Sqrt).then_inc(root_ready, 1)

                tiles(act, body)

            @block.vector
            def _(dve):
                dve.sem_inc(normed, 2)
                dve.wait_ge(gains_loaded, 16)

                def body(tile, i, it):
                    rows = B if isinstance(tile, int) else P
                    for b in range(2):
                        dve.wait_ge(hi_ready, tile * 2 + b + 1)
                        dve.tensor_tensor(t_lo[i][:, b * 4:b * 4 + 4, :],
                                          turned[b][:].rearrange("p (t q) -> p t q", q=P),
                                          t_hi[i][:, b * 4:b * 4 + 4, :].bitcast(F32), ALU.subtract).then_inc(split, 1)
                    dve.wait_ge(stored[i], (it + 1) * 16)
                    dve.wait_ge(loaded[i], (it + 1) * 32)
                    for n in range(HALVES):
                        dve.wait_ge(multiplied, tile * 2 + n + 1)
                        dve.tensor_tensor(res[i][0:rows, n * BANK:(n + 1) * BANK], out[i * 2 + n][0:rows, :],
                                          x_in[i][0:rows, n * BANK:(n + 1) * BANK], ALU.add).then_inc(added, 1)
                    dve.wait_ge(added, tile * 2 + 6)
                    dve.tensor_tensor_reduce(square[0:rows, :], res[i][0:rows, :], res[i][0:rows, :], 1.0, 0.0, ALU.mult,
                                             ALU.add, stat[0:rows, 0:1]).then_inc(step, 1)
                    dve.wait_ge(step, tile * 2 + 1)
                    dve.tensor_scalar(stat[0:rows, 1:2], stat[0:rows, 0:1], 1.0 / D, EPS, ALU.mult,
                                      ALU.add).then_inc(mean_ready, 1)
                    dve.wait_ge(root_ready, tile + 1)
                    dve.reciprocal(stat[0:rows, 3:4], stat[0:rows, 2:3]).then_inc(step, 1)
                    dve.wait_ge(step, tile * 2 + 2)
                    dve.scalar_tensor_tensor(out=res[i][0:rows, :], in0=res[i][0:rows, :], scalar=stat[0:rows, 3:4],
                                             in1=gains[0:rows, :], op0=ALU.mult, op1=ALU.mult).then_inc(normed, 1)
                    dve.wait_ge(normed, tile + 3)

                tiles(dve, body)


def unpack_sample(nc, core, sample, s_raw, s_sigmoid, s_silu, fox_k_s, fox_v_s, gates, gated):
    with ExitStack() as ctx:
        part = [ctx.enter_context(nc.sbuf_tensor(f"up_part{i}", [P, W], F32)) for i in range(2)]
        sigmoid = ctx.enter_context(nc.sbuf_tensor("up_sigmoid", [P, W], F32))
        silu = ctx.enter_context(nc.sbuf_tensor("up_silu", [P, W], F32))
        zeros = ctx.enter_context(nc.sbuf_tensor("up_zeros", [P - B, W], F32))
        loaded, summed, sigmoid_ready, silu_ready, cleared, stored = (
            core.sem(f"up_{n}") for n in ("loaded", "summed", "sigmoid_ready", "silu_ready", "cleared", "stored"))
        with nc.Block() as block:
            @block.sync
            def _(sp):
                for i in range(2):
                    sp.dma_start(part[i][:], sample[:, i * B:(i + 1) * B, :]).then_inc(loaded, 16)
                sp.wait_ge(cleared, 1)
                n = 0
                for g in range(NGATE):
                    sp.dma_start(gates[g, T + B:T + P, :], zeros[:]).then_inc(stored, 16)
                for b in range(3):
                    sp.dma_start(gated[T + B:T + P, b * W:(b + 1) * W], zeros[:]).then_inc(stored, 16)
                n += NGATE + 3
                sp.wait_ge(summed, 1)
                sp.dma_start(s_raw, part[0][:]).then_inc(stored, 16)
                for name, dst in (("fk", fox_k_s), ("fv", fox_v_s)):
                    g = len(TURNED) + PLAIN.index(name)
                    sp.dma_start(dst, part[0][g * B:(g + 1) * B, :]).then_inc(stored, 16)
                sp.wait_ge(sigmoid_ready, 1)
                sp.dma_start(s_sigmoid, sigmoid[:]).then_inc(stored, 16)
                for g in range(NGATE):
                    at = (FIRST_GATE + g) * B
                    sp.dma_start(gates[g, T:T + B, :], sigmoid[at:at + B, :]).then_inc(stored, 16)
                sp.wait_ge(silu_ready, 1)
                sp.dma_start(s_silu, silu[:]).then_inc(stored, 16)
                n += 5 + NGATE
                sp.wait_ge(stored, n * 16)

            @block.gpsimd
            def _(pool):
                pool.memset(zeros[:], 0.0).then_inc(cleared, 1)

            @block.vector
            def _(dve):
                dve.wait_ge(loaded, 32)
                dve.tensor_tensor(part[0][:], part[0][:], part[1][:], ALU.add).then_inc(summed, 1)
                dve.wait_ge(sigmoid_ready, 1)
                dve.tensor_tensor(silu[:], part[0][:], sigmoid[:], ALU.mult).then_inc(silu_ready, 1)

            @block.scalar
            def _(act):
                act.wait_ge(summed, 1)
                act.activation(sigmoid[:], part[0][:], ACT.Sigmoid).then_inc(sigmoid_ready, 1)


def attend_cache(nc, core, tag, heads, pages, k_pages, v_pages, query, z_row, gated, table=None, logf_pages=None,
                 key_new=None, value_new=None, logf_new=None):
    dim = W // heads
    scale = dim ** -0.5
    GP = min(4, pages)
    GB = pages // GP
    SLOTS = 4
    RB = SLOTS // GB
    GROUPS = B * GB
    paged = table is not None
    with ExitStack() as ctx:
        def sb(name, shape, dt=F32):
            return ctx.enter_context(nc.sbuf_tensor(f"{tag}_{name}", shape, dt))

        def psum(name, shape):
            return ctx.enter_context(nc.psum_tensor(f"{tag}_{name}", shape, F32))

        slot = [sb(f"slot{s}", [P, GP, W]) for s in range(SLOTS)]
        q_all = sb("q_all", [P, B, W])
        scores = sb("scores", [P, B, pages, heads])
        most = sb("most", [P, B, heads])
        sums = sb("sums", [P, B, heads])
        bias, spread = sb("bias", [B, heads]), sb("spread", [B, B, heads])
        own = {n: sb(n, [B, heads]) for n in ("most_b", "total", "inverse")}
        probs = [sb(f"probs{s}", [P, GP, heads]) for s in range(SLOTS)]
        head_mask = sb("head_mask", [heads, W])
        masked, row = sb("masked", [heads, W]), sb("row", [1, W])
        ones = sb("ones", [P, P])
        o, z = sb("o", [B, W]), sb("z", [B, W])
        o_dram = nc.dram_tensor(f"{tag}_o_rows", (B, W), F32, kind="Internal").ap()
        most_t = psum("most_t", [B, heads, P])
        spread_all = psum("spread_all", [P, B, heads])
        small_bank = psum("small", [P, 2, heads])
        small, suffix_all = small_bank[0:B, 0, :], small_bank[:, 1, :]
        o_heads = psum("o_heads", [heads, W])
        o_row = psum("o_row", [1, W])
        if paged:
            table_sb = sb("table", [1, B * pages], I32)
            rows_sb = sb("rows", [P, 1], I32)
            logf = sb("logf", [P, PAGE, heads])
            run = sb("run", [P, heads, PAGE])
            later = sb("later", [P, P])
            back_bias = psum("back_bias", [P, heads, P])
            suffix = sb("suffix", [P, heads])
            q_b, k_b, v_b = sb("q_b", [B, W]), sb("k_b", [B, W]), sb("v_b", [B, W])
            product_b = sb("product_b", [B, W])
            gate_b, s_new, p_new = sb("gate_b", [B, heads]), sb("s_new", [B, heads]), sb("p_new", [B, heads])

        def sem(name):
            return core.sem(f"{tag}_{name}")

        ready = [sem(f"loaded{s}") for s in range(SLOTS)]
        slot_free = sem("slot_free")
        start_loaded, rows_loaded, logf_loaded, z_loaded = sem("start_loaded"), sem("rows_loaded"), \
            sem("logf_loaded"), sem("z_loaded")
        consts, pool_step = sem("consts"), sem("pool_step")
        multiplied, step = sem("multiplied"), sem("step")
        run_ready, suffix_ready, bias_turned = sem("run_ready"), sem("suffix_ready"), sem("bias_turned")
        back_ready, suffix_taken = sem("back_ready"), sem("suffix_taken")
        most_ready, most_turned, spread_ready, spread_done = sem("most_ready"), sem("most_turned"), \
            sem("spread_ready"), sem("spread_done")
        new_asked, new_ready = sem("new_asked"), sem("new_ready")
        exp_asked, exp_ready, sums_ready, sums_done = sem("exp_asked"), sem("exp_ready"), sem("sums_ready"), \
            sem("sums_done")
        probs_ready, masked_ready, row_ready, row_copied = sem("probs_ready"), \
            sem("masked_ready"), sem("row_ready"), sem("row_copied")
        paced = sem("paced")
        row_stored, o_loaded, done, stored = sem("row_stored"), sem("o_loaded"), sem("done"), sem("stored")
        START = 5 if paged else 0

        with nc.Block() as block:
            @block.sync
            def _(sp):
                sp.sem_inc(slot_free, SLOTS)
                if paged:
                    sp.dma_start(table_sb[:], table.rearrange("b (o g) -> o (b g)", o=1)).then_inc(rows_loaded, 16)
                    with nc.allow_non_contiguous_dma(reason="a table of 128 pages, one in a partition"):
                        sp.dma_start(rows_sb[:], table.rearrange("b (g o) -> (b g) o", o=1)).then_inc(rows_loaded, 16)
                    sp.wait_ge(rows_loaded, 32)
                sp.dma_start(q_all[:], query.partition_broadcast(P)).then_inc(start_loaded, 16)

                def load(source, first):
                    with sp.Fori(0, B // RB) as it:
                        for s in range(SLOTS):
                            r, g = s // GB, s % GB
                            group = it * SLOTS + s
                            sp.wait_ge(slot_free, group + first + 1)
                            for p in range(GP):
                                n = group * GP + p
                                page = sp.value_load(table_sb[0:1, bass.ds(n, 1)], min_val=0,
                                                     max_val=source.shape[0] - 1) if paged else n
                                sp.dma_start(slot[s][:, p, :], source[bass.ds(page, 1)].rearrange("o p n -> (o p) n")
                                             ).then_inc(ready[s], 16)

                load(k_pages, 0)
                if paged:
                    for dst, src in ((q_b, query), (k_b, key_new), (v_b, value_new), (gate_b, logf_new)):
                        sp.dma_start(dst[:], src).then_inc(start_loaded, 16)
                sp.dma_start(z[:], z_row).then_inc(z_loaded, 16)
                load(v_pages, GROUPS)
                sp.wait_ge(row_stored, B * 16)
                sp.dma_start(o[:], o_dram).then_inc(o_loaded, 16)
                sp.wait_ge(done, 1)
                sp.dma_start(gated, o[:]).then_inc(stored, 16)
                sp.wait_ge(stored, 16)

            @block.gpsimd
            def _(pool):
                link = linker(pool, pool_step)
                link(pool.memset(ones[:], 1.0))
                link(pool.memset(head_mask[:], 1.0))
                own_columns = head_mask[:].rearrange("h (g d) -> h g d", d=dim)
                link(pool.affine_select(out=own_columns, in_=own_columns, compare_op=ALU.is_equal, fill=0.0, base=0,
                                        pattern=[[-1, heads], [0, dim]], channel_multiplier=1))
                if paged:
                    link(pool.memset(later[:], 1.0))
                    by_row = later[:].rearrange("x (b g) -> x b g", g=pages)
                    link(pool.affine_select(out=by_row, in_=by_row, compare_op=ALU.is_ge, fill=0.0, base=0,
                                            pattern=[[-pages, B], [-1, pages]], channel_multiplier=1))
                    link(pool.affine_select(out=by_row, in_=by_row, compare_op=ALU.is_ge, fill=0.0, base=pages - 1,
                                            pattern=[[pages, B], [0, pages]], channel_multiplier=-1))
                    pool.wait_ge(rows_loaded, 32)
                    pool.indirect_dma_start(out=logf[:].rearrange("p t h -> p (t h)"), out_offset=None,
                                            in_=logf_pages.rearrange("n t h -> n (t h)"),
                                            in_offset=bass.IndirectOffsetOnAxis(ap=rows_sb[:, 0:1], axis=0)
                                            ).then_inc(logf_loaded, 16)
                pool.sem_inc(consts, 1)

            @block.vector
            def _(dve):
                link = linker(dve, step)
                dve.wait_ge(consts, 1)
                if paged:
                    dve.wait_ge(logf_loaded, 16)
                    for h in range(heads):
                        last = dve.tensor_tensor_scan(run[:, h, :], ones[:], logf[:, :, h], 0.0, ALU.mult, ALU.add)
                    last.then_inc(run_ready, 1)
                    dve.wait_ge(suffix_ready, 1)
                    link(dve.tensor_copy(suffix[:], suffix_all))
                    dve.sem_inc(suffix_taken, 1)
                    dve.tensor_tensor(run[:], suffix[:].unsqueeze(2).to_broadcast([P, heads, PAGE]), run[:],
                                      ALU.subtract).then_inc(bias_turned, 1)
                dve.wait_ge(start_loaded, 16)
                with dve.Fori(0, B // RB) as it:
                    for s in range(SLOTS):
                        r, g = s // GB, s % GB
                        group = it * SLOTS + s
                        at = q_all[:, bass.ds(it * RB + r, 1), :].to_broadcast([P, GP, W])
                        dve.wait_ge(ready[s], (it + 1) * 16 * GP)
                        dve.tensor_tensor(slot[s][:], slot[s][:], at, ALU.mult).then_inc(multiplied, 1)
                        dve.wait_ge(multiplied, group + 1)
                        dve.tensor_reduce(scores[:, bass.ds(it * RB + r, 1), g * GP:(g + 1) * GP, :]
                                          .rearrange("p o g h -> p (o g) h"),
                                          slot[s][:].rearrange("p g (h d) -> p g h d", d=dim), AX.X,
                                          ALU.add).then_inc(slot_free, 1)
                dve.wait_ge(slot_free, GROUPS + SLOTS)
                flat = scores[:].rearrange("p b g h -> p (b g) h")
                if paged:
                    dve.wait_ge(back_ready, 1)
                    link(dve.scalar_tensor_tensor(out=flat, in0=flat, scalar=scale,
                                                  in1=back_bias[:].rearrange("p h n -> p n h"), op0=ALU.mult,
                                                  op1=ALU.add))
                else:
                    link(dve.tensor_scalar(flat, flat, scale, None, ALU.mult))
                dve.tensor_reduce(most[:], scores[:].rearrange("p b g h -> p b h g"), AX.X, ALU.max
                                  ).then_inc(most_ready, 1)
                if paged:
                    dve.wait_ge(start_loaded, START * 16)
                    link(dve.tensor_tensor(product_b[:], q_b[:], k_b[:], ALU.mult))
                    link(dve.tensor_reduce(s_new[:], product_b[:].rearrange("b (h d) -> b h d", d=dim), AX.X, ALU.add))
                    link(dve.tensor_scalar(s_new[:], s_new[:], scale, None, ALU.mult))
                dve.wait_ge(most_turned, 1)
                link(dve.tensor_reduce(own["most_b"][:], most_t[:], AX.X, ALU.max))
                if paged:
                    link(dve.tensor_tensor(own["most_b"][:], own["most_b"][:], gate_b[:], ALU.add))
                    link(dve.tensor_tensor(own["most_b"][:], own["most_b"][:], s_new[:], ALU.max))
                    link(dve.tensor_tensor(bias[:], gate_b[:], own["most_b"][:], ALU.subtract))
                    link(dve.tensor_tensor(s_new[:], s_new[:], own["most_b"][:], ALU.subtract))
                    dve.sem_inc(new_asked, 1)
                else:
                    link(dve.tensor_scalar(bias[:], own["most_b"][:], -1.0, None, ALU.mult))
                dve.tensor_tensor(spread[:], core.ident[0:B, 0:B].unsqueeze(2).to_broadcast([B, B, heads]),
                                  bias[:].unsqueeze(1).to_broadcast([B, B, heads]), ALU.mult).then_inc(spread_ready, 1)
                dve.wait_ge(spread_done, 1)
                dve.wait_ge(most_turned, 1)
                dve.tensor_tensor(scores[:], scores[:], spread_all[:].unsqueeze(2).to_broadcast([P, B, pages, heads]),
                                  ALU.add).then_inc(exp_asked, 1)
                dve.wait_ge(exp_ready, 1)
                dve.tensor_reduce(sums[:], scores[:].rearrange("p b g h -> p b h g"), AX.X, ALU.add
                                  ).then_inc(sums_ready, 1)
                dve.wait_ge(sums_done, 1)
                if paged:
                    dve.wait_ge(new_ready, 1)
                    link(dve.tensor_tensor(own["total"][:], small, p_new[:], ALU.add))
                else:
                    link(dve.tensor_copy(own["total"][:], small))
                link(dve.reciprocal(own["inverse"][:], own["total"][:]))
                dve.sem_inc(masked_ready, 1)
                with dve.Fori(0, B) as b:
                    dve.wait_ge(slot_free, (b + 1) * GB + GROUPS + SLOTS)
                    dve.tensor_tensor(masked[:], o_heads[:], head_mask[:], ALU.mult).then_inc(masked_ready, 1)
                    dve.wait_ge(row_ready, b + 1)
                    dve.tensor_copy(row[:], o_row[:]).then_inc(row_copied, 1)
                    dve.wait_ge(row_stored, (b + 1) * 16)
                dve.wait_ge(o_loaded, 16)
                by_head = o[:].rearrange("b (h d) -> b h d", d=dim)
                if paged:
                    link(dve.tensor_tensor(product_b[:].rearrange("b (h d) -> b h d", d=dim),
                                           v_b[:].rearrange("b (h d) -> b h d", d=dim),
                                           p_new[:].unsqueeze(2).to_broadcast([B, heads, dim]), ALU.mult))
                    link(dve.tensor_tensor(o[:], o[:], product_b[:], ALU.add))
                link(dve.tensor_tensor(by_head, by_head, own["inverse"][:].unsqueeze(2).to_broadcast([B, heads, dim]),
                                       ALU.mult))
                dve.wait_ge(z_loaded, 16)
                dve.tensor_tensor(o[:], o[:], z[:], ALU.mult).then_inc(done, 1)

            @block.scalar
            def _(act):
                if paged:
                    act.wait_ge(new_asked, 1)
                    act.activation(p_new[:], s_new[:], ACT.Exp).then_inc(new_ready, 1)
                act.wait_ge(exp_asked, 1)
                act.activation(scores[:], scores[:], ACT.Exp).then_inc(exp_ready, 1)
                with act.Fori(0, B // RB) as it:
                    for s in range(SLOTS):
                        r, g = s // GB, s % GB
                        act.wait_ge(slot_free, it * SLOTS + s + GROUPS + 1)
                        act.wait_ge(exp_ready, 1)
                        act.activation(probs[s][:], scores[:, bass.ds(it * RB + r, 1), g * GP:(g + 1) * GP, :]
                                       .rearrange("p o g h -> p (o g) h"), ACT.Copy).then_inc(probs_ready, 1)
                        if g == GB - 1:
                            b = it * RB + r
                            act.wait_ge(row_copied, b + 1)
                            act.dma_start(o_dram[bass.ds(b, 1), :], row[:]).then_inc(row_stored, 16)

            @block.tensor
            def _(pe):
                pe.wait_ge(consts, 1)
                if paged:
                    pe.wait_ge(run_ready, 1)
                    pe.matmul(suffix_all, later[:], run[:, :, PAGE - 1], start=True, stop=True).then_inc(suffix_ready, 1)
                    pe.wait_ge(bias_turned, 1)
                    for h in range(heads):
                        m = pe.transpose(back_bias[:, h, :], run[:, h, :], core.ident[:])
                    m.then_inc(back_ready, 1)
                pe.wait_ge(most_ready, 1)
                for h in range(heads):
                    m = pe.transpose(most_t[:, h, :], most[:, :, h], core.ident[:])
                m.then_inc(most_turned, 1)
                pe.wait_ge(spread_ready, 1)
                pe.matmul(spread_all[:].rearrange("p b h -> p (b h)"), ones[0:B, :],
                          spread[:].rearrange("c b h -> c (b h)"), start=True, stop=True).then_inc(spread_done, 1)
                pe.wait_ge(sums_ready, 1)
                for h in range(heads):
                    m = pe.matmul(small[:, h:h + 1], sums[:, :, h], ones[:, 0:1], start=True, stop=True)
                m.then_inc(sums_done, 1)
                with pe.Fori(0, B // RB) as it:
                    for s in range(SLOTS):
                        r, g = s // GB, s % GB
                        group = it * SLOTS + s
                        if g == 0:
                            pe.wait_ge(masked_ready, it * RB + r + 1)
                        pe.wait_ge(probs_ready, group + 1)
                        pe.wait_ge(ready[s], (it + 1 + B // RB) * 16 * GP)
                        for p in range(GP):
                            m = pe.matmul(o_heads[:], probs[s][:, p, :], slot[s][:, p, :], start=(g == 0 and p == 0),
                                          stop=(g == GB - 1 and p == GP - 1))
                        m.then_inc(slot_free, 1)
                        if g == GB - 1:
                            pe.wait_ge(masked_ready, it * RB + r + 2)
                            pe.sem_inc(paced, 1)
                            pe.matmul(o_row[:], ones[0:heads, 0:1], masked[:], start=True, stop=True).then_inc(row_ready, 1)


def recur_sample(nc, core, sigmoid, query, values, z_row, state_in, gain, gated, state_out):
    with ExitStack() as ctx:
        def sb(name, shape):
            return ctx.enter_context(nc.sbuf_tensor(f"rs_{name}", shape, F32))

        sg, q = sb("sg", [B, W]), sb("q", [B, W])
        f_t, k_t, q_t = sb("f_t", [P, HH, B]), sb("k_t", [P, HH, B]), sb("q_t", [P, HH, B])
        state, v, kv = [sb(f"state{i}", [P, HH, P]) for i in range(2)], [sb(f"v{i}", [P, HH, P]) for i in range(2)], \
            [sb(f"kv{i}", [P, HH, P]) for i in range(2)]
        o_t, o, square = sb("o_t", [P, HH, B]), sb("o", [B, W]), sb("square", [B, W])
        z, gains, stat = sb("z", [B, W]), sb("gains", [B, W]), sb("stat", [B, 3, HH])
        turned = ctx.enter_context(nc.psum_tensor("rs_turned", [P, 2, HH, B], F32))
        out = [ctx.enter_context(nc.psum_tensor(f"rs_out{i}", [P, HH, B], F32)) for i in range(2)]
        back = ctx.enter_context(nc.psum_tensor("rs_back", [B, W], F32))
        primer = nc.dram_tensor("rs_primer", (2, P), F32, kind="Internal").ap()

        def sem(name):
            return core.sem(f"rs_{name}")

        loaded, small_loaded, turned_ready, step = sem("loaded"), sem("small_loaded"), sem("turned_ready"), sem("step")
        state_loaded, stored = [sem(f"state_loaded{i}") for i in range(2)], [sem(f"stored{i}") for i in range(2)]
        used = sem("used")
        ready, kv_ready, out_ready, taken = sem("ready"), sem("kv_ready"), sem("out_ready"), sem("taken")
        back_ready, mean_ready, root_ready, done, o_stored, faded = sem("back_ready"), sem("mean_ready"), \
            sem("root_ready"), sem("done"), sem("o_stored"), sem("faded")

        with nc.Block() as block:
            @block.sync
            def _(sp):
                sp.dma_start(sg[:], sigmoid).then_inc(loaded, 16)
                sp.dma_start(q[:], query).then_inc(loaded, 16)
                sp.dma_start(z[:], z_row).then_inc(small_loaded, 16)
                sp.dma_start(gains[:], gain.partition_broadcast(B)).then_inc(small_loaded, 16)
                for i in range(2):
                    sp.dma_start(primer[i:i + 1, :], core.ident[0:1, :]).then_inc(stored[i], 16)
                with sp.Fori(0, B // 2) as it:
                    for i in range(2):
                        b = it * 2 + i
                        sp.wait_ge(taken, b + 1)
                        sp.wait_ge(stored[i], (it + 1) * 16)
                        sp.dma_start(state[i][:], state_in[bass.ds(b, 1)].rearrange("o h k v -> k (o h) v")
                                     ).then_inc(state_loaded[i], 16)
                        sp.dma_start(v[i][:], values[bass.ds(b, 1), :].to_broadcast([P, W])
                                     .rearrange("p (h d) -> p h d", h=HH)).then_inc(state_loaded[i], 16)
                    for i in range(2):
                        b = it * 2 + i
                        sp.wait_ge(ready, b + 1)
                        sp.dma_start(state_out[bass.ds(b, 1)].rearrange("o h k v -> k (o h) v"), state[i][:]
                                     ).then_inc(stored[i], 16)
                sp.wait_ge(done, 1)
                sp.dma_start(gated, o[:]).then_inc(o_stored, 16)
                sp.wait_ge(o_stored, 16)
                for i in range(2):
                    sp.wait_ge(stored[i], (B // 2 + 1) * 16)

            @block.tensor
            def _(pe):
                pe.wait_ge(loaded, 32)
                for n, src in enumerate((sg, q)):
                    for h in range(HH):
                        m = pe.transpose(turned[:, n, h, :], src[:, h * P:(h + 1) * P], core.ident[0:B, 0:B])
                m.then_inc(turned_ready, 1)
                pe.wait_ge(step, 2 + 2 * HH)
                with pe.Fori(0, B // 2) as it:
                    for i in range(2):
                        b = it * 2 + i
                        pe.wait_ge(ready, b + 1)
                        pe.wait_ge(taken, b + 1)
                        for h in range(HH):
                            m = pe.matmul(out[i][:, h, :], state[i][:, h, :], q_t[:, h, :], start=True, stop=True)
                        m.then_inc(out_ready, 1)
                pe.wait_ge(taken, B + 2)
                for h in range(HH):
                    m = pe.transpose(back[:, h * P:(h + 1) * P], o_t[:, h, :], core.ident[:])
                m.then_inc(back_ready, 1)

            @block.vector
            def _(dve):
                link = linker(dve, step)
                dve.wait_ge(turned_ready, 1)
                link(dve.tensor_copy(q_t[:], turned[:, 1]))
                for h in range(HH):
                    link(dve.tensor_scalar(f_t[:, h, :], turned[:, 0, h, :], core.rest[:, h:h + 1],
                                           core.bound[:, h:h + 1], ALU.mult, ALU.add))
                    link(dve.tensor_scalar(k_t[:, h, :], f_t[:, h, :], -1.0, 1.0, ALU.mult, ALU.add))
                dve.sem_inc(step, 1)
                link.done[0] += 1
                with dve.Fori(0, B // 2) as it:
                    for i in range(2):
                        b = it * 2 + i
                        dve.wait_ge(state_loaded[i], (it + 1) * 32)
                        dve.tensor_tensor(kv[i][:], v[i][:], k_t[:, :, bass.ds(b, 1)].to_broadcast([P, HH, P]),
                                          ALU.mult).then_inc(kv_ready, 1)
                        dve.tensor_tensor(state[i][:], state[i][:], f_t[:, :, bass.ds(b, 1)].to_broadcast([P, HH, P]),
                                          ALU.mult).then_inc(faded, 1)
                        dve.wait_ge(faded, b + 1)
                        dve.wait_ge(kv_ready, b + 1)
                        dve.tensor_tensor(state[i][:], state[i][:], kv[i][:], ALU.add).then_inc(ready, 1)
                dve.wait_ge(back_ready, 1)
                heads = [t[:].rearrange("b (h d) -> b h d", h=HH) for t in (o, square)]
                link(dve.tensor_copy(o[:], back[:]))
                link(dve.tensor_tensor(square[:], o[:], o[:], ALU.mult))
                link(dve.tensor_reduce(stat[:, 0, :], heads[1], AX.X, ALU.add))
                dve.tensor_scalar(stat[:, 1, :], stat[:, 0, :], 1.0 / HD, EPS, ALU.mult, ALU.add).then_inc(mean_ready, 1)
                dve.wait_ge(root_ready, 1)
                link(dve.reciprocal(stat[:, 2, :], stat[:, 1, :]))
                link(dve.tensor_tensor(heads[0], heads[0], stat[:, 2, :].unsqueeze(2).to_broadcast([B, HH, HD]),
                                       ALU.mult))
                dve.wait_ge(small_loaded, 32)
                link(dve.tensor_tensor(o[:], o[:], gains[:], ALU.mult))
                dve.tensor_tensor(o[:], o[:], z[:], ALU.mult).then_inc(done, 1)

            @block.scalar
            def _(act):
                act.sem_inc(taken, 2)
                with act.Fori(0, B // 2) as it:
                    for i in range(2):
                        b = it * 2 + i
                        act.wait_ge(out_ready, b + 1)
                        act.activation(o_t[:, :, bass.ds(b, 1)], out[i][:, :, bass.ds(b, 1)], ACT.Copy
                                       ).then_inc(taken, 1)
                act.wait_ge(mean_ready, 1)
                act.activation(stat[:, 1, :], stat[:, 1, :], ACT.Sqrt).then_inc(root_ready, 1)


def decoder_step(nc, x_prompt, x_sample, mem_prompt, cache_fox_k, cache_fox_v, cache_fox_logf, page_table, state_hgrn,
                 cache_mem_k, cache_mem_v, norm_g, w_in, b_fgate, hg_norm_g, lb_param, mem_norm_g, w_mk, w_mv, w_pa,
                 w_pb, w_pm, w_o, final_norm_g, y_prompt, y_sample, fox_k_prompt, fox_v_prompt, fox_logf_prompt,
                 state_prompt, mem_k_prompt, mem_v_prompt, fox_k_sample, fox_v_sample, fox_logf_sample, state_sample):
    def dram(name, shape):
        return nc.dram_tensor(name, shape, F32, kind="Internal").ap()

    rows = NT * P + P
    turned, plain = dram("turned", (len(TURNED), W, T)), dram("plain", (len(PN) - 1 + NGATE, rows, W))
    sample, neg_c = dram("sample", (NGROUP, 2 * B, W)), dram("neg_c", (FH, T))
    s_raw, s_sigmoid, s_silu = (dram(n, (NGROUP * B, W)) for n in ("s_raw", "s_sigmoid", "s_silu"))
    gated, mixed = dram("gated", (rows, 3 * W)), dram("mixed", (rows, D))
    gates = plain[PN["gate"]:PN["gate"] + NGATE]

    fox_k, fox_v = (t[0, 0].rearrange("t h d -> t (h d)") for t in (fox_k_prompt, fox_v_prompt))
    mem_k, mem_v = (t[0, 0].rearrange("t h d -> t (h d)") for t in (mem_k_prompt, mem_v_prompt))
    fox_k_s, fox_v_s = (t[0].rearrange("b o h d -> (b o) (h d)") for t in (fox_k_sample, fox_v_sample))
    logf_s = fox_logf_sample[0].rearrange("b o h -> (b o) h")
    k_pages, v_pages = (t[0].rearrange("n t h d -> n t (h d)") for t in (cache_fox_k, cache_fox_v))
    mem_k_pages, mem_v_pages = (t[0].rearrange("b (g t) h d -> (b g) t (h d)", t=PAGE)
                                for t in (cache_mem_k, cache_mem_v))
    x, x_s = x_prompt[0], x_sample.rearrange("b o d -> (b o) d")
    hg_gain = hg_norm_g[0]

    def of(group, spilled):
        at = (TURNED + PLAIN).index(group) * B
        return spilled[at:at + B, :]

    with ExitStack() as ctx:
        core = Core(nc, ctx)
        constants(nc, core)
        with nc.cleanup_on_exit():
            with ExitStack() as inner:
                mem_hi, mem_lo = (inner.enter_context(nc.sbuf_tensor(n, [P, KT, NM], F32R)) for n in ("mem_hi", "mem_lo"))
                normalise_rows(nc, core, "tokens", mem_prompt[0], mem_norm_g[0], mem_hi, mem_lo, NM // P, P, 2)
                project_memory(nc, core, mem_hi, mem_lo, [w_mk[0], w_mv[0]], [mem_k, mem_v])
            with ExitStack() as inner:
                x_hi, x_lo = (inner.enter_context(nc.sbuf_tensor(n, [P, KT, T], F32R)) for n in ("x_hi", "x_lo"))
                xs = inner.enter_context(nc.sbuf_tensor("xs_both", [P, KT, SAMPLE_COLUMNS], F32R))
                xs_hi, xs_lo = xs[:, :, 0:B], xs[:, :, B:2 * B]
                normalise_rows(nc, core, "x", x, norm_g[0], x_hi, x_lo, NT, P, 2)
                clear(nc, core, xs)
                normalise_rows(nc, core, "xs", x_s, norm_g[0], xs_hi, xs_lo, 1, B, 1)
                forget_gates(nc, core, x_hi, x_lo, xs_hi, xs_lo, w_in[0][:, COL["ff"]:COL["ff"] + FH], b_fgate[0],
                             fox_logf_prompt[0, 0], logf_s, neg_c)
                project_inputs(nc, core, x_hi, x_lo, xs, w_in[0], turned, plain, fox_k, fox_v, sample)
        with nc.cleanup_on_exit():
            unpack_sample(nc, core, sample, s_raw, s_sigmoid, s_silu, fox_k_s, fox_v_s, gates, gated)
            attend_cache(nc, core, "paged", FH, T // PAGE, k_pages, v_pages, of("fq", s_raw), of("fz", s_silu),
                         gated[T:T + B, 0:W], page_table, cache_fox_logf[0], of("fk", s_raw), of("fv", s_raw), logf_s)
            attend_cache(nc, core, "mem_cache", HH, NM // PAGE, mem_k_pages, mem_v_pages, of("mq", s_raw),
                         of("mz", s_silu), gated[T:T + B, 2 * W:3 * W])
            attend_prompt(nc, core, turned[PT["fq"]], fox_k, fox_v, plain[PN["fz"]][0:T, :], neg_c, gated[0:T, 0:W])
        lower_bound(nc, core, lb_param)
        recur_sample(nc, core, of("hf", s_sigmoid), of("hq", s_silu), of("hi", s_raw), of("hz", s_silu),
                     state_hgrn[0], hg_gain, gated[T:T + B, W:2 * W], state_sample[0])
        recur_prompt(nc, core, turned[PT["hq"]], turned[PT["hf"]], plain[PN["hi"]][0:T, :], plain[PN["hz"]][0:T, :],
                     hg_gain, gated[0:T, W:2 * W], state_prompt[0, 0])
        attend_memory(nc, core, turned[PT["mq"]], mem_k, mem_v, plain[PN["mz"]][0:T, :], gated[0:T, 2 * W:3 * W])
        merge_branches(nc, core, gated, gates, [w_pa[0], w_pb[0], w_pm[0]], mixed)
        finish_rows(nc, core, mixed, w_o[0], x, x_s, final_norm_g, y_prompt[0],
                    y_sample.rearrange("b o d -> (b o) d"))


_INS = ["x_prompt", "x_sample", "mem_prompt", "cache_fox_k", "cache_fox_v", "cache_fox_logf", "page_table",
        "state_hgrn", "cache_mem_k", "cache_mem_v", "norm_g", "w_in", "b_fgate", "hg_norm_g", "lb_param", "mem_norm_g",
        "w_mk", "w_mv", "w_pa", "w_pb", "w_pm", "w_o", "final_norm_g"]
_OUTS = [(1, 2048, 1024), (8, 1, 1024), (1, 1, 2048, 8, 64), (1, 1, 2048, 8, 64), (1, 1, 2048, 8),
         (1, 1, 4, 128, 128), (1, 1, 256, 4, 128), (1, 1, 256, 4, 128), (1, 8, 1, 8, 64), (1, 8, 1, 8, 64),
         (1, 8, 1, 8), (1, 8, 4, 128, 128)]


def kernel(**inputs):
    import numpy as _np
    import concourse.bacc as _bacc
    from concourse import mybir as _mybir
    from concourse.bass_utils import run_bass_kernel_spmd as _run

    nc = _bacc.Bacc("TRN2", target_bir_lowering=False, num_devices=1)
    arrays, args = {}, []
    for name in _INS:
        a = _np.ascontiguousarray(inputs[name])
        arrays[f"in_{name}_dram"] = a
        args.append(nc.dram_tensor(f"in_{name}_dram", a.shape, _mybir.dt.from_np(a.dtype), kind="ExternalInput").ap())
    for i, shape in enumerate(_OUTS):
        args.append(nc.dram_tensor(f"out_{i}_dram", shape, _mybir.dt.float32, kind="ExternalOutput").ap())
    decoder_step(nc, *args)
    r = _run(nc, [arrays], core_ids=[0])
    return tuple(r.results[0][f"out_{i}_dram"] for i in range(len(_OUTS)))
```

```python
from contextlib import ExitStack

import numpy as np

import concourse.bass as bass
from concourse import mybir

F32 = mybir.dt.float32
F32R = mybir.dt.float32r
I32 = mybir.dt.int32
ALU = mybir.AluOpType
ACT = mybir.ActivationFunctionType
AX = mybir.AxisListType

P = 128
D = 1024
KT = D // P
T = 2048
NT = T // P
B = 8
NM = 256
W = 512
FH, FD = 8, 64
HH, HD = 4, 128
EPS = 1e-6
PAGE = 128
BANK = 512
NEG = -1e30

COL = {}
at = 0
for name, width in (("fq", W), ("fk", W), ("fv", W), ("ff", FH), ("fz", W), ("hq", W), ("hf", W), ("hi", W),
                    ("hz", W), ("mq", W), ("mz", W), ("ga", D), ("gb", D), ("gm", D)):
    COL[name] = at
    at += width
N_IN = at

TURNED = ["fq", "mq", "hf", "hq"]
PLAIN = ["fk", "fv", "hi", "fz", "hz", "mz"]
KIND = {"fq": "scale", "mq": "copy", "hf": "sigmoid", "hq": "silu", "fk": "copy", "fv": "copy", "hi": "copy",
        "fz": "silu", "hz": "silu", "mz": "silu"}
NGATE = 3 * D // W
FIRST_GATE = len(TURNED) + len(PLAIN)
NGROUP = FIRST_GATE + NGATE
PT = {"fq": 0, "mq": 1, "hf": 2, "hq": 3}
PN = {"hi": 0, "fz": 1, "hz": 2, "mz": 3, "gate": 4}
SAMPLE_COLUMNS = 66
UNITS = 16


class Core:

    def __init__(self, nc, ctx):
        self.nc, self.ctx = nc, ctx
        self.ident = ctx.enter_context(nc.sbuf_tensor("ident", [P, P], F32))

    def sem(self, name):
        return self.nc.alloc_semaphore(name=name)


def linker(eng, sem, base=0):
    done = [0]

    def link(ins):
        done[0] += 1
        ins.then_inc(sem, 1)
        eng.wait_ge(sem, base + done[0])
    link.done = done
    return link


def rows_of(dram, start, count):
    return dram[bass.ds(start, count), :]


def constants(nc, core):
    cleared = core.sem("cleared")
    with nc.Block() as block:
        @block.gpsimd
        def _(pool):
            pool.memset(core.ident[:], 0.0).then_inc(cleared, 1)
            pool.wait_ge(cleared, 1)
            pool.affine_select(out=core.ident[:], in_=core.ident[:], compare_op=ALU.not_equal, fill=1.0, base=0,
                               pattern=[[-1, P]], channel_multiplier=1)


def clear(nc, core, tile):
    with nc.Block() as block:
        @block.gpsimd
        def _(pool):
            pool.memset(tile[:].bitcast(F32), 0.0)


def normalise_rows(nc, core, tag, src, gain, hi, lo, tiles, rows, slots):
    with ExitStack() as ctx:
        def sb(name, shape, dt=F32):
            return ctx.enter_context(nc.sbuf_tensor(f"{tag}_{name}", shape, dt))

        x = [sb(f"x{r}", [rows, D]) for r in range(slots)]
        square = sb("square", [rows, D])
        normed = [sb(f"normed{r}", [rows, D]) for r in range(slots)]
        gains = sb("gains", [rows, D])
        stat = sb("stat", [rows, 3])
        turned = [ctx.enter_context(nc.psum_tensor(f"{tag}_turned{r}", [P, KT, P], F32)) for r in range(slots)]
        x_loaded = [core.sem(f"{tag}_x_loaded{r}") for r in range(slots)]
        gains_loaded = core.sem(f"{tag}_gains_loaded")
        x_used = core.sem(f"{tag}_x_used")
        stat_step = core.sem(f"{tag}_stat_step")
        normed_ready = core.sem(f"{tag}_normed_ready")
        turned_ready = core.sem(f"{tag}_turned_ready")
        turned_used = core.sem(f"{tag}_turned_used")
        hi_ready = core.sem(f"{tag}_hi_ready")
        mean_ready = core.sem(f"{tag}_mean_ready")
        root_ready = core.sem(f"{tag}_root_ready")

        with nc.Block() as block:
            @block.sync
            def _(sp):
                sp.dma_start(gains[:], gain.partition_broadcast(rows)).then_inc(gains_loaded, 16)
                with sp.Fori(0, tiles // slots) as i:
                    for r in range(slots):
                        sp.wait_ge(x_used, i * slots + r + 1)
                        sp.dma_start(x[r][:], rows_of(src, (i * slots + r) * rows, rows)).then_inc(x_loaded[r], 16)

            @block.vector
            def _(dve):
                dve.sem_inc(x_used, slots)
                dve.wait_ge(gains_loaded, 16)
                with dve.Fori(0, tiles // slots) as i:
                    for r in range(slots):
                        link = linker(dve, stat_step, (i * slots + r) * 2)
                        dve.wait_ge(x_loaded[r], (i + 1) * 16)
                        link(dve.tensor_tensor_reduce(square[:], x[r][:], x[r][:], 1.0, 0.0, ALU.mult, ALU.add,
                                                      stat[:, 0:1]))
                        dve.tensor_scalar(stat[:, 1:2], stat[:, 0:1], 1.0 / D, EPS, ALU.mult,
                                          ALU.add).then_inc(mean_ready, 1)
                        dve.wait_ge(root_ready, i * slots + r + 1)
                        link(dve.reciprocal(stat[:, 2:3], stat[:, 1:2]))
                        dve.scalar_tensor_tensor(out=normed[r][:], in0=x[r][:], scalar=stat[:, 2:3], in1=gains[:],
                                                 op0=ALU.mult, op1=ALU.mult).then_inc(normed_ready, 1)
                        dve.wait_ge(normed_ready, i * slots + r + 1)
                        dve.sem_inc(x_used, 1)
                    for r in range(slots):
                        dve.wait_ge(turned_ready, i * slots + r + 1)
                        dve.wait_ge(hi_ready, i * slots + r + 1)
                        at = bass.ds((i * slots + r) * rows, rows)
                        dve.tensor_tensor(lo[:, :, at], turned[r][:, :, 0:rows], hi[:, :, at].bitcast(F32),
                                          ALU.subtract).then_inc(turned_used, 1)

            @block.tensor
            def _(pe):
                pe.sem_inc(turned_used, slots)
                with pe.Fori(0, tiles // slots) as i:
                    for r in range(slots):
                        pe.wait_ge(turned_used, i * slots + r + 1)
                        pe.wait_ge(normed_ready, i * slots + r + 1)
                        for k in range(KT):
                            last = pe.transpose(turned[r][:, k, 0:rows], normed[r][:, k * P:(k + 1) * P],
                                                core.ident[0:rows, 0:rows])
                        last.then_inc(turned_ready, 1)

            @block.scalar
            def _(act):
                with act.Fori(0, tiles // slots) as i:
                    for r in range(slots):
                        act.wait_ge(mean_ready, i * slots + r + 1)
                        act.activation(stat[:, 1:2], stat[:, 1:2], ACT.Sqrt).then_inc(root_ready, 1)
                    for r in range(slots):
                        act.wait_ge(turned_ready, i * slots + r + 1)
                        act.activation(hi[:, :, bass.ds((i * slots + r) * rows, rows)], turned[r][:, :, 0:rows],
                                       ACT.Copy).then_inc(hi_ready, 1)


def product(pe, out, a, b, first, last):
    pe.matmul(out, a[0], b[0], start=first, stop=False)
    pe.matmul(out, a[1], b[0], start=False, stop=False)
    return pe.matmul(out, a[0], b[1], start=False, stop=last)


def project_memory(nc, core, mem_hi, mem_lo, weights, outputs):
    tiles = NM // P
    with ExitStack() as ctx:
        def sb(name, shape, dt=F32):
            return ctx.enter_context(nc.sbuf_tensor(f"mkv_{name}", shape, dt))

        raw = [sb(f"raw{g}", [P, KT, W]) for g in range(2)]
        whi = [sb(f"whi{g}", [P, KT, W], F32R) for g in range(2)]
        wlo = [sb(f"wlo{g}", [P, KT, W], F32R) for g in range(2)]
        stage = sb("stage", [P, 2, tiles, W])
        out = ctx.enter_context(nc.psum_tensor("mkv_out", [P, 2, tiles, W], F32))
        raw_loaded = [core.sem(f"mkv_raw_loaded{g}") for g in range(2)]
        hi_ready = core.sem("mkv_hi_ready")
        lo_ready = core.sem("mkv_lo_ready")
        out_ready = core.sem("mkv_out_ready")
        staged = core.sem("mkv_staged")
        stored = core.sem("mkv_stored")

        with nc.Block() as block:
            @block.sync
            def _(sp):
                for g in range(2):
                    sp.dma_start(raw[g][:], weights[g].rearrange("(k p) n -> p k n", p=P)).then_inc(raw_loaded[g], 16)
                for g in range(2):
                    for t in range(tiles):
                        sp.wait_ge(staged, g * tiles + t + 1)
                        sp.dma_start(outputs[g][t * P:(t + 1) * P, :], stage[:, g, t, :]).then_inc(stored, 16)
                sp.wait_ge(stored, 16 * 2 * tiles)

            @block.scalar
            def _(act):
                for g in range(2):
                    act.wait_ge(raw_loaded[g], 16)
                    act.activation(whi[g][:], raw[g][:], ACT.Copy).then_inc(hi_ready, 1)
                for n in range(2 * tiles):
                    act.wait_ge(out_ready, n + 1)
                    act.activation(stage[:, n // tiles, n % tiles, :], out[:, n // tiles, n % tiles, :],
                                   ACT.Copy).then_inc(staged, 1)

            @block.vector
            def _(dve):
                for g in range(2):
                    dve.wait_ge(hi_ready, g + 1)
                    dve.tensor_tensor(wlo[g][:], raw[g][:], whi[g][:].bitcast(F32), ALU.subtract).then_inc(lo_ready, 1)

            @block.tensor
            def _(pe):
                for g in range(2):
                    pe.wait_ge(lo_ready, g + 1)
                    for t in range(tiles):
                        for k in range(KT):
                            m = product(pe, out[:, g, t, :],
                                        (mem_hi[:, k, t * P:(t + 1) * P], mem_lo[:, k, t * P:(t + 1) * P]),
                                        (whi[g][:, k, :], wlo[g][:, k, :]), k == 0, k == KT - 1)
                        m.then_inc(out_ready, 1)


def forget_gates(nc, core, x_hi, x_lo, xs_hi, xs_lo, w_ff, bias, logf_p, logf_s, neg_c):
    N = NT * FH + FH
    with ExitStack() as ctx:
        def sb(name, shape, dt=F32):
            return ctx.enter_context(nc.sbuf_tensor(f"ff_{name}", shape, dt))

        raw = sb("raw", [P, KT, FH])
        whi, wlo = (sb(n, [P, KT, SAMPLE_COLUMNS], F32R) for n in ("whi", "wlo"))
        biases = sb("biases", [P, FH])
        z, e, u, r, low = (sb(n, [P, NT + 1, FH]) for n in ("z", "e", "u", "r", "low"))
        logf = sb("logf", [P, NT + 1, FH])
        turned = sb("turned", [FH, T])
        summed = sb("summed", [FH, T])
        one_row = sb("one_row", [FH, T])
        out = ctx.enter_context(nc.psum_tensor("ff_out", [P, NT + 1, FH], F32))
        wide = ctx.enter_context(nc.psum_tensor("ff_wide", [SAMPLE_COLUMNS, T], F32))
        flipped = wide[0:FH, :]
        padded, wide_ready, wide_copied = (core.sem(f"ff_{n}") for n in ("padded", "wide_ready", "wide_copied"))
        loaded, split, out_ready, step = (core.sem(f"ff_{n}") for n in ("loaded", "split", "out_ready", "step"))
        exp_ready, exp_asked, ln_asked, ln_ready = (core.sem(f"ff_{n}") for n in
                                                    ("exp_ready", "exp_asked", "ln_asked", "ln_ready"))
        logf_ready, flipped_ready, sum_ready, stored = (core.sem(f"ff_{n}") for n in
                                                        ("logf_ready", "flipped_ready", "sum_ready", "stored"))

        with nc.Block() as block:
            @block.sync
            def _(sp):
                with nc.allow_non_contiguous_dma(reason="eight columns of the weights, eight gates of a row"):
                    sp.dma_start(raw[:], w_ff.rearrange("(k p) n -> p k n", p=P)).then_inc(loaded, 16)
                    sp.dma_start(biases[:], bias.partition_broadcast(P)).then_inc(loaded, 16)
                    sp.wait_ge(logf_ready, 1)
                    sp.dma_start(logf_p.rearrange("(t p) h -> p t h", p=P), logf[:, 0:NT, :]).then_inc(stored, 16)
                    sp.dma_start(logf_s, logf[0:B, NT, :]).then_inc(stored, 16)
                sp.wait_ge(sum_ready, 1)
                sp.dma_start(neg_c, summed[:]).then_inc(stored, 16)
                sp.wait_ge(stored, 48)

            @block.vector
            def _(dve):
                link = linker(dve, step)
                dve.wait_ge(loaded, 32)
                dve.wait_ge(padded, 1)
                link(dve.tensor_copy(whi[:, :, 0:FH], raw[:]))
                dve.tensor_tensor(wlo[:, :, 0:FH], raw[:], whi[:, :, 0:FH].bitcast(F32), ALU.subtract
                                  ).then_inc(split, 1)
                link(dve.memset(z[:], 0.0))
                link(dve.memset(one_row[:], 1.0))
                for c in range(T // BANK):
                    dve.wait_ge(wide_ready, c + 1)
                    dve.tensor_copy(turned[:, c * BANK:(c + 1) * BANK], wide[0:FH, c * BANK:(c + 1) * BANK]
                                    ).then_inc(wide_copied, 1)
                dve.wait_ge(out_ready, 1)
                link(dve.tensor_tensor(z[:, 0:NT, :], out[:, 0:NT, :],
                                       biases[:].unsqueeze(1).to_broadcast([P, NT, FH]), ALU.add))
                link(dve.tensor_tensor(z[0:B, NT, :], out[0:B, NT, :], biases[0:B, :], ALU.add))
                dve.scalar_tensor_tensor(out=u[:], in0=z[:], scalar=-1.0, in1=z[:], op0=ALU.mult,
                                         op1=ALU.max).then_inc(exp_asked, 1)
                link(dve.tensor_scalar(low[:], z[:], 0.0, None, ALU.min))
                dve.wait_ge(exp_ready, 1)
                dve.tensor_scalar(u[:], e[:], 1.0, None, ALU.add).then_inc(ln_asked, 1)
                dve.wait_ge(ln_asked, 1)
                link(dve.scalar_tensor_tensor(out=r[:], in0=u[:], scalar=-1.0, in1=e[:], op0=ALU.add,
                                              op1=ALU.subtract))
                dve.wait_ge(ln_ready, 1)
                link(dve.reciprocal(u[:], u[:]))
                link(dve.tensor_tensor(r[:], r[:], u[:], ALU.mult))
                link(dve.tensor_tensor(z[:], z[:], r[:], ALU.subtract))
                dve.tensor_tensor(logf[:], low[:], z[:], ALU.subtract).then_inc(logf_ready, 1)
                dve.wait_ge(flipped_ready, 1)
                link(dve.tensor_scalar(turned[:], flipped, -1.0, None, ALU.mult))
                dve.tensor_tensor_scan(summed[:], one_row[:], turned[:], 0.0, ALU.mult, ALU.add).then_inc(sum_ready, 1)

            @block.gpsimd
            def _(pool):
                pool.memset(whi[:].bitcast(F32), 0.0)
                pool.memset(wlo[:].bitcast(F32), 0.0).then_inc(padded, 1)

            @block.scalar
            def _(act):
                act.wait_ge(exp_asked, 1)
                act.activation(e[:], u[:], ACT.Exp, scale=-1.0).then_inc(exp_ready, 1)
                act.wait_ge(ln_asked, 1)
                act.activation(z[:], u[:], ACT.Ln).then_inc(ln_ready, 1)

            @block.tensor
            def _(pe):
                pe.wait_ge(split, 1)
                for c in range(T // BANK):
                    rows = slice(c * BANK, (c + 1) * BANK)
                    for k in range(KT):
                        m = product(pe, wide[:, rows], (whi[:, k, :], wlo[:, k, :]), (x_hi[:, k, rows], x_lo[:, k, rows]),
                                    k == 0, k == KT - 1)
                    m.then_inc(wide_ready, 1)
                for k in range(KT):
                    pe.matmul(out[0:B, NT, :], xs_hi[:, k, :].bitcast(F32), raw[:, k, :], start=(k == 0), stop=False)
                    pe.matmul(out[0:B, NT, :], xs_lo[:, k, :].bitcast(F32), raw[:, k, :], start=False,
                              stop=(k == KT - 1))
                for t in range(NT):
                    pe.wait_ge(wide_copied, t * P // BANK + 1)
                    m = pe.transpose(out[:, t, :], turned[:, t * P:(t + 1) * P], core.ident[0:FH, 0:FH])
                m.then_inc(out_ready, 1)
                pe.wait_ge(logf_ready, 1)
                for t in range(NT):
                    m = pe.transpose(flipped[:, t * P:(t + 1) * P], logf[:, t, :], core.ident[:])
                m.then_inc(flipped_ready, 1)


def project_inputs(nc, core, x_hi, x_lo, xs_both, w_in, turned, plain, fox_k, fox_v, sample):
    STAGES = 4
    ROUNDS = UNITS // STAGES
    USES = ROUNDS + 1
    with ExitStack() as ctx:
        def sb(name, shape, dt=F32):
            return ctx.enter_context(nc.sbuf_tensor(f"in_{name}", shape, dt))

        raw = [sb(f"raw{r}", [P, W]) for r in range(2)]
        whi = [sb(f"whi{r}", [P, KT, W], F32R) for r in range(2)]
        wlo = [sb(f"wlo{r}", [P, KT, W], F32R) for r in range(2)]
        stage = [sb(f"stage{s}", [P, W]) for s in range(STAGES)]
        out = [ctx.enter_context(nc.psum_tensor(f"in_out{s}", [P, BANK], F32)) for s in range(STAGES)]
        out_s = ctx.enter_context(nc.psum_tensor("in_out_s", [P, BANK], F32))
        primer = nc.dram_tensor("in_primer", (STAGES, P), F32, kind="Internal").ap()

        raw_loaded = [core.sem(f"in_raw_loaded{r}") for r in range(2)]
        split = core.sem("in_split")
        multiplied = core.sem("in_multiplied")
        out_ready = core.sem("in_out_ready")
        sigmoid_ready = core.sem("in_sigmoid_ready")
        taken = core.sem("in_taken")
        stored = [core.sem(f"in_stored{s}") for s in range(STAGES)]
        taken_s = core.sem("in_taken_s")
        paced = core.sem("in_paced")

        names = TURNED + PLAIN
        silus_before = [sum(KIND[n] == "silu" for n in names[:g]) for g in range(len(names))]

        with nc.Block() as block:
            @block.sync
            def _(sp):
                def load(g, column, k, slot):
                    sp.wait_ge(split, 2 * (g * KT + k) + 2)
                    sp.dma_start(raw[slot][:], w_in[bass.ds(k * P, P), bass.ds(column, W)]).then_inc(raw_loaded[slot], 16)

                def store_group(g, place, following):
                    with sp.Fori(0, ROUNDS) as q:
                        if following is not None:
                            for r in range(2):
                                load(g + 1, following, q * 2 + r, r)
                        for s in range(STAGES):
                            sp.wait_ge(taken, STAGES + g * UNITS + q * STAGES + s + 1)
                            sp.dma_start(place(q, s), stage[s][:]).then_inc(stored[s], 16)
                    sp.wait_ge(taken_s, g + 2)
                    sp.dma_start(sample[bass.ds(g, 1)].rearrange("o p n -> (o p) n"), stage[0][0:2 * B, :]).then_inc(stored[0], 16)

                for s in range(STAGES):
                    sp.dma_start(primer[s:s + 1, :], core.ident[0:1, :]).then_inc(stored[s], 16)
                with sp.Fori(0, KT // 2) as q:
                    for r in range(2):
                        load(0, COL[names[0]], q * 2 + r, r)
                for g, name in enumerate(names):
                    following = COL[names[g + 1]] if g + 1 < FIRST_GATE else COL["ga"]
                    if name in PT:
                        dst = turned[PT[name]]
                        store_group(g, lambda q, s, dst=dst: dst[bass.ds(q * P, P), s * W:(s + 1) * W], following)
                    else:
                        dst = fox_k if name == "fk" else fox_v if name == "fv" else plain[PN[name]]
                        store_group(g, lambda q, s, dst=dst: dst[bass.ds((q * STAGES + s) * P, P), :], following)

                def gate_place(j):
                    return lambda q, s: plain[bass.ds(j + PN["gate"], 1), bass.ds((q * STAGES + s) * P, P), :] \
                        .rearrange("o t n -> (o t) n")

                with sp.Fori(0, NGATE - 1) as j:
                    store_group(j + FIRST_GATE, gate_place(j), j * W + COL["ga"] + W)
                store_group(NGROUP - 1, gate_place(NGATE - 1), None)
                for s in range(STAGES):
                    sp.wait_ge(stored[s], 16 * (1 + NGROUP * (USES if s == 0 else ROUNDS)))

            @block.gpsimd
            def _(pool):
                pool.sem_inc(split, 4)
                with pool.Fori(0, NGROUP // 2) as pair:
                    for r in range(2):
                        pool.wait_ge(multiplied, pair * 2 + r + 1)
                        for k in range(KT):
                            n = (pair * 2 + r) * KT + k
                            pool.wait_ge(raw_loaded[k % 2], ((pair * 2 + r) * (KT // 2) + k // 2 + 1) * 16)
                            pool.sem_inc(paced, 1)
                            pool.tensor_copy(whi[r][:, k, :], raw[k % 2][:]).then_inc(split, 1)
                            pool.wait_ge(split, n * 2 + 5)
                            pool.tensor_tensor(wlo[r][:, k, :], raw[k % 2][:], whi[r][:, k, :].bitcast(F32),
                                               ALU.subtract).then_inc(split, 1)

            @block.tensor
            def _(pe):
                pe.sem_inc(multiplied, 2)
                pe.sem_inc(taken, STAGES)
                pe.sem_inc(taken_s, 1)

                def group(g, r, is_turned):
                    for u in range(UNITS):
                        pe.wait_ge(taken, g * UNITS + u + 1)
                        c, b = u // STAGES, u % STAGES
                        for k in range(KT):
                            if u == 0:
                                pe.wait_ge(split, (g * KT + k) * 2 + 6)
                            w = (whi[r], wlo[r])
                            x = (x_hi, x_lo)
                            if is_turned:
                                m = product(pe, out[u % STAGES][:], [a[:, k, c * P:(c + 1) * P] for a in w],
                                            [a[:, k, b * W:(b + 1) * W] for a in x], k == 0, k == KT - 1)
                            else:
                                m = product(pe, out[u % STAGES][:], [a[:, k, u * P:(u + 1) * P] for a in x],
                                            [a[:, k, :] for a in w], k == 0, k == KT - 1)
                        m.then_inc(out_ready, 1)
                    pe.wait_ge(taken_s, g + 1)
                    for k in range(KT):
                        pe.matmul(out_s[0:SAMPLE_COLUMNS, :], xs_both[:, k, :], whi[r][:, k, :], start=(k == 0),
                                  stop=False)
                        m = pe.matmul(out_s[0:SAMPLE_COLUMNS, :], xs_both[:, k, :], wlo[r][:, k, :], start=False,
                                      stop=(k == KT - 1))
                    m.then_inc(multiplied, 1)

                with pe.Fori(0, len(TURNED) // 2) as pair:
                    for r in range(2):
                        group(pair * 2 + r, r, True)
                with pe.Fori(len(TURNED) // 2, NGROUP // 2) as pair:
                    for r in range(2):
                        group(pair * 2 + r, r, False)

            @block.scalar
            def _(act):
                def group(g, kind):
                    how = {"copy": (ACT.Copy, 1.0), "scale": (ACT.Copy, FD ** -0.5)}.get(kind, (ACT.Sigmoid, 1.0))
                    signal = sigmoid_ready if kind == "silu" else taken
                    act.wait_ge(taken, STAGES + g * UNITS)
                    with act.Fori(0, ROUNDS) as q:
                        for s in range(STAGES):
                            act.wait_ge(out_ready, g * UNITS + q * STAGES + s + 1)
                            act.wait_ge(stored[s], (g * (USES if s == 0 else ROUNDS) + q + 1) * 16)
                            act.activation(stage[s][:], out[s][:], how[0], scale=how[1]).then_inc(signal, 1)
                    act.wait_ge(multiplied, g + 3)
                    act.wait_ge(taken, STAGES + (g + 1) * UNITS)
                    act.wait_ge(stored[0], (g * USES + ROUNDS + 1) * 16)
                    act.activation(stage[0][0:2 * B, :], out_s[0:2 * B, :], ACT.Copy).then_inc(taken_s, 1)

                for g, name in enumerate(names):
                    group(g, KIND[name])
                with act.Fori(FIRST_GATE, NGROUP) as g:
                    group(g, "sigmoid")

            @block.vector
            def _(dve):
                for g, name in enumerate(names):
                    if KIND[name] == "silu":
                        n = silus_before[g]
                        with dve.Fori(0, ROUNDS) as q:
                            for s in range(STAGES):
                                dve.wait_ge(sigmoid_ready, q * STAGES + s + 1 + n * UNITS)
                                dve.tensor_tensor(stage[s][:], stage[s][:], out[s][:], ALU.mult).then_inc(taken, 1)


def attend_prompt(nc, core, queries, fox_k, fox_v, z_fox, neg_c, gated):
    QUADS = NT // 4
    HEADS = 2
    S_BANKS = 3
    CHUNKS = [i // 4 + 1 for i in range(NT)]
    S_HEAD = sum(CHUNKS)
    J_HEAD = sum(4 * (q + 1) for q in range(QUADS))
    J_AT = [sum(4 * (p + 1) for p in range(q)) for q in range(QUADS)]
    S_AT = [sum(CHUNKS[:i]) for i in range(NT)]
    TURN_BANKS = 3
    PT_SLOTS = 4
    SPREAD = 0.8
    DEPTH = 2
    quads = [(h, q) for h in range(HEADS) for q in range(QUADS)]

    def chunks_of(h, q):
        return [("score", h, i, c) for i in range(4 * q, 4 * q + 4) for c in range(CHUNKS[i])]

    steps = [("set", 0)] + [("keys", 0, b) for b in range(QUADS)]
    for i in range(4):
        steps += [("score", 0, i, 0), ("exp", 0, i)]
    for n, (h, q) in enumerate(quads):
        ahead = [("score", quads[n + 1][0], i, c) for i in range(4 * quads[n + 1][1], 4 * quads[n + 1][1] + 4)
                 for c in range(CHUNKS[i])] if n + 1 < len(quads) else []
        keys = 4 * (q + 1)
        spread = max(1, round(keys * SPREAD))
        late = []
        for j in range(keys):
            some = ahead[len(ahead) * min(j, spread) // spread:len(ahead) * min(j + 1, spread) // spread]
            steps += some
            if h == 0 and q == 1 and j == keys - 2:
                steps += [("set", 1)]
            if h == 0 and q == 2 and j % 3 == 0:
                steps += [("keys", 1, j // 3)]
            steps += [("key", h, q, j)]
            steps += late
            late = [("exp", st[1], st[2]) for st in some if st[3] == CHUNKS[st[2]] - 1]
            if j == DEPTH - 1 and n > 0:
                steps += [("out", *quads[n - 1])]
            if j == DEPTH + 1 and n > 0:
                steps += [("back", *quads[n - 1])]
        steps += late
    steps += [("out", *quads[-1]), ("back", *quads[-1])]
    turn_at = {st: n for n, st in enumerate(s for s in steps if s[0] in ("keys", "key", "back"))}
    TURNS = len(turn_at)
    assert TURNS % TURN_BANKS == 0 and J_HEAD % PT_SLOTS == 0

    with ExitStack() as ctx:
        def sb(name, shape, dt=F32):
            return ctx.enter_context(nc.sbuf_tensor(f"fox_{name}", shape, dt))

        def pair(name, shape, dt=F32):
            return [sb(f"{name}{h}", shape, dt) for h in range(HEADS)]

        q_both = pair("q_both", [P, T], F32R)
        k_hi, k_lo = pair("k_hi", [P, T], F32R), pair("k_lo", [P, T], F32R)
        v_both = pair("v_both", [P, NT, 2 * FD], F32R)
        q_raw = sb("q_raw", [P, T])
        k_raw = sb("k_raw", [P, NT, 2 * FD])
        v_raw = sb("v_raw", [P, NT, FD])
        z = pair("z", [P, NT, FD])
        bias = pair("bias", [P, T])
        mask = sb("mask", [P, P])
        mask_r, ident_r = sb("mask_r", [P, P], F32R), sb("ident_r", [P, P], F32R)
        halves = sb("halves", [P, P])
        probs = sb("probs", [P, 8, T])
        most = sb("most", [P, 8, CHUNKS[-1]])
        neg_most = sb("neg_most", [P, 8])
        row_sum = sb("row_sum", [P, HEADS * NT])
        inverse = sb("inverse", [P, 4])
        pt_hi, pt_lo = sb("pt_hi", [P, PT_SLOTS, BANK], F32R), sb("pt_lo", [P, PT_SLOTS, BANK], F32R)
        o_turned = sb("o_turned", [P, BANK])
        o_rows = pair("o_rows", [P, NT, FD])

        def psum(name, n):
            return [ctx.enter_context(nc.psum_tensor(f"fox_{name}{i}", [P, BANK], F32)) for i in range(n)]

        scores, turned, o_sum = psum("scores", S_BANKS), psum("turned", TURN_BANKS), psum("o_sum", 2)

        def bank_of(st):
            return turned[turn_at[st] % TURN_BANKS]

        def sem(name):
            return core.sem(f"fox_{name}")

        raw_loaded, z_loaded, bias_loaded = sem("raw_loaded"), [sem(f"z_loaded{h}") for h in range(HEADS)], \
            [sem(f"bias_loaded{h}") for h in range(HEADS)]
        raw_free = sem("raw_free")
        consts_ready = sem("consts_ready")
        q_hi_ready, q_ready, v_ready = sem("q_hi_ready"), sem("q_ready"), sem("v_ready")
        turned_ready, turned_used = sem("turned_ready"), sem("turned_used")
        keys_hi = sem("keys_hi")
        scored, scores_used = sem("scored"), sem("scores_used")
        most_ready, exp_ready = sem("most_ready"), sem("exp_ready")
        hi_ready = sem("hi_ready")
        multiplied = sem("multiplied")
        o_copied = sem("o_copied")
        rows_ready, rows_stored = sem("rows_ready"), sem("rows_stored")
        started, inverse_ready = sem("started"), sem("inverse_ready")
        paced = sem("paced")

        with nc.Block() as block:
            @block.gpsimd
            def _(pool):
                link = linker(pool, started)
                link(pool.memset(mask[:], 0.0))
                link(pool.memset(halves[:], 0.0))
                pool.affine_select(out=mask[:], in_=mask[:], compare_op=ALU.is_ge, fill=NEG, base=0,
                                   pattern=[[-1, P]], channel_multiplier=1)
                for n, base in enumerate((0, -FD, FD)):
                    link(pool.affine_select(out=halves[:], in_=halves[:], compare_op=ALU.not_equal, fill=1.0,
                                            base=base, pattern=[[-1, P]], channel_multiplier=1))
                link(pool.tensor_copy(mask_r[:], mask[:]))
                link(pool.tensor_copy(ident_r[:], core.ident[:]))
                pool.sem_inc(consts_ready, 1)

            @block.sync
            def _(sp):
                def rows(dram, head):
                    return dram.rearrange("(t p) c -> p t c", p=P)[:, :, bass.ds(head * FD, FD)]

                def load(head, h):
                    sp.wait_ge(raw_free, head + 1)
                    for half in range(2):
                        sp.dma_start(q_raw[half * FD:(half + 1) * FD, :],
                                     rows_of(queries, head * FD, FD)).then_inc(raw_loaded, 16)
                        sp.dma_start(k_raw[:, :, half * FD:(half + 1) * FD], rows(fox_k, head)).then_inc(raw_loaded, 16)
                    sp.dma_start(v_raw[:], rows(fox_v, head)).then_inc(raw_loaded, 16)
                    sp.dma_start(bias[h][:], neg_c[bass.ds(head, 1), :].to_broadcast([P, T])).then_inc(bias_loaded[h], 16)
                    sp.dma_start(z[h][:], rows(z_fox, head)).then_inc(z_loaded[h], 16)

                def store(head, h):
                    sp.wait_ge(rows_ready, (head + 3) * QUADS)
                    sp.dma_start(rows(gated, head), o_rows[h][:]).then_inc(rows_stored, 16)

                sp.sem_inc(raw_free, 1)
                with nc.allow_non_contiguous_dma(reason="a head's 64 columns of a row"):
                    for h in range(HEADS):
                        load(h, h)
                    with sp.Fori(1, FH // HEADS) as it:
                        for h in range(HEADS):
                            head = it * HEADS + h
                            store(head - HEADS, h)
                            sp.wait_ge(rows_stored, (head - 1) * 16)
                            load(head, h)
                    for h in range(HEADS):
                        store(FH - HEADS + h, h)
                    sp.wait_ge(rows_stored, FH * 16)

            @block.tensor
            def _(pe):
                pe.sem_inc(scores_used, S_BANKS)
                pe.sem_inc(turned_used, TURN_BANKS)
                pe.sem_inc(multiplied, PT_SLOTS)
                pe.sem_inc(o_copied, 2)
                pe.wait_ge(consts_ready, 1)
                with pe.Fori(0, FH // HEADS) as it:
                    pending = []

                    def values(h, q, j):
                        n, skip = h * QUADS + q, max(0, j - 4 * q) * P
                        pe.wait_ge(turned_used, it * TURNS + turn_at["key", h, q, j] + TURN_BANKS + 1)
                        if j == 0:
                            pe.wait_ge(v_ready, it * HEADS + h + 1)
                            pe.wait_ge(o_copied, it * len(quads) + n + 1)
                        for m, p in enumerate((pt_hi, pt_lo)):
                            last = pe.matmul(o_sum[n % 2][:, skip:BANK], v_both[h][:, j, :],
                                             p[:, (J_AT[q] + j) % PT_SLOTS, skip:BANK], start=(j == 0 and m == 0),
                                             stop=(j == 4 * q + 3 and m == 1))
                        last.then_inc(multiplied, 1)

                    for st in steps:
                        kind, h, *rest = st
                        head = it * HEADS + h
                        if kind == "keys":
                            b = rest[0]
                            pe.wait_ge(raw_loaded, (head + 1) * 80)
                            pe.wait_ge(turned_used, it * TURNS + turn_at[st] + 1)
                            for t in range(4):
                                last = pe.transpose(bank_of(st)[:, t * P:(t + 1) * P], k_raw[:, 4 * b + t, :], core.ident[:])
                            last.then_inc(turned_ready, 1)
                        if kind == "score":
                            i, c = rest
                            if i == 0:
                                pe.wait_ge(q_ready, head + 1)
                                pe.wait_ge(turned_used, it * TURNS + turn_at["keys", h, QUADS - 1] + TURN_BANKS + 1)
                            s = h * S_HEAD + S_AT[i] + c
                            pe.wait_ge(scores_used, it * HEADS * S_HEAD + S_BANKS + max(0, s - S_BANKS + 1))
                            width = min(BANK, (i + 1) * P - c * BANK)
                            out, keys = scores[s % S_BANKS][:, 0:width], slice(c * BANK, c * BANK + width)
                            pe.matmul(out, q_both[h][:, i * P:(i + 1) * P], k_hi[h][:, keys], start=True, stop=False)
                            last = pe.matmul(out, q_both[h][:, i * P:(i + 1) * P], k_lo[h][:, keys], start=False,
                                             stop=c < CHUNKS[i] - 1)
                            if c == CHUNKS[i] - 1:
                                last = pe.matmul(out[:, width - P:width], ident_r[:], mask_r[:], start=False, stop=True)
                            last.then_inc(scored, 1)
                        if kind == "key":
                            q, j = rest
                            if j == 0:
                                pe.wait_ge(exp_ready, head * NT + 4 * q + 4)
                            pe.wait_ge(turned_used, it * TURNS + turn_at[st] + 1)
                            for t in range(max(0, j - 4 * q), 4):
                                last = pe.transpose(bank_of(st)[:, t * P:(t + 1) * P],
                                                    probs[:, q % 2 * 4 + t, j * P:(j + 1) * P], core.ident[:])
                            last.then_inc(turned_ready, 1)
                            if len(pending) == DEPTH:
                                values(*pending.pop(0))
                            pending.append((h, q, j))
                        if kind == "out" and st is steps[-2]:
                            while pending:
                                values(*pending.pop(0))
                        if kind == "back":
                            n = h * QUADS + rest[0]
                            pe.wait_ge(o_copied, it * len(quads) + n + 3)
                            pe.wait_ge(turned_used, it * TURNS + turn_at[st] + 1)
                            for t in range(4):
                                last = pe.matmul(bank_of(st)[:, t * P:(t + 1) * P], o_turned[:, t * P:(t + 1) * P], halves[:],
                                                 start=True, stop=True)
                            last.then_inc(turned_ready, 1)

            @block.scalar
            def _(act):
                with act.Fori(0, FH // HEADS) as it:
                    for st in steps:
                        kind, h, *rest = st
                        head = it * HEADS + h
                        if kind == "set":
                            act.wait_ge(raw_loaded, (head + 1) * 80)
                            act.activation(q_both[h][:], q_raw[:], ACT.Copy).then_inc(q_hi_ready, 1)
                            act.activation(v_both[h][:, :, 0:FD], v_raw[:], ACT.Copy).then_inc(q_hi_ready, 1)
                        if kind == "keys":
                            b = rest[0]
                            act.wait_ge(turned_ready, it * TURNS + turn_at[st] + 1)
                            act.activation(k_hi[h][:, b * BANK:(b + 1) * BANK], bank_of(st)[:],
                                           ACT.Copy).then_inc(keys_hi, 1)
                        if kind == "exp":
                            i = rest[0]
                            slot = i // 4 % 2 * 4 + i % 4
                            act.wait_ge(most_ready, (head + 2) * NT + i + 1)
                            act.activation(probs[:, slot, 0:(i + 1) * P], probs[:, slot, 0:(i + 1) * P], ACT.Exp,
                                           bias=neg_most[:, slot:slot + 1],
                                           accum_out=row_sum[:, h * NT + i:h * NT + i + 1]).then_inc(exp_ready, 1)
                        if kind == "key":
                            q, j = rest
                            zeta = head * J_HEAD + J_AT[q] + j
                            skip = max(0, j - 4 * q) * P
                            act.wait_ge(turned_ready, it * TURNS + turn_at[st] + 1)
                            act.wait_ge(multiplied, zeta + 1)
                            act.activation(pt_hi[:, (J_AT[q] + j) % PT_SLOTS, skip:BANK],
                                           bank_of(st)[:, skip:BANK], ACT.Copy).then_inc(hi_ready, 1)
                        if kind == "out":
                            q = rest[0]
                            n = h * QUADS + q
                            act.wait_ge(multiplied, head * J_HEAD + J_AT[q] + 4 * (q + 1) + PT_SLOTS)
                            act.wait_ge(rows_ready, it * len(quads) + n + 2 * QUADS)
                            act.activation(o_turned[:], o_sum[n % 2][:], ACT.Copy).then_inc(o_copied, 1)

            @block.vector
            def _(dve):
                dve.sem_inc(most_ready, 2 * NT)
                dve.sem_inc(rows_ready, 2 * QUADS)
                with dve.Fori(0, FH // HEADS) as it:
                    for st in steps:
                        kind, h, *rest = st
                        head = it * HEADS + h
                        if kind == "set":
                            dve.wait_ge(q_hi_ready, head * 2 + 1)
                            dve.tensor_tensor(q_both[h][FD:P, :], q_raw[FD:P, :], q_both[h][FD:P, :].bitcast(F32),
                                              ALU.subtract).then_inc(q_ready, 1)
                            dve.wait_ge(q_hi_ready, head * 2 + 2)
                            dve.tensor_tensor(v_both[h][:, :, FD:2 * FD], v_raw[:], v_both[h][:, :, 0:FD].bitcast(F32),
                                              ALU.subtract).then_inc(v_ready, 1)
                        if kind == "keys":
                            b = rest[0]
                            dve.wait_ge(keys_hi, head * QUADS + b + 1)
                            keys = slice(b * BANK, (b + 1) * BANK)
                            dve.tensor_tensor(k_lo[h][:, keys], bank_of(st)[:], k_hi[h][:, keys].bitcast(F32),
                                              ALU.subtract).then_inc(turned_used, 1)
                            if b == QUADS - 1:
                                dve.wait_ge(v_ready, head + 1)
                                dve.sem_inc(raw_free, 1)
                        if kind == "score":
                            i, c = rest
                            slot = i // 4 % 2 * 4 + i % 4
                            if i == 0:
                                dve.wait_ge(bias_loaded[h], (it + 1) * 16)
                            s = h * S_HEAD + S_AT[i] + c
                            bank = scores[s % S_BANKS]
                            dve.wait_ge(scored, it * HEADS * S_HEAD + s + 1)
                            dve.sem_inc(paced, 1)
                            width = min(BANK, (i + 1) * P - c * BANK)
                            keys = slice(c * BANK, c * BANK + width)
                            dve.tensor_tensor_reduce(probs[:, slot, keys], bank[:, 0:width], bias[h][:, keys], 1.0,
                                                     NEG, ALU.add, ALU.max, most[:, slot, c:c + 1]
                                                     ).then_inc(scores_used, 1)
                            if c < CHUNKS[i] - 1:
                                continue
                            dve.wait_ge(scores_used, it * HEADS * S_HEAD + S_BANKS + s + 1)
                            dve.tensor_reduce(neg_most[:, slot:slot + 1], most[:, slot, 0:CHUNKS[i]], AX.X, ALU.max,
                                              negate=True).then_inc(most_ready, 1)
                        if kind == "key":
                            q, j = rest
                            skip = max(0, j - 4 * q) * P
                            dve.wait_ge(hi_ready, head * J_HEAD + J_AT[q] + j + 1)
                            b = (J_AT[q] + j) % PT_SLOTS
                            dve.tensor_tensor(pt_lo[:, b, skip:BANK], bank_of(st)[:, skip:BANK],
                                              pt_hi[:, b, skip:BANK].bitcast(F32), ALU.subtract).then_inc(turned_used, 1)
                        if kind == "back":
                            q = rest[0]
                            n = it * len(quads) + h * QUADS + q
                            dve.wait_ge(exp_ready, head * NT + 4 * q + 4)
                            dve.reciprocal(inverse[:], row_sum[:, h * NT + 4 * q:h * NT + 4 * q + 4]
                                           ).then_inc(inverse_ready, 1)
                            dve.wait_ge(inverse_ready, n + 1)
                            if q == 0:
                                dve.wait_ge(z_loaded[h], (it + 1) * 16)
                            dve.wait_ge(turned_ready, it * TURNS + turn_at[st] + 1)
                            for t in range(4):
                                last = dve.scalar_tensor_tensor(out=o_rows[h][:, 4 * q + t, :],
                                                                in0=bank_of(st)[:, t * P:t * P + FD],
                                                                scalar=inverse[:, t:t + 1], in1=z[h][:, 4 * q + t, :],
                                                                op0=ALU.mult, op1=ALU.mult)
                            last.then_inc(rows_ready, 1)
                            dve.wait_ge(rows_ready, n + 2 * QUADS + 1)
                            dve.sem_inc(turned_used, 1)


def lower_bound(nc, core, lb_param):
    core.bound = core.ctx.enter_context(nc.sbuf_tensor("bound", [P, HH], F32))
    core.rest = core.ctx.enter_context(nc.sbuf_tensor("rest", [P, HH], F32))
    with ExitStack() as ctx:
        def sb(name, shape):
            return ctx.enter_context(nc.sbuf_tensor(f"lb_{name}", shape, F32))

        layers, shifted, most, total = sb("layers", [P, 2, HH]), sb("shifted", [P, 2, HH]), sb("most", [P, HH]), \
            sb("total", [P, HH])
        loaded, step, asked, exp_ready = (core.sem(f"lb_{n}") for n in ("loaded", "step", "asked", "exp_ready"))
        with nc.Block() as block:
            @block.sync
            def _(sp):
                with nc.allow_non_contiguous_dma(reason="1024 parameters, turned"):
                    for layer in range(2):
                        sp.dma_start(layers[:, layer, :],
                                     lb_param[layer].rearrange("(h p) -> p h", p=P)).then_inc(loaded, 16)

            @block.vector
            def _(dve):
                link = linker(dve, step)
                dve.wait_ge(loaded, 32)
                link(dve.tensor_tensor(most[:], layers[:, 0, :], layers[:, 1, :], ALU.max))
                link(dve.tensor_tensor(shifted[:], layers[:], most[:].unsqueeze(1).to_broadcast([P, 2, HH]),
                                       ALU.subtract))
                dve.sem_inc(asked, 1)
                dve.wait_ge(exp_ready, 1)
                link(dve.tensor_tensor(total[:], shifted[:, 0, :], shifted[:, 1, :], ALU.add))
                link(dve.reciprocal(total[:], total[:]))
                link(dve.tensor_tensor(core.bound[:], shifted[:, 0, :], total[:], ALU.mult))
                link(dve.tensor_scalar(core.rest[:], core.bound[:], -1.0, 1.0, ALU.mult, ALU.add))

            @block.scalar
            def _(act):
                act.wait_ge(asked, 1)
                act.activation(shifted[:], shifted[:], ACT.Exp).then_inc(exp_ready, 1)


def recur_prompt(nc, core, queries, gates, values, z_hg, gain, gated, state_out, cache):
    CH = 4
    BLOCKS = T // (CH * P)
    LEVELS = [P // 2, P // 4, P // 8]
    LEAF = P // 8
    CLAMP = 85.0
    NL = len(LEVELS)
    UNITS_, CHUNKS_ = HH, HH * CH
    DS = NL + 2
    ES = NL + 4

    with ExitStack() as ctx:
        def sb(name, shape, dt=F32):
            return ctx.enter_context(nc.sbuf_tensor(f"hg_{name}", shape, dt))

        def per_head(name, shape):
            return [sb(f"{name}{h}", shape) for h in range(HH)]

        def psum(name, n):
            return [ctx.enter_context(nc.psum_tensor(f"hg_{name}{i}", [P, BANK], F32)) for i in range(n)]

        q, f = per_head("q", [P, BANK]), per_head("f", [P, BANK])
        k, b = per_head("k", [P, BANK]), per_head("b", [P, BANK])
        level = [per_head(f"level{n}_", [P, BANK]) for n in range(NL)]
        leaf_q, leaf_k = per_head("leaf_q", [P, BANK]), per_head("leaf_k", [P, BANK])
        q_run, k_rest = per_head("q_run", [P, BANK]), per_head("k_rest", [P, BANK])
        decay = per_head("decay", [P, CH])
        log_f = sb("log_f", [P, BANK])
        v, z = sb("v", [P, CH, W]), sb("z", [P, CH, W])
        gains = sb("gains", [P, W])
        masks = sb("masks", [P, NL + 1, P])
        masked = [sb(f"masked{i}", [P, NL + 1, P]) for i in range(2)]
        weights = [sb(f"weights{i}", [P, P]) for i in range(2)]
        k_rows = [sb(f"k_rows{i}", [P, P]) for i in range(2)]
        state = sb("state", [P, HH, P])
        o_rows, square = sb("o_rows", [P, CH, W]), sb("square", [P, CH, W])
        stat = sb("stat", [P, CH * HH])
        root = sb("root", [P, CH * HH])
        primer = nc.dram_tensor("hg_primer", (1, P), F32, kind="Internal").ap()
        att = psum("att", 2)
        turned, o_sum, kv = (psum(n, 1)[0][:, 0:P] for n in ("turned", "o_sum", "kv"))
        paged = CacheAttention(nc, core, ctx, *cache)
        HALF = BLOCKS // 2
        assert paged.GROUPS == HALF * CHUNKS_

        def round_of(blk, n):
            return blk * (CHUNKS_ // paged.SLOTS) + n // paged.SLOTS, n % paged.SLOTS

        def sem(name):
            return core.sem(f"hg_{name}")

        raw_loaded = [sem(f"raw_loaded{h}") for h in range(HH)]
        v_loaded, z_loaded, gains_loaded = sem("v_loaded"), sem("z_loaded"), sem("gains_loaded")
        unit_ready = sem("unit_ready")
        consts, consts_step = sem("consts"), sem("consts_step")
        f_ready, k_ready, log_ready, b_ready = sem("f_ready"), sem("k_ready"), sem("log_ready"), sem("b_ready")
        diff_ready, exp_ready = sem("diff_ready"), sem("exp_ready")
        diff_step = sem("diff_step")
        att_ready, att_used, weights_ready = sem("att_ready"), sem("att_used"), sem("weights_ready")
        turned_ready, k_rows_ready = sem("turned_ready"), sem("k_rows_ready")
        o_ready, o_taken = sem("o_ready"), sem("o_taken")
        kv_ready, state_ready = sem("kv_ready"), sem("state_ready")
        masked_ready, post_step, mean_ready, root_ready = sem("masked_ready"), sem("post_step"), \
            sem("mean_ready"), sem("root_ready")
        rows_ready, stored, state_stored = sem("rows_ready"), sem("stored"), sem("state_stored")
        paced = sem("paced")
        POST = 5

        with nc.Block() as block:
            @block.sync
            def _(sp):
                sp.dma_start(gains[:], gain.partition_broadcast(P)).then_inc(gains_loaded, 16)
                paged.sync_start(sp)

                def block_of(blk, first_block, source, first):
                    columns, rows = bass.ds(blk * BANK, BANK), bass.ds(blk * BANK, BANK)
                    for h in range(HH):
                        sp.wait_ge(unit_ready, blk * HH + h + 1)
                        sp.dma_start(q[h][:], queries[h * P:(h + 1) * P, columns]).then_inc(raw_loaded[h], 16)
                        sp.dma_start(f[h][:], gates[h * P:(h + 1) * P, columns]).then_inc(raw_loaded[h], 16)
                    for n in range(CHUNKS_):
                        if n == paged.SLOTS:
                            sp.wait_ge(state_ready, (blk + 1) * CHUNKS_)
                            sp.dma_start(v[:], values[rows, :].rearrange("(c p) n -> p c n", p=P)).then_inc(v_loaded, 16)
                        if n == paged.SLOTS + 1:
                            sp.wait_ge(rows_ready, blk + 1)
                            sp.dma_start(z[:], z_hg[rows, :].rearrange("(c p) n -> p c n", p=P)).then_inc(z_loaded, 16)
                        paged.load_group(sp, source, first, *round_of(blk - first_block, n))

                with sp.Fori(0, HALF) as blk:
                    block_of(blk, 0, paged.k_pages, 0)
                with sp.Fori(HALF, BLOCKS) as blk:
                    block_of(blk, HALF, paged.v_pages, paged.GROUPS)
                paged.sync_end(sp)
                sp.wait_ge(state_ready, (BLOCKS + 1) * CHUNKS_)
                sp.dma_start(state_out.rearrange("h k v -> k h v"), state[:]).then_inc(state_stored, 16)
                sp.wait_ge(state_stored, 16)
                sp.wait_ge(stored, 16 * (BLOCKS + 1))

            @block.gpsimd
            def _(pool):
                link = linker(pool, consts_step)
                link(pool.memset(masks[:], 1.0))
                for n, width in enumerate([2 * half for half in LEVELS] + [LEAF]):
                    tile = masks[:, n, :].rearrange("s (g t) -> s g t", t=width)
                    groups = P // width
                    link(pool.affine_select(out=tile, in_=tile, compare_op=ALU.is_ge, fill=0.0, base=0,
                                            pattern=[[-width, groups], [0, width]], channel_multiplier=1))
                    link(pool.affine_select(out=tile, in_=tile, compare_op=ALU.is_ge, fill=0.0, base=width - 1,
                                            pattern=[[width, groups], [0, width]], channel_multiplier=-1))
                for n in range(NL):
                    link(pool.tensor_tensor(masks[:, n, :], masks[:, n, :], masks[:, n + 1, :], ALU.subtract))
                for n in range(NL + 1):
                    link(pool.affine_select(out=masks[:, n, :], in_=masks[:, n, :], compare_op=ALU.is_ge, fill=0.0,
                                            base=0, pattern=[[1, P]], channel_multiplier=-1))
                link(pool.memset(state[:], 0.0))
                pool.sem_inc(consts, 1)
                paged.pool_start(pool)

                def prepare(blk, h):
                    unit = blk * HH + h
                    pool.wait_ge(state_ready, blk * CHUNKS_ + (h + 1) * CH)
                    pool.wait_ge(raw_loaded[h], (blk + 1) * 32)
                    pool.sem_inc(paced, 1)
                    pool.tensor_scalar(f[h][:], f[h][:], core.rest[:, h:h + 1], core.bound[:, h:h + 1], ALU.mult,
                                       ALU.add).then_inc(f_ready, 1)
                    pool.wait_ge(f_ready, unit + 1)
                    pool.sem_inc(paced, 1)
                    pool.tensor_scalar(k[h][:], f[h][:], -1.0, 1.0, ALU.mult, ALU.add).then_inc(k_ready, 1)
                    pool.wait_ge(b_ready, unit + 1)

                    def difference(out, height, row):
                        blocks = b[h][:].rearrange("p (g t) -> p g t", t=height)
                        return pool.tensor_tensor(
                            out[:].rearrange("p (g t) -> p g t", t=height), blocks,
                            blocks[:, :, row:row + 1].to_broadcast([P, BANK // height, height]), ALU.subtract)

                    for n, half in enumerate(LEVELS):
                        difference(level[n][h], 2 * half, half - 1).then_inc(diff_ready, 1)
                    difference(k_rest[h], P, P - 1).then_inc(diff_ready, 1)
                    difference(leaf_k[h], LEAF, LEAF // 2 - 1).then_inc(diff_step, 1)
                    pool.wait_ge(diff_step, unit + 1)
                    pool.sem_inc(paced, 1)
                    pool.tensor_scalar(leaf_k[h][:], leaf_k[h][:], CLAMP, -CLAMP, ALU.min,
                                       ALU.max).then_inc(diff_ready, 1)

                with pool.Fori(0, HALF) as blk:
                    in_order(lambda h: prepare(blk, h), lambda h, c: None, lambda h, c: None,
                             lambda n: paged.pool_keys(pool, *round_of(blk, n)))
                with pool.Fori(HALF, BLOCKS) as blk:
                    def row(n):
                        if n % paged.GB == paged.GB - 1:
                            paged.store_row(pool, (blk - HALF) * (CHUNKS_ // paged.GB) + n // paged.GB,
                                            n // paged.GB % 2)

                    in_order(lambda h: prepare(blk, h), lambda h, c: None, lambda h, c: None, row)

            @block.scalar
            def _(act):
                act.dma_start(primer, core.ident[0:1, :]).then_inc(stored, 16)

                def prepare(blk, h):
                    unit = blk * HH + h
                    act.wait_ge(f_ready, unit + 1)
                    act.activation(log_f[:], f[h][:], ACT.Ln).then_inc(log_ready, 1)
                    act.wait_ge(b_ready, unit + 1)
                    ends = b[h][:].rearrange("p (c t) -> p c t", t=P)[:, :, P - 1]
                    act.wait_ge(state_ready, blk * CHUNKS_ + (h + 1) * CH)
                    act.activation(decay[h][:], ends, ACT.Exp)
                    act.activation(q_run[h][:], b[h][:], ACT.Exp).then_inc(exp_ready, 1)
                    for n, half in enumerate(LEVELS):
                        act.wait_ge(diff_ready, unit * DS + n + 1)
                        halves = level[n][h][:].rearrange("p (g u t) -> p g u t", u=2, t=half)
                        act.activation(halves[:, :, 1, :], halves[:, :, 1, :], ACT.Exp)
                        act.activation(halves[:, :, 0, :], halves[:, :, 0, :], ACT.Exp, scale=-1.0).then_inc(exp_ready, 1)
                    act.wait_ge(diff_ready, unit * DS + NL + 1)
                    act.activation(k_rest[h][:], k_rest[h][:], ACT.Exp, scale=-1.0).then_inc(exp_ready, 1)
                    act.wait_ge(diff_ready, unit * DS + NL + 2)
                    act.activation(leaf_q[h][:], leaf_k[h][:], ACT.Exp).then_inc(exp_ready, 1)
                    act.wait_ge(exp_ready, unit * ES + NL + 3)
                    act.activation(leaf_k[h][:], leaf_k[h][:], ACT.Exp, scale=-1.0).then_inc(exp_ready, 1)

                def rows_of_keys(blk, h, c):
                    n = h * CH + c
                    act.wait_ge(turned_ready, blk * CHUNKS_ + n + 1)
                    act.wait_ge(kv_ready, blk * CHUNKS_ + n + 1)
                    act.activation(k_rows[n % 2][:], turned, ACT.Copy).then_inc(k_rows_ready, 1)

                def take(blk, h, c):
                    n = h * CH + c
                    if n == 0:
                        act.wait_ge(stored, (blk + 1) * 16)
                    act.wait_ge(o_ready, blk * CHUNKS_ + n + 1)
                    act.activation(o_rows[:, c, h * P:(h + 1) * P], o_sum, ACT.Copy).then_inc(o_taken, 1)

                def block_of(blk, extra):
                    in_order(lambda h: prepare(blk, h), lambda h, c: rows_of_keys(blk, h, c),
                             lambda h, c: take(blk, h, c), extra)
                    act.wait_ge(mean_ready, blk + 1)
                    act.activation(root[:], stat[:], ACT.Sqrt).then_inc(root_ready, 1)
                    act.wait_ge(rows_ready, blk + 2)
                    act.dma_start(gated[bass.ds(blk * BANK, BANK), :].rearrange("(c p) n -> p c n", p=P), o_rows[:]
                                  ).then_inc(stored, 16)

                with act.Fori(0, HALF) as blk:
                    block_of(blk, lambda n: None)
                paged.scalar_middle(act)
                with act.Fori(HALF, BLOCKS) as blk:
                    block_of(blk, lambda n: paged.scalar_values(act, *round_of(blk - HALF, n)))

            @block.vector
            def _(dve):
                dve.sem_inc(unit_ready, UNITS_)
                dve.sem_inc(att_used, 2)
                dve.sem_inc(state_ready, CHUNKS_)
                dve.sem_inc(rows_ready, 1)
                dve.wait_ge(consts, 1)
                paged.vector_start(dve)

                def prepare(blk, h):
                    unit = blk * HH + h
                    dve.wait_ge(log_ready, unit + 1)
                    for c in range(CH):
                        at = slice(c * P, (c + 1) * P)
                        last = dve.tensor_tensor_scan(b[h][:, at], paged.ones[:], log_f[:, at], 0.0, ALU.mult, ALU.add)
                    last.then_inc(b_ready, 1)
                    dve.wait_ge(k_ready, unit + 1)
                    dve.wait_ge(exp_ready, unit * ES + 1)
                    dve.tensor_tensor(q_run[h][:], q_run[h][:], q[h][:], ALU.mult)
                    for n, half in enumerate(LEVELS):
                        dve.wait_ge(exp_ready, unit * ES + n + 2)
                        for u, factor in enumerate((k[h], q[h])):
                            at = [t[:].rearrange("p (g u t) -> p g u t", u=2, t=half)[:, :, u, :]
                                  for t in (level[n][h], factor)]
                            dve.tensor_tensor(at[0], at[0], at[1], ALU.mult)
                    dve.wait_ge(exp_ready, unit * ES + NL + 2)
                    dve.tensor_tensor(k_rest[h][:], k_rest[h][:], k[h][:], ALU.mult)
                    dve.wait_ge(exp_ready, unit * ES + NL + 4)
                    dve.tensor_tensor(leaf_q[h][:], leaf_q[h][:], q[h][:], ALU.mult)
                    dve.tensor_tensor(leaf_k[h][:], leaf_k[h][:], k[h][:], ALU.mult).then_inc(unit_ready, 1)

                def weigh(blk, h, c):
                    n = h * CH + c
                    dve.wait_ge(att_ready, blk * CHUNKS_ + n + 1)
                    dve.tensor_tensor(masked[n % 2][:], att[n % 2][:].rearrange("s (n t) -> s n t", t=P), masks[:],
                                      ALU.mult).then_inc(att_used, 1)
                    dve.wait_ge(att_used, blk * CHUNKS_ + n + 3)
                    dve.tensor_reduce(weights[n % 2][:], masked[n % 2][:].rearrange("s n t -> s t n"), AX.X,
                                      ALU.add).then_inc(weights_ready, 1)

                def advance(blk, h, c):
                    n = h * CH + c
                    dve.wait_ge(weights_ready, blk * CHUNKS_ + n + 1)
                    dve.wait_ge(kv_ready, blk * CHUNKS_ + n + 3)
                    dve.wait_ge(o_ready, blk * CHUNKS_ + n + 1)
                    dve.scalar_tensor_tensor(out=state[:, h, :], in0=state[:, h, :], scalar=decay[h][:, c:c + 1],
                                             in1=kv, op0=ALU.mult, op1=ALU.add).then_inc(state_ready, 1)

                def block_of(blk, extra):
                    in_order(lambda h: prepare(blk, h), lambda h, c: weigh(blk, h, c), lambda h, c: advance(blk, h, c),
                             extra)
                    link = linker(dve, post_step, blk * POST)
                    dve.wait_ge(o_taken, blk * CHUNKS_ + CHUNKS_ + 2)
                    link(dve.tensor_tensor(square[:], o_rows[:], o_rows[:], ALU.mult))
                    heads = [t[:].rearrange("p c (h d) -> p (c h) d", d=HD) for t in (square, o_rows)]
                    link(dve.tensor_reduce(stat[:], heads[0], AX.X, ALU.add))
                    dve.tensor_scalar(stat[:], stat[:], 1.0 / HD, EPS, ALU.mult, ALU.add).then_inc(mean_ready, 1)
                    dve.wait_ge(root_ready, blk + 1)
                    link(dve.reciprocal(root[:], root[:]))
                    link(dve.tensor_tensor(heads[1], heads[1],
                                           root[:].unsqueeze(2).to_broadcast([P, CH * HH, HD]), ALU.mult))
                    dve.wait_ge(gains_loaded, 16)
                    link(dve.tensor_tensor(o_rows[:], o_rows[:], gains[:].unsqueeze(1).to_broadcast([P, CH, W]),
                                           ALU.mult))
                    dve.wait_ge(z_loaded, (blk + 1) * 16)
                    dve.tensor_tensor(o_rows[:], o_rows[:], z[:], ALU.mult).then_inc(rows_ready, 1)

                with dve.Fori(0, HALF) as blk:
                    block_of(blk, lambda n: paged.vector_keys(dve, *round_of(blk, n)))
                paged.vector_middle(dve)
                with dve.Fori(HALF, BLOCKS) as blk:
                    def row(n):
                        if n % paged.GB == paged.GB - 1:
                            b = n // paged.GB
                            paged.copy_row(dve, (blk - HALF) * (CHUNKS_ // paged.GB) + b, b % 2,
                                           (blk - HALF) * (CHUNKS_ // paged.GB // 2) + b // 2)

                    block_of(blk, row)
                paged.vector_end(dve)

            @block.tensor
            def _(pe):
                pe.sem_inc(k_rows_ready, 2)
                pe.sem_inc(kv_ready, 2)
                pe.sem_inc(o_taken, 2)

                def pairs(blk, h, c):
                    n = h * CH + c
                    at = slice(c * P, (c + 1) * P)
                    if c == 0:
                        pe.wait_ge(unit_ready, blk * HH + h + 1 + UNITS_)
                    pe.wait_ge(att_used, blk * CHUNKS_ + n + 1)
                    for m in range(NL):
                        pe.matmul(att[n % 2][:, m * P:(m + 1) * P], level[m][h][:, at], level[m][h][:, at],
                                  start=True, stop=True)
                    pe.matmul(att[n % 2][:, NL * P:(NL + 1) * P], leaf_k[h][:, at], leaf_q[h][:, at], start=True,
                              stop=True).then_inc(att_ready, 1)
                    pe.wait_ge(k_rows_ready, blk * CHUNKS_ + n + 2)
                    pe.transpose(turned, k_rest[h][:, at], core.ident[:]).then_inc(turned_ready, 1)

                def sums(blk, h, c):
                    n = h * CH + c
                    at = slice(c * P, (c + 1) * P)
                    if n == 0:
                        pe.wait_ge(v_loaded, (blk + 1) * 16)
                    pe.wait_ge(o_taken, blk * CHUNKS_ + n + 2)
                    pe.wait_ge(weights_ready, blk * CHUNKS_ + n + 1)
                    pe.matmul(o_sum, weights[n % 2][:], v[:, c, h * P:(h + 1) * P], start=True,
                              stop=False)
                    pe.wait_ge(state_ready, (blk + 1) * CHUNKS_ + n)
                    pe.matmul(o_sum, q_run[h][:, at], state[:, h, :], start=False,
                              stop=True).then_inc(o_ready, 1)
                    pe.wait_ge(k_rows_ready, blk * CHUNKS_ + n + 3)
                    pe.matmul(kv, k_rows[n % 2][:], v[:, c, h * P:(h + 1) * P], start=True,
                              stop=True).then_inc(kv_ready, 1)

                pe.wait_ge(consts, 1)
                paged.tensor_start(pe)

                def block_of(blk, extra):
                    in_order(lambda h: None, lambda h, c: pairs(blk, h, c), lambda h, c: sums(blk, h, c), extra)

                with pe.Fori(0, HALF) as blk:
                    block_of(blk, lambda n: None)
                paged.tensor_middle(pe)
                with pe.Fori(HALF, BLOCKS) as blk:
                    block_of(blk, lambda n: paged.tensor_values(pe, *round_of(blk - HALF, n), n // paged.GB % 2))


def in_order(prepare, early, late, extra):
    chunks = [(h, c) for h in range(HH) for c in range(HH)]
    for n, (h, c) in enumerate(chunks):
        if n == 0:
            prepare(0)
        if c == 0 and h + 1 < HH:
            prepare(h + 1)
        early(h, c)
        if n > 0:
            late(*chunks[n - 1])
        extra(n)
    late(*chunks[-1])


def attend_memory(nc, core, queries, mem_k, mem_v, z_mem, gated):
    ST = NM // P
    BLK = 4
    TILES = 2 * BLK
    PAIRS = HH // 2
    SCALE = HD ** -0.5
    PASSES = NT // TILES

    with ExitStack() as ctx:
        def sb(name, shape, dt=F32):
            return ctx.enter_context(nc.sbuf_tensor(f"mem_{name}", shape, dt))

        def psum(name):
            return [ctx.enter_context(nc.psum_tensor(f"mem_{name}{i}", [P, BANK], F32)) for i in range(2)]

        k_rows, v = sb("k_rows", [P, ST, W]), sb("v", [P, ST, W])
        keys = sb("keys", [P, HH, NM])
        q = [sb(f"q{i}", [P, HH, BLK * P]) for i in range(2)]
        z = [sb(f"z{i}", [P, BLK, W]) for i in range(2)]
        o_rows = [sb(f"o_rows{i}", [P, BLK, W]) for i in range(2)]
        probs = [sb(f"probs{i}", [P, HH, NM]) for i in range(2)]
        neg_most = sb("neg_most", [P, 4, HH])
        bias = sb("bias", [P, 4, HH])
        row_sum, inverse = sb("row_sum", [P, 4, HH]), sb("inverse", [P, HH])
        pt = [sb(f"pt{i}", [P, BANK]) for i in range(4)]
        primer = nc.dram_tensor("mem_primer", (2, P), F32, kind="Internal").ap()
        scores, turned, o_sum = psum("scores"), psum("turned"), psum("o_sum")

        def sem(name):
            return core.sem(f"mem_{name}")

        kv_loaded, k_flipped, keys_ready = sem("kv_loaded"), sem("k_flipped"), sem("keys_ready")
        q_loaded, z_loaded = [sem(f"q_loaded{i}") for i in range(2)], [sem(f"z_loaded{i}") for i in range(2)]
        scored, exp_ready = sem("scored"), sem("exp_ready")
        most_step, bias_ready = sem("most_step"), sem("bias_ready")
        pt_ready, pt_copied = sem("pt_ready"), sem("pt_copied")
        o_ready = sem("o_ready")
        inverse_ready, rows_ready = sem("inverse_ready"), sem("rows_ready")
        stored = [sem(f"stored{i}") for i in range(2)]

        with nc.Block() as block:
            @block.sync
            def _(sp):
                def rows(dram, blk):
                    return dram[bass.ds(blk * BLK * P, BLK * P), :].rearrange("(t p) c -> p t c", p=P)

                sp.dma_start(k_rows[:], mem_k.rearrange("(t p) c -> p t c", p=P)).then_inc(kv_loaded, 16)
                sp.dma_start(v[:], mem_v.rearrange("(t p) c -> p t c", p=P)).then_inc(kv_loaded, 16)
                for i in range(2):
                    sp.dma_start(primer[i:i + 1, :], core.ident[0:1, :]).then_inc(stored[i], 16)
                with sp.Fori(0, PASSES) as it:
                    for i in range(2):
                        blk = it * 2 + i
                        sp.wait_ge(rows_ready, (blk + 1) * BLK)
                        sp.dma_start(q[i][:], queries[:, bass.ds(blk * BLK * P, BLK * P)]
                                     .rearrange("(h p) t -> p h t", p=P)).then_inc(q_loaded[i], 16)
                        sp.dma_start(z[i][:], rows(z_mem, blk)).then_inc(z_loaded[i], 16)
                    for i in range(2):
                        blk = it * 2 + i
                        sp.wait_ge(rows_ready, (blk + 3) * BLK)
                        sp.dma_start(rows(gated, blk), o_rows[i][:]).then_inc(stored[i], 16)
                for i in range(2):
                    sp.wait_ge(stored[i], 16 * (PASSES + 1))

            def in_step(score, turn, value):
                for u in range(TILES + 2):
                    if u < TILES:
                        score(u)
                    if 0 <= u - 1 < TILES:
                        turn(u - 1)
                    if u >= 2:
                        value(u - 2)

            @block.tensor
            def _(pe):
                pe.sem_inc(exp_ready, 2)
                pe.wait_ge(kv_loaded, 32)
                for t in range(ST):
                    for h in range(HH):
                        m = pe.transpose(turned[t][:, h * P:(h + 1) * P], k_rows[:, t, h * P:(h + 1) * P], core.ident[:])
                m.then_inc(k_flipped, 1)
                pe.wait_ge(keys_ready, 1)
                with pe.Fori(0, PASSES) as it:
                    def score(u):
                        for p in range(PAIRS):
                            n = (it * TILES + u) * PAIRS + p
                            if u % BLK == 0:
                                pe.wait_ge(q_loaded[u // BLK], (it + 1) * 16)
                            pe.wait_ge(exp_ready, n + 1)
                            for e in range(2):
                                h = 2 * p + e
                                m = pe.matmul(scores[p][:, e * NM:(e + 1) * NM],
                                              q[u // BLK][:, h, u % BLK * P:(u % BLK + 1) * P], keys[:, h, :],
                                              start=True, stop=True)
                            m.then_inc(scored, 1)

                    def turn(u):
                        for p in range(PAIRS):
                            n = (it * TILES + u) * PAIRS + p
                            pe.wait_ge(exp_ready, n + 3)
                            pe.wait_ge(pt_copied, n + 1)
                            for e in range(2):
                                for t in range(ST):
                                    m = pe.transpose(turned[p][:, (e * ST + t) * P:(e * ST + t + 1) * P],
                                                     probs[u % 2][:, 2 * p + e, t * P:(t + 1) * P], core.ident[:])
                            m.then_inc(pt_ready, 1)

                    def value(u):
                        tile = it * TILES + u
                        pe.wait_ge(pt_copied, (tile + 1) * PAIRS + 2)
                        pe.wait_ge(rows_ready, tile + 2 * BLK - 1)
                        for h in range(HH):
                            for t in range(ST):
                                m = pe.matmul(o_sum[u % 2][:, h * P:(h + 1) * P],
                                              pt[u % 2 * 2 + h // 2][:, (h % 2 * ST + t) * P:(h % 2 * ST + t + 1) * P],
                                              v[:, t, h * P:(h + 1) * P], start=(t == 0), stop=(t == ST - 1))
                        m.then_inc(o_ready, 1)

                    in_step(score, turn, value)

            @block.vector
            def _(dve):
                dve.sem_inc(pt_copied, 2)
                dve.sem_inc(rows_ready, 2 * BLK)
                dve.wait_ge(k_flipped, 1)
                for t in range(ST):
                    m = dve.tensor_copy(keys[:, :, t * P:(t + 1) * P], turned[t][:].rearrange("d (h s) -> d h s", s=P))
                m.then_inc(keys_ready, 1)
                with dve.Fori(0, PASSES) as it:
                    def score(u):
                        for p in range(PAIRS):
                            n = (it * TILES + u) * PAIRS + p
                            two = slice(2 * p, 2 * p + 2)
                            dve.wait_ge(scored, n + 1)
                            dve.tensor_reduce(neg_most[:, u % 4, two],
                                              scores[p][:].rearrange("p (e s) -> p e s", s=NM), AX.X, ALU.max,
                                              negate=True).then_inc(most_step, 1)
                            dve.wait_ge(most_step, n + 1)
                            dve.tensor_scalar(bias[:, u % 4, two], neg_most[:, u % 4, two], SCALE, None,
                                              ALU.mult).then_inc(bias_ready, 1)

                    def turn(u):
                        for p in range(PAIRS):
                            n = (it * TILES + u) * PAIRS + p
                            dve.wait_ge(pt_ready, n + 1)
                            dve.tensor_copy(pt[u % 2 * 2 + p][:], turned[p][:]).then_inc(pt_copied, 1)

                    def value(u):
                        tile = it * TILES + u
                        dve.wait_ge(exp_ready, (tile + 1) * PAIRS + 2)
                        dve.reciprocal(inverse[:], row_sum[:, u % 4, :]).then_inc(inverse_ready, 1)
                        if u % BLK == 0:
                            dve.wait_ge(z_loaded[u // BLK], (it + 1) * 16)
                            dve.wait_ge(stored[u // BLK], (it + 1) * 16)
                        dve.wait_ge(o_ready, tile + 1)
                        dve.wait_ge(inverse_ready, tile + 1)
                        for h in range(HH):
                            at = slice(h * P, (h + 1) * P)
                            m = dve.scalar_tensor_tensor(out=o_rows[u // BLK][:, u % BLK, at], in0=o_sum[u % 2][:, at],
                                                         scalar=inverse[:, h:h + 1], in1=z[u // BLK][:, u % BLK, at],
                                                         op0=ALU.mult, op1=ALU.mult)
                        m.then_inc(rows_ready, 1)
                        dve.wait_ge(rows_ready, tile + 2 * BLK + 1)

                    in_step(score, turn, value)

            @block.scalar
            def _(act):
                with act.Fori(0, PASSES) as it:
                    for u in range(TILES):
                        for p in range(PAIRS):
                            n = (it * TILES + u) * PAIRS + p
                            act.wait_ge(bias_ready, n + 1)
                            for h in (2 * p, 2 * p + 1):
                                m = act.activation(probs[u % 2][:, h, :], scores[p][:, h % 2 * NM:(h % 2 + 1) * NM],
                                                   ACT.Exp, scale=SCALE, bias=bias[:, u % 4, h:h + 1],
                                                   accum_out=row_sum[:, u % 4, h:h + 1])
                            m.then_inc(exp_ready, 1)


def weights_split(nc, core, tag, ctx, loads):
    tiles = sum(w.shape[0] // P for w in loads)
    hi = ctx.enter_context(nc.sbuf_tensor(f"{tag}_w_hi", [P, tiles, D], F32R))
    lo = ctx.enter_context(nc.sbuf_tensor(f"{tag}_w_lo", [P, tiles, D], F32R))
    with ExitStack() as inner:
        raw = [inner.enter_context(nc.sbuf_tensor(f"{tag}_w_raw{r}", [P, 2, D], F32)) for r in range(3)]
        loaded = [core.sem(f"{tag}_w_loaded{r}") for r in range(3)]
        hi_ready, lo_ready = core.sem(f"{tag}_w_hi_ready"), core.sem(f"{tag}_w_lo_ready")
        sources = [w.rearrange("(t p) n -> p t n", p=P)[:, t:t + 2, :] for w in loads for t in range(0, w.shape[0] // P, 2)]
        with nc.Block() as block:
            @block.sync
            def _(sp):
                for n, src in enumerate(sources):
                    if n >= 3:
                        sp.wait_ge(lo_ready, n - 2)
                    sp.dma_start(raw[n % 3][:], src).then_inc(loaded[n % 3], 16)

            @block.scalar
            def _(act):
                for n in range(len(sources)):
                    act.wait_ge(loaded[n % 3], 16 * (n // 3 + 1))
                    act.activation(hi[:, 2 * n:2 * n + 2, :], raw[n % 3][:], ACT.Copy).then_inc(hi_ready, 1)

            @block.vector
            def _(dve):
                for n in range(len(sources)):
                    dve.wait_ge(hi_ready, n + 1)
                    dve.tensor_tensor(lo[:, 2 * n:2 * n + 2, :], raw[n % 3][:], hi[:, 2 * n:2 * n + 2, :].bitcast(F32),
                                      ALU.subtract).then_inc(lo_ready, 1)
    return hi, lo


def merge_branches(nc, core, gated, gates, w_branches, mixed):
    TILES = NT + 1
    BT = W // P
    NB = 3
    KTILES = NB * BT
    HALVES = D // BANK
    with ExitStack() as ctx:
        def sb(name, shape, dt=F32):
            return [ctx.enter_context(nc.sbuf_tensor(f"mb_{name}{i}", shape, dt)) for i in range(2)]

        w_hi, w_lo = weights_split(nc, core, "mb", ctx, w_branches)
        g_in = sb("g_in", [P, KTILES * P])
        gate = sb("gate", [P, NB * HALVES, BANK])
        t_hi, t_lo = sb("t_hi", [P, KTILES, P], F32R), sb("t_lo", [P, KTILES, P], F32R)
        total = sb("total", [P, HALVES, BANK])
        term = ctx.enter_context(nc.sbuf_tensor("mb_term", [P, 2, BANK], F32))
        turned = [ctx.enter_context(nc.psum_tensor(f"mb_turned{i}", [P, BANK], F32)) for i in range(2)]
        out = [ctx.enter_context(nc.psum_tensor(f"mb_out{i}", [P, BANK], F32)) for i in range(NB * HALVES)]
        primer = nc.dram_tensor("mb_primer", (2, P), F32, kind="Internal").ap()

        def sem(name):
            return core.sem(f"mb_{name}")

        loaded = [sem(f"loaded{i}") for i in range(2)]
        gate_loaded = [sem(f"gate_loaded{i}") for i in range(2)]
        stored = [sem(f"stored{i}") for i in range(2)]
        turned_ready, hi_ready, split = sem("turned_ready"), sem("hi_ready"), sem("split")
        multiplied = sem("multiplied")
        term_ready = sem("term_ready")
        total_ready = sem("total_ready")
        summed = sem("summed")
        PER = NB * HALVES

        def tiles(eng, turn, body):
            for b in range(NB):
                turn(0, 0, 0, b)
            with eng.Fori(0, TILES // 2) as it:
                for i in range(2):
                    body(it * 2 + i, i, it, lambda b, i=i: turn(it * 2 + i + 1, 1 - i, it + i, b))
            body(TILES - 1, 0, TILES // 2, lambda b: None)

        def bank_of(i, b):
            return turned[(i * NB + b) % 2]

        with nc.Block() as block:
            @block.sync
            def _(sp):
                def load_rows(tile, i):
                    sp.dma_start(g_in[i][:], gated[bass.ds(tile * P, P), :]).then_inc(loaded[i], 16)

                def load_gates(tile, i):
                    sp.dma_start(gate[i][:], gates[:, bass.ds(tile * P, P), :].rearrange("g p n -> p g n")
                                 ).then_inc(gate_loaded[i], 16)

                def reload(tile, i):
                    sp.wait_ge(turned_ready, (tile + 1) * NB)
                    load_rows(tile + 2, i)
                    sp.wait_ge(total_ready, tile + 3)
                    load_gates(tile + 2, i)

                def store(tile, i):
                    sp.wait_ge(total_ready, tile + 3)
                    sp.dma_start(mixed[bass.ds(tile * P, P), :], total[i][:].rearrange("p h n -> p (h n)")
                                 ).then_inc(stored[i], 16)

                for i in range(2):
                    sp.dma_start(primer[i:i + 1, :], core.ident[0:1, :]).then_inc(stored[i], 16)
                    load_rows(i, i)
                    load_gates(i, i)
                with sp.Fori(0, (TILES - 3) // 2) as it:
                    for i in range(2):
                        reload(it * 2 + i, i)
                        store(it * 2 + i, i)
                reload(TILES - 3, 0)
                store(TILES - 3, 0)
                store(TILES - 2, 1)
                store(TILES - 1, 0)
                sp.wait_ge(stored[0], 16 * (TILES // 2 + 2))
                sp.wait_ge(stored[1], 16 * (TILES // 2 + 1))

            @block.tensor
            def _(pe):
                pe.sem_inc(split, 2)
                pe.sem_inc(term_ready, PER)

                def turn(tile, i, it, b):
                    if b == 0:
                        pe.wait_ge(loaded[i], (it + 1) * 16)
                    pe.wait_ge(split, tile * NB + b + 1)
                    for t in range(BT):
                        m = pe.transpose(bank_of(i, b)[:, t * P:(t + 1) * P],
                                         g_in[i][:, (b * BT + t) * P:(b * BT + t + 1) * P], core.ident[:])
                    m.then_inc(turned_ready, 1)

                def body(tile, i, it, turn_next):
                    for b in range(NB):
                        pe.wait_ge(split, tile * NB + b + 3)
                        for n in range(HALVES):
                            u = b * HALVES + n
                            pe.wait_ge(term_ready, tile * PER + u + 1)
                            for k in range(BT):
                                kk = b * BT + k
                                m = product(pe, out[u][:], (t_hi[i][:, kk, :], t_lo[i][:, kk, :]),
                                            [w[:, kk, n * BANK:(n + 1) * BANK] for w in (w_hi, w_lo)], k == 0,
                                            k == BT - 1)
                            m.then_inc(multiplied, 1)
                        if b == 0:
                            turn_next(0)
                            turn_next(1)
                        if b == 1:
                            turn_next(2)

                tiles(pe, turn, body)

            @block.scalar
            def _(act):
                def turn(tile, i, it, b):
                    act.wait_ge(turned_ready, tile * NB + b + 1)
                    act.activation(t_hi[i][:, b * BT:(b + 1) * BT, :],
                                   bank_of(i, b)[:].rearrange("p (t q) -> p t q", q=P), ACT.Copy).then_inc(hi_ready, 1)

                def body(tile, i, it, turn_next):
                    for b in range(NB):
                        turn_next(b)

                tiles(act, turn, body)

            @block.vector
            def _(dve):
                dve.sem_inc(total_ready, 2)

                def turn(tile, i, it, b):
                    at = slice(b * BT, (b + 1) * BT)
                    dve.wait_ge(hi_ready, tile * NB + b + 1)
                    dve.tensor_tensor(t_lo[i][:, at, :], bank_of(i, b)[:].rearrange("p (t q) -> p t q", q=P),
                                      t_hi[i][:, at, :].bitcast(F32), ALU.subtract).then_inc(split, 1)

                def body(tile, i, it, turn_next):
                    dve.wait_ge(stored[i], (it + 1) * 16)
                    dve.wait_ge(gate_loaded[i], (it + 1) * 16)
                    for b in range(NB):
                        for n in range(HALVES):
                            u = b * HALVES + n
                            dve.wait_ge(multiplied, tile * PER + u + 1)
                            to = total[i][:, n, :] if b == 0 else term[:, n, :]
                            dve.tensor_tensor(to, out[u][:], gate[i][:, u, :], ALU.mult).then_inc(term_ready, 1)
                            dve.wait_ge(term_ready, tile * PER + u + 1 + PER)
                            if b:
                                m = dve.tensor_tensor(total[i][:, n, :], total[i][:, n, :], term[:, n, :], ALU.add)
                                if b < NB - 1 or n < HALVES - 1:
                                    m.then_inc(summed, 1)
                                else:
                                    m.then_inc(total_ready, 1)
                        if b:
                            dve.wait_ge(summed, tile * 3 + (2 if b == 1 else 3))
                        if b == 0:
                            turn_next(0)
                            turn_next(1)
                        if b == 1:
                            turn_next(2)

                tiles(dve, turn, body)


def finish_rows(nc, core, mixed, w_o, x, x_s, gain, y, y_s):
    TILES = NT + 1
    HALVES = D // BANK
    with ExitStack() as ctx:
        def one(name, shape, dt=F32):
            return ctx.enter_context(nc.sbuf_tensor(f"fin_{name}", shape, dt))

        def sb(name, shape, dt=F32):
            return [one(f"{name}{i}", shape, dt) for i in range(2)]

        w_hi, w_lo = weights_split(nc, core, "fin", ctx, [w_o])
        m_in, x_in = sb("m_in", [P, D]), sb("x_in", [P, D])
        t_hi, t_lo = sb("t_hi", [P, KT, P], F32R), sb("t_lo", [P, KT, P], F32R)
        res, square = sb("res", [P, D]), one("square", [P, D])
        gains = one("gains", [P, D])
        stat = one("stat", [P, 4])
        turned = [ctx.enter_context(nc.psum_tensor(f"fin_turned{i}", [P, BANK], F32)) for i in range(2)]
        out = [ctx.enter_context(nc.psum_tensor(f"fin_out{i}", [P, BANK], F32)) for i in range(4)]
        primer = nc.dram_tensor("fin_primer", (2, P), F32, kind="Internal").ap()

        def sem(name):
            return core.sem(f"fin_{name}")

        loaded = [sem(f"loaded{i}") for i in range(2)]
        x_loaded = [sem(f"x_loaded{i}") for i in range(2)]
        stored = [sem(f"stored{i}") for i in range(2)]
        gains_loaded, cleared = sem("gains_loaded"), sem("cleared")
        turned_ready, hi_ready, split = sem("turned_ready"), sem("hi_ready"), sem("split")
        multiplied, added = sem("multiplied"), sem("added")
        step, mean_ready, root_ready = sem("step"), sem("mean_ready"), sem("root_ready")
        normed = sem("normed")

        def tiles(eng, turn, body):
            turn(0, 0, 0)
            with eng.Fori(0, TILES // 2) as it:
                for i in range(2):
                    body(it * 2 + i, i, it, lambda i=i: turn(it * 2 + i + 1, 1 - i, it + i))
            body(TILES - 1, 0, TILES // 2, lambda: None)

        with nc.Block() as block:
            @block.sync
            def _(sp):
                def load_rows(tile, i):
                    sp.dma_start(m_in[i][:], mixed[bass.ds(tile * P, P), :]).then_inc(loaded[i], 16)

                def load_x(tile, i, sample=False):
                    if sample:
                        sp.dma_start(x_in[i][0:B, :], x_s).then_inc(x_loaded[i], 16)
                    else:
                        sp.dma_start(x_in[i][:], x[bass.ds(tile * P, P), :]).then_inc(x_loaded[i], 16)

                def reload(tile, i, sample=False):
                    sp.wait_ge(turned_ready, tile * 2 + 2)
                    load_rows(tile + 2, i)
                    sp.wait_ge(added, tile * 2 + 6)
                    load_x(tile + 2, i, sample)

                def store(tile, i, sample=False):
                    sp.wait_ge(normed, tile + 3)
                    if sample:
                        sp.dma_start(y_s, res[i][0:B, :]).then_inc(stored[i], 16)
                    else:
                        sp.dma_start(y[bass.ds(tile * P, P), :], res[i][:]).then_inc(stored[i], 16)

                sp.dma_start(gains[:], gain.partition_broadcast(P)).then_inc(gains_loaded, 16)
                for i in range(2):
                    sp.dma_start(primer[i:i + 1, :], core.ident[0:1, :]).then_inc(stored[i], 16)
                    load_rows(i, i)
                    load_x(i, i)
                with sp.Fori(0, (TILES - 3) // 2) as it:
                    for i in range(2):
                        reload(it * 2 + i, i)
                        store(it * 2 + i, i)
                reload(TILES - 3, 0, True)
                store(TILES - 3, 0)
                store(TILES - 2, 1)
                store(TILES - 1, 0, True)
                sp.wait_ge(stored[0], 16 * (TILES // 2 + 2))
                sp.wait_ge(stored[1], 16 * (TILES // 2 + 1))

            @block.tensor
            def _(pe):
                pe.sem_inc(split, 2)
                pe.sem_inc(added, 4)

                def turn(tile, i, it):
                    pe.wait_ge(loaded[i], (it + 1) * 16)
                    for b in range(2):
                        pe.wait_ge(split, tile * 2 + b + 1)
                        for t in range(4):
                            m = pe.transpose(turned[b][:, t * P:(t + 1) * P],
                                             m_in[i][:, (b * 4 + t) * P:(b * 4 + t + 1) * P], core.ident[:])
                        m.then_inc(turned_ready, 1)

                def body(tile, i, it, turn_next):
                    for n in range(HALVES):
                        pe.wait_ge(added, tile * 2 + n + 1)
                        for k in range(KT):
                            if n == 0 and k % 4 == 0:
                                pe.wait_ge(split, tile * 2 + k // 4 + 3)
                            m = product(pe, out[i * 2 + n][:], (t_hi[i][:, k, :], t_lo[i][:, k, :]),
                                        [w[:, k, n * BANK:(n + 1) * BANK] for w in (w_hi, w_lo)], k == 0, k == KT - 1)
                        m.then_inc(multiplied, 1)
                        if n == 0:
                            turn_next()

                tiles(pe, turn, body)

            @block.scalar
            def _(act):
                def turn(tile, i, it):
                    for b in range(2):
                        act.wait_ge(turned_ready, tile * 2 + b + 1)
                        act.activation(t_hi[i][:, b * 4:b * 4 + 4, :], turned[b][:].rearrange("p (t q) -> p t q", q=P),
                                       ACT.Copy).then_inc(hi_ready, 1)

                def body(tile, i, it, turn_next):
                    turn_next()
                    act.wait_ge(mean_ready, tile + 1)
                    act.activation(stat[:, 2:3], stat[:, 1:2], ACT.Sqrt).then_inc(root_ready, 1)

                tiles(act, turn, body)

            @block.vector
            def _(dve):
                dve.sem_inc(normed, 2)
                dve.wait_ge(gains_loaded, 16)

                def turn(tile, i, it):
                    for b in range(2):
                        dve.wait_ge(hi_ready, tile * 2 + b + 1)
                        dve.tensor_tensor(t_lo[i][:, b * 4:b * 4 + 4, :],
                                          turned[b][:].rearrange("p (t q) -> p t q", q=P),
                                          t_hi[i][:, b * 4:b * 4 + 4, :].bitcast(F32), ALU.subtract).then_inc(split, 1)

                def body(tile, i, it, turn_next):
                    rows = B if isinstance(tile, int) else P
                    dve.wait_ge(stored[i], (it + 1) * 16)
                    dve.wait_ge(x_loaded[i], (it + 1) * 16)
                    for n in range(HALVES):
                        dve.wait_ge(multiplied, tile * 2 + n + 1)
                        dve.tensor_tensor(res[i][0:rows, n * BANK:(n + 1) * BANK], out[i * 2 + n][0:rows, :],
                                          x_in[i][0:rows, n * BANK:(n + 1) * BANK], ALU.add).then_inc(added, 1)
                        if n == 0:
                            turn_next()
                    dve.wait_ge(added, tile * 2 + 6)
                    dve.tensor_tensor_reduce(square[0:rows, :], res[i][0:rows, :], res[i][0:rows, :], 1.0, 0.0, ALU.mult,
                                             ALU.add, stat[0:rows, 0:1]).then_inc(step, 1)
                    dve.wait_ge(step, tile * 2 + 1)
                    dve.tensor_scalar(stat[0:rows, 1:2], stat[0:rows, 0:1], 1.0 / D, EPS, ALU.mult,
                                      ALU.add).then_inc(mean_ready, 1)
                    dve.wait_ge(root_ready, tile + 1)
                    dve.reciprocal(stat[0:rows, 3:4], stat[0:rows, 2:3]).then_inc(step, 1)
                    dve.wait_ge(step, tile * 2 + 2)
                    dve.scalar_tensor_tensor(out=res[i][0:rows, :], in0=res[i][0:rows, :], scalar=stat[0:rows, 3:4],
                                             in1=gains[0:rows, :], op0=ALU.mult, op1=ALU.mult).then_inc(normed, 1)
                    dve.wait_ge(normed, tile + 3)

                tiles(dve, turn, body)


def unpack_sample(nc, core, sample, s_raw, s_sigmoid, s_silu, fox_k_s, fox_v_s, gates, gated):
    with ExitStack() as ctx:
        part = [ctx.enter_context(nc.sbuf_tensor(f"up_part{i}", [P, W], F32)) for i in range(2)]
        sigmoid = ctx.enter_context(nc.sbuf_tensor("up_sigmoid", [P, W], F32))
        silu = ctx.enter_context(nc.sbuf_tensor("up_silu", [P, W], F32))
        zeros = ctx.enter_context(nc.sbuf_tensor("up_zeros", [P - B, W], F32))
        loaded, summed, sigmoid_ready, silu_ready, cleared, stored = (
            core.sem(f"up_{n}") for n in ("loaded", "summed", "sigmoid_ready", "silu_ready", "cleared", "stored"))
        with nc.Block() as block:
            @block.sync
            def _(sp):
                for i in range(2):
                    sp.dma_start(part[i][:], sample[:, i * B:(i + 1) * B, :]).then_inc(loaded, 16)
                sp.wait_ge(cleared, 1)
                n = 0
                for g in range(NGATE):
                    sp.dma_start(gates[g, T + B:T + P, :], zeros[:]).then_inc(stored, 16)
                for b in range(3):
                    sp.dma_start(gated[T + B:T + P, b * W:(b + 1) * W], zeros[:]).then_inc(stored, 16)
                n += NGATE + 3
                sp.wait_ge(summed, 1)
                sp.dma_start(s_raw, part[0][:]).then_inc(stored, 16)
                for name, dst in (("fk", fox_k_s), ("fv", fox_v_s)):
                    g = len(TURNED) + PLAIN.index(name)
                    sp.dma_start(dst, part[0][g * B:(g + 1) * B, :]).then_inc(stored, 16)
                sp.wait_ge(sigmoid_ready, 1)
                sp.dma_start(s_sigmoid, sigmoid[:]).then_inc(stored, 16)
                for g in range(NGATE):
                    at = (FIRST_GATE + g) * B
                    sp.dma_start(gates[g, T:T + B, :], sigmoid[at:at + B, :]).then_inc(stored, 16)
                sp.wait_ge(silu_ready, 1)
                sp.dma_start(s_silu, silu[:]).then_inc(stored, 16)
                n += 5 + NGATE
                sp.wait_ge(stored, n * 16)

            @block.gpsimd
            def _(pool):
                pool.memset(zeros[:], 0.0).then_inc(cleared, 1)

            @block.vector
            def _(dve):
                dve.wait_ge(loaded, 32)
                dve.tensor_tensor(part[0][:], part[0][:], part[1][:], ALU.add).then_inc(summed, 1)
                dve.wait_ge(sigmoid_ready, 1)
                dve.tensor_tensor(silu[:], part[0][:], sigmoid[:], ALU.mult).then_inc(silu_ready, 1)

            @block.scalar
            def _(act):
                act.wait_ge(summed, 1)
                act.activation(sigmoid[:], part[0][:], ACT.Sigmoid).then_inc(sigmoid_ready, 1)


class CacheAttention:

    def __init__(self, nc, core, ctx, tag, heads, pages, k_pages, v_pages, query, z_row, gated, table=None,
                 logf_pages=None, key_new=None, value_new=None, logf_new=None):
        self.nc, self.core, self.heads, self.pages = nc, core, heads, pages
        self.k_pages, self.v_pages, self.query, self.z_row, self.gated = k_pages, v_pages, query, z_row, gated
        self.table_dram, self.logf_pages, self.news = table, logf_pages, (key_new, value_new, logf_new)
        self.dim = W // heads
        self.scale = self.dim ** -0.5
        self.GP = min(4, pages)
        self.GB = pages // self.GP
        self.SLOTS = 4
        self.RB = self.SLOTS // self.GB
        self.ROUNDS = B // self.RB
        self.GROUPS = B * self.GB
        self.paged = table is not None

        def sb(name, shape, dt=F32):
            return ctx.enter_context(nc.sbuf_tensor(f"{tag}_{name}", shape, dt))

        def psum(name, shape):
            return ctx.enter_context(nc.psum_tensor(f"{tag}_{name}", shape, F32))

        def sem(name):
            return core.sem(f"{tag}_{name}")

        self.slot = [sb(f"slot{s}", [P, self.GP, W]) for s in range(self.SLOTS)]
        self.q_all = sb("q_all", [P, B, W])
        self.scores = sb("scores", [P, B, pages, heads])
        self.most, self.sums = sb("most", [P, B, heads]), sb("sums", [P, B, heads])
        self.bias, self.spread = sb("bias", [B, heads]), sb("spread", [B, B, heads])
        self.most_b, self.total, self.inverse = (sb(n, [B, heads]) for n in ("most_b", "total", "inverse"))
        self.probs = [sb(f"probs{s}", [P, self.GP, heads]) for s in range(self.SLOTS)]
        self.row = [sb(f"row{i}", [B, W]) for i in range(2)]
        self.ones = sb("ones", [P, P])
        self.o, self.z = sb("o", [B, W]), self.row[1]
        self.o_dram = nc.dram_tensor(f"{tag}_o_rows", (B, heads * (W + self.dim)), F32, kind="Internal").ap()
        self.primer = nc.dram_tensor(f"{tag}_primer", (2, P), F32, kind="Internal").ap()
        self.wide = psum("wide", [P, 2, BANK])
        flat = self.wide[:].rearrange("p i n -> p (i n)")[:, 0:heads * P]
        self.back_bias = flat.rearrange("p (h n) -> p h n", n=P)
        self.most_t = flat[0:B].rearrange("p (h n) -> p h n", n=P)
        small = psum("small", [P, B + 2, heads])
        self.spread_all, self.small, self.suffix_all = small[:, 0:B, :], small[0:B, B, :], small[:, B + 1, :]
        if self.paged:
            self.table_sb, self.rows_sb = sb("table", [1, B * pages], I32), sb("rows", [P, 1], I32)
            self.logf, self.run = sb("logf", [P, PAGE, heads]), sb("run", [P, heads, PAGE])
            self.later, self.suffix = sb("later", [P, P]), sb("suffix", [P, heads])
            self.q_b, self.k_b = self.o, sb("k_b", [B, W])
            self.v_b, self.product_b = self.k_b, self.row[0]
            self.gate_b, self.s_new, self.p_new = (sb(n, [B, heads]) for n in ("gate_b", "s_new", "p_new"))

        self.ready = [sem(f"loaded{s}") for s in range(self.SLOTS)]
        self.slot_free = sem("slot_free")
        self.start_loaded, self.rows_loaded, self.new_loaded, self.logf_loaded, self.z_loaded = (
            sem(n) for n in ("start_loaded", "rows_loaded", "new_loaded", "logf_loaded", "z_loaded"))
        self.consts, self.pool_step, self.step, self.paced = (sem(n) for n in ("consts", "pool_step", "step", "paced"))
        self.multiplied = {"dve": sem("multiplied_dve"), "pool": sem("multiplied_pool")}
        self.run_ready, self.suffix_ready, self.bias_turned, self.back_ready = (
            sem(n) for n in ("run_ready", "suffix_ready", "bias_turned", "back_ready"))
        self.most_ready, self.most_turned, self.spread_ready, self.spread_done = (
            sem(n) for n in ("most_ready", "most_turned", "spread_ready", "spread_done"))
        self.new_asked, self.new_ready, self.exp_asked, self.exp_ready, self.sums_ready, self.sums_done = (
            sem(n) for n in ("new_asked", "new_ready", "exp_asked", "exp_ready", "sums_ready", "sums_done"))
        self.probs_ready = sem("probs_ready")
        self.row_copied = sem("row_copied")
        self.row_stored = [sem(f"row_stored{i}") for i in range(2)]
        self.o_loaded, self.done, self.stored = sem("o_loaded"), sem("done"), sem("stored")

    def sync_start(self, sp):
        nc = self.nc
        sp.sem_inc(self.slot_free, self.SLOTS)
        if self.paged:
            sp.dma_start(self.table_sb[:], self.table_dram.rearrange("b (o g) -> o (b g)", o=1)
                         ).then_inc(self.rows_loaded, 16)
            with nc.allow_non_contiguous_dma(reason="a table of 128 pages, one in a partition"):
                sp.dma_start(self.rows_sb[:], self.table_dram.rearrange("b (g o) -> (b g) o", o=1)
                             ).then_inc(self.rows_loaded, 16)
            sp.wait_ge(self.rows_loaded, 32)
        sp.dma_start(self.q_all[:], self.query.partition_broadcast(P)).then_inc(self.start_loaded, 16)
        if self.paged:
            key_new, _, logf_new = self.news
            for dst, src in ((self.q_b, self.query), (self.k_b, key_new), (self.gate_b, logf_new)):
                sp.dma_start(dst[:], src).then_inc(self.new_loaded, 16)

    def load_group(self, sp, source, first, it, s):
        group = it * self.SLOTS + s
        sp.wait_ge(self.slot_free, group + first + 1)
        for p in range(self.GP):
            n = group * self.GP + p
            page = sp.value_load(self.table_sb[0:1, bass.ds(n, 1)], min_val=0,
                                 max_val=source.shape[0] - 1) if self.paged else n
            sp.dma_start(self.slot[s][:, p, :], source[bass.ds(page, 1)].rearrange("o p n -> (o p) n")
                         ).then_inc(self.ready[s], 16)

    def sync_end(self, sp):
        for i in range(2):
            sp.wait_ge(self.row_stored[i], (B // 2 + 1) * 16)
        sp.dma_start(self.z[:], self.z_row).then_inc(self.z_loaded, 16)
        if self.paged:
            sp.dma_start(self.v_b[:], self.news[1]).then_inc(self.new_loaded, 16)
        own = self.o_dram.rearrange("b (h x) -> b h x", h=self.heads)[:, :, 0:self.dim]
        sp.dma_start(self.o[:].rearrange("b (h d) -> b h d", h=self.heads), own).then_inc(self.o_loaded, 16)
        sp.wait_ge(self.done, 1)
        sp.dma_start(self.gated, self.o[:]).then_inc(self.stored, 16)
        sp.wait_ge(self.stored, 16)

    def pool_start(self, pool):
        link = linker(pool, self.pool_step)
        for i in range(2):
            pool.dma_start(self.primer[i:i + 1, :], self.core.ident[0:1, :]).then_inc(self.row_stored[i], 16)
        link(pool.memset(self.ones[:], 1.0))
        if self.paged:
            pages = self.pages
            link(pool.memset(self.later[:], 1.0))
            by_row = self.later[:].rearrange("x (b g) -> x b g", g=pages)
            link(pool.affine_select(out=by_row, in_=by_row, compare_op=ALU.is_ge, fill=0.0, base=0,
                                    pattern=[[-pages, B], [-1, pages]], channel_multiplier=1))
            link(pool.affine_select(out=by_row, in_=by_row, compare_op=ALU.is_ge, fill=0.0, base=pages - 1,
                                    pattern=[[pages, B], [0, pages]], channel_multiplier=-1))
            pool.wait_ge(self.rows_loaded, 32)
            pool.indirect_dma_start(out=self.logf[:].rearrange("p t h -> p (t h)"), out_offset=None,
                                    in_=self.logf_pages.rearrange("n t h -> n (t h)"),
                                    in_offset=bass.IndirectOffsetOnAxis(ap=self.rows_sb[:, 0:1], axis=0)
                                    ).then_inc(self.logf_loaded, 16)
        pool.sem_inc(self.consts, 1)
        pool.wait_ge(self.start_loaded, 16)

    def multiply(self, eng, name, it, s):
        at = self.q_all[:, bass.ds(it * self.RB + s // self.GB, 1), :].to_broadcast([P, self.GP, W])
        eng.wait_ge(self.ready[s], (it + 1) * 16 * self.GP)
        eng.sem_inc(self.paced, 1)
        eng.tensor_tensor(self.slot[s][:], self.slot[s][:], at, ALU.mult).then_inc(self.multiplied[name], 1)

    def pool_keys(self, pool, it, s):
        if s > 0:
            self.multiply(pool, "pool", it, s)

    def store_row(self, pool, b, i):
        pool.wait_ge(self.row_copied, b + 3)
        pool.dma_start(self.o_dram[bass.ds(b, 1), 0:self.heads * W].rearrange("o (h n) -> (o h) n", n=W),
                       self.row[i][0:self.heads]).then_inc(self.row_stored[i], 16)

    def vector_start(self, dve):
        self.link = link = linker(dve, self.step)
        dve.wait_ge(self.consts, 1)
        if self.paged:
            dve.wait_ge(self.logf_loaded, 16)
            for h in range(self.heads):
                last = dve.tensor_tensor_scan(self.run[:, h, :], self.ones[:], self.logf[:, :, h], 0.0, ALU.mult,
                                              ALU.add)
            last.then_inc(self.run_ready, 1)
            dve.wait_ge(self.suffix_ready, 1)
            link(dve.tensor_copy(self.suffix[:], self.suffix_all))
            dve.tensor_tensor(self.run[:], self.suffix[:].unsqueeze(2).to_broadcast([P, self.heads, PAGE]),
                              self.run[:], ALU.subtract).then_inc(self.bias_turned, 1)
        dve.wait_ge(self.start_loaded, 16)

    def vector_keys(self, dve, it, s):
        r, g, GP = s // self.GB, s % self.GB, self.GP
        if s == 0:
            self.multiply(dve, "dve", it, s)
            dve.wait_ge(self.multiplied["dve"], it + 1)
        else:
            dve.wait_ge(self.multiplied["pool"], it * (self.SLOTS - 1) + s)
        dve.tensor_reduce(self.scores[:, bass.ds(it * self.RB + r, 1), g * GP:(g + 1) * GP, :]
                          .rearrange("p o g h -> p (o g) h"),
                          self.slot[s][:].rearrange("p g (h d) -> p g h d", d=self.dim), AX.X,
                          ALU.add).then_inc(self.slot_free, 1)

    def vector_middle(self, dve):
        link, scores, heads, pages = self.link, self.scores, self.heads, self.pages
        dve.wait_ge(self.slot_free, self.GROUPS + self.SLOTS)
        flat = scores[:].rearrange("p b g h -> p (b g) h")
        if self.paged:
            dve.wait_ge(self.back_ready, 1)
            link(dve.scalar_tensor_tensor(out=flat, in0=flat, scalar=self.scale,
                                          in1=self.back_bias.rearrange("p h n -> p n h"), op0=ALU.mult, op1=ALU.add))
        else:
            link(dve.tensor_scalar(flat, flat, self.scale, None, ALU.mult))
        dve.tensor_reduce(self.most[:], scores[:].rearrange("p b g h -> p b h g"), AX.X, ALU.max
                          ).then_inc(self.most_ready, 1)
        if self.paged:
            dve.wait_ge(self.new_loaded, 48)
            link(dve.tensor_tensor(self.product_b[:], self.q_b[:], self.k_b[:], ALU.mult))
            link(dve.tensor_reduce(self.s_new[:], self.product_b[:].rearrange("b (h d) -> b h d", d=self.dim), AX.X,
                                   ALU.add))
            link(dve.tensor_scalar(self.s_new[:], self.s_new[:], self.scale, None, ALU.mult))
        dve.wait_ge(self.most_turned, 1)
        link(dve.tensor_reduce(self.most_b[:], self.most_t, AX.X, ALU.max))
        if self.paged:
            link(dve.tensor_tensor(self.most_b[:], self.most_b[:], self.gate_b[:], ALU.add))
            link(dve.tensor_tensor(self.most_b[:], self.most_b[:], self.s_new[:], ALU.max))
            link(dve.tensor_tensor(self.bias[:], self.gate_b[:], self.most_b[:], ALU.subtract))
            link(dve.tensor_tensor(self.s_new[:], self.s_new[:], self.most_b[:], ALU.subtract))
            dve.sem_inc(self.new_asked, 1)
        else:
            link(dve.tensor_scalar(self.bias[:], self.most_b[:], -1.0, None, ALU.mult))
        dve.tensor_tensor(self.spread[:], self.core.ident[0:B, 0:B].unsqueeze(2).to_broadcast([B, B, heads]),
                          self.bias[:].unsqueeze(1).to_broadcast([B, B, heads]), ALU.mult
                          ).then_inc(self.spread_ready, 1)
        dve.wait_ge(self.spread_done, 1)
        dve.wait_ge(self.most_turned, 1)
        dve.tensor_tensor(scores[:], scores[:], self.spread_all.unsqueeze(2).to_broadcast([P, B, pages, heads]),
                          ALU.add).then_inc(self.exp_asked, 1)
        dve.wait_ge(self.exp_ready, 1)
        dve.tensor_reduce(self.sums[:], scores[:].rearrange("p b g h -> p b h g"), AX.X, ALU.add
                          ).then_inc(self.sums_ready, 1)
        dve.wait_ge(self.sums_done, 1)
        if self.paged:
            dve.wait_ge(self.new_ready, 1)
            link(dve.tensor_tensor(self.total[:], self.small, self.p_new[:], ALU.add))
        else:
            link(dve.tensor_copy(self.total[:], self.small))
        link(dve.reciprocal(self.inverse[:], self.total[:]))
        dve.sem_inc(self.row_copied, 2)

    def copy_row(self, dve, b, i, use):
        dve.wait_ge(self.slot_free, (b + 1) * self.GB + self.GROUPS + self.SLOTS)
        dve.wait_ge(self.row_stored[i], (use + 1) * 16)
        dve.tensor_copy(self.row[i][0:self.heads], self.wide[0:self.heads, i, :]).then_inc(self.row_copied, 1)

    def vector_end(self, dve):
        link = self.link
        dve.wait_ge(self.o_loaded, 16)
        by_head = self.o[:].rearrange("b (h d) -> b h d", d=self.dim)
        if self.paged:
            dve.wait_ge(self.new_loaded, 64)
            link(dve.tensor_tensor(self.product_b[:].rearrange("b (h d) -> b h d", d=self.dim),
                                   self.v_b[:].rearrange("b (h d) -> b h d", d=self.dim),
                                   self.p_new[:].unsqueeze(2).to_broadcast([B, self.heads, self.dim]), ALU.mult))
            link(dve.tensor_tensor(self.o[:], self.o[:], self.product_b[:], ALU.add))
        link(dve.tensor_tensor(by_head, by_head,
                               self.inverse[:].unsqueeze(2).to_broadcast([B, self.heads, self.dim]), ALU.mult))
        dve.wait_ge(self.z_loaded, 16)
        dve.tensor_tensor(self.o[:], self.o[:], self.z[:], ALU.mult).then_inc(self.done, 1)

    def scalar_middle(self, act):
        if self.paged:
            act.wait_ge(self.new_asked, 1)
            act.activation(self.p_new[:], self.s_new[:], ACT.Exp).then_inc(self.new_ready, 1)
        act.wait_ge(self.exp_asked, 1)
        act.activation(self.scores[:], self.scores[:], ACT.Exp).then_inc(self.exp_ready, 1)
        act.wait_ge(self.exp_ready, 1)

    def scalar_values(self, act, it, s):
        r, g, GP = s // self.GB, s % self.GB, self.GP
        act.wait_ge(self.slot_free, it * self.SLOTS + s + self.GROUPS + 1)
        act.activation(self.probs[s][:], self.scores[:, bass.ds(it * self.RB + r, 1), g * GP:(g + 1) * GP, :]
                       .rearrange("p o g h -> p (o g) h"), ACT.Copy).then_inc(self.probs_ready, 1)

    def tensor_start(self, pe):
        pe.wait_ge(self.consts, 1)
        if self.paged:
            pe.wait_ge(self.run_ready, 1)
            pe.matmul(self.suffix_all, self.later[:], self.run[:, :, PAGE - 1], start=True, stop=True
                      ).then_inc(self.suffix_ready, 1)
            pe.wait_ge(self.bias_turned, 1)
            for h in range(self.heads):
                m = pe.transpose(self.back_bias[:, h, :], self.run[:, h, :], self.core.ident[:])
            m.then_inc(self.back_ready, 1)

    def tensor_middle(self, pe):
        pe.wait_ge(self.most_ready, 1)
        for h in range(self.heads):
            m = pe.transpose(self.most_t[:, h, :], self.most[:, :, h], self.core.ident[:])
        m.then_inc(self.most_turned, 1)
        pe.wait_ge(self.spread_ready, 1)
        pe.matmul(self.spread_all.rearrange("p b h -> p (b h)"), self.ones[0:B, :],
                  self.spread[:].rearrange("c b h -> c (b h)"), start=True, stop=True).then_inc(self.spread_done, 1)
        pe.wait_ge(self.sums_ready, 1)
        for h in range(self.heads):
            m = pe.matmul(self.small[:, h:h + 1], self.sums[:, :, h], self.ones[:, 0:1], start=True, stop=True)
        m.then_inc(self.sums_done, 1)

    def tensor_values(self, pe, it, s, i):
        g = s % self.GB
        if g == 0:
            pe.wait_ge(self.row_copied, it * self.RB + s // self.GB + 1)
        pe.wait_ge(self.probs_ready, it * self.SLOTS + s + 1)
        pe.wait_ge(self.ready[s], (it + 1 + self.ROUNDS) * 16 * self.GP)
        for p in range(self.GP):
            m = pe.matmul(self.wide[0:self.heads, i, :], self.probs[s][:, p, :], self.slot[s][:, p, :],
                          start=(g == 0 and p == 0), stop=(g == self.GB - 1 and p == self.GP - 1))
        m.then_inc(self.slot_free, 1)


def attend_cache(nc, core, *arguments):
    with ExitStack() as ctx:
        a = CacheAttention(nc, core, ctx, *arguments)
        with nc.Block() as block:
            @block.sync
            def _(sp):
                a.sync_start(sp)
                for source, first in ((a.k_pages, 0), (a.v_pages, a.GROUPS)):
                    with sp.Fori(0, a.ROUNDS) as it:
                        for s in range(a.SLOTS):
                            a.load_group(sp, source, first, it, s)
                a.sync_end(sp)

            @block.gpsimd
            def _(pool):
                a.pool_start(pool)
                with pool.Fori(0, a.ROUNDS) as it:
                    for s in range(a.SLOTS):
                        a.pool_keys(pool, it, s)
                with pool.Fori(0, a.ROUNDS) as it:
                    for s in range(a.SLOTS):
                        a.store_row(pool, it * a.RB + s, s % 2)

            @block.vector
            def _(dve):
                a.vector_start(dve)
                with dve.Fori(0, a.ROUNDS) as it:
                    for s in range(a.SLOTS):
                        a.vector_keys(dve, it, s)
                a.vector_middle(dve)
                with dve.Fori(0, a.ROUNDS) as it:
                    for s in range(a.SLOTS):
                        a.copy_row(dve, it * a.RB + s, s % 2, it * (a.RB // 2) + s // 2)
                a.vector_end(dve)

            @block.scalar
            def _(act):
                a.scalar_middle(act)
                with act.Fori(0, a.ROUNDS) as it:
                    for s in range(a.SLOTS):
                        a.scalar_values(act, it, s)

            @block.tensor
            def _(pe):
                a.tensor_start(pe)
                a.tensor_middle(pe)
                with pe.Fori(0, a.ROUNDS) as it:
                    for s in range(a.SLOTS):
                        a.tensor_values(pe, it, s, s % 2)


def recur_sample(nc, core, sigmoid, query, values, z_row, state_in, gain, gated, state_out):
    with ExitStack() as ctx:
        def sb(name, shape):
            return ctx.enter_context(nc.sbuf_tensor(f"rs_{name}", shape, F32))

        sg, q = sb("sg", [B, W]), sb("q", [B, W])
        f_t, k_t, q_t = sb("f_t", [P, HH, B]), sb("k_t", [P, HH, B]), sb("q_t", [P, HH, B])
        state, v, kv = [sb(f"state{i}", [P, HH, P]) for i in range(2)], [sb(f"v{i}", [P, HH, P]) for i in range(2)], \
            [sb(f"kv{i}", [P, HH, P]) for i in range(2)]
        o_t, o, square = sb("o_t", [P, HH, B]), sb("o", [B, W]), sb("square", [B, W])
        z, gains, stat = sb("z", [B, W]), sb("gains", [B, W]), sb("stat", [B, 3, HH])
        turned = ctx.enter_context(nc.psum_tensor("rs_turned", [P, 2, HH, B], F32))
        out = [ctx.enter_context(nc.psum_tensor(f"rs_out{i}", [P, HH, B], F32)) for i in range(2)]
        back = ctx.enter_context(nc.psum_tensor("rs_back", [B, W], F32))
        primer = nc.dram_tensor("rs_primer", (2, P), F32, kind="Internal").ap()

        def sem(name):
            return core.sem(f"rs_{name}")

        loaded, small_loaded, turned_ready, step = sem("loaded"), sem("small_loaded"), sem("turned_ready"), sem("step")
        state_loaded, stored = [sem(f"state_loaded{i}") for i in range(2)], [sem(f"stored{i}") for i in range(2)]
        used = sem("used")
        ready, kv_ready, out_ready, taken = sem("ready"), sem("kv_ready"), sem("out_ready"), sem("taken")
        back_ready, mean_ready, root_ready, done, o_stored, faded = sem("back_ready"), sem("mean_ready"), \
            sem("root_ready"), sem("done"), sem("o_stored"), sem("faded")

        with nc.Block() as block:
            @block.sync
            def _(sp):
                sp.dma_start(sg[:], sigmoid).then_inc(loaded, 16)
                sp.dma_start(q[:], query).then_inc(loaded, 16)
                sp.dma_start(z[:], z_row).then_inc(small_loaded, 16)
                sp.dma_start(gains[:], gain.partition_broadcast(B)).then_inc(small_loaded, 16)
                for i in range(2):
                    sp.dma_start(primer[i:i + 1, :], core.ident[0:1, :]).then_inc(stored[i], 16)
                with sp.Fori(0, B // 2) as it:
                    for i in range(2):
                        b = it * 2 + i
                        sp.wait_ge(taken, b + 1)
                        sp.wait_ge(stored[i], (it + 1) * 16)
                        sp.dma_start(state[i][:], state_in[bass.ds(b, 1)].rearrange("o h k v -> k (o h) v")
                                     ).then_inc(state_loaded[i], 16)
                        sp.dma_start(v[i][:], values[bass.ds(b, 1), :].to_broadcast([P, W])
                                     .rearrange("p (h d) -> p h d", h=HH)).then_inc(state_loaded[i], 16)
                    for i in range(2):
                        b = it * 2 + i
                        sp.wait_ge(ready, b + 1)
                        sp.dma_start(state_out[bass.ds(b, 1)].rearrange("o h k v -> k (o h) v"), state[i][:]
                                     ).then_inc(stored[i], 16)
                sp.wait_ge(done, 1)
                sp.dma_start(gated, o[:]).then_inc(o_stored, 16)
                sp.wait_ge(o_stored, 16)
                for i in range(2):
                    sp.wait_ge(stored[i], (B // 2 + 1) * 16)

            @block.tensor
            def _(pe):
                pe.wait_ge(loaded, 32)
                for n, src in enumerate((sg, q)):
                    for h in range(HH):
                        m = pe.transpose(turned[:, n, h, :], src[:, h * P:(h + 1) * P], core.ident[0:B, 0:B])
                m.then_inc(turned_ready, 1)
                pe.wait_ge(step, 2 + 2 * HH)
                with pe.Fori(0, B // 2) as it:
                    for i in range(2):
                        b = it * 2 + i
                        pe.wait_ge(ready, b + 1)
                        pe.wait_ge(taken, b + 1)
                        for h in range(HH):
                            m = pe.matmul(out[i][:, h, :], state[i][:, h, :], q_t[:, h, :], start=True, stop=True)
                        m.then_inc(out_ready, 1)
                pe.wait_ge(taken, B + 2)
                for h in range(HH):
                    m = pe.transpose(back[:, h * P:(h + 1) * P], o_t[:, h, :], core.ident[:])
                m.then_inc(back_ready, 1)

            @block.vector
            def _(dve):
                link = linker(dve, step)
                dve.wait_ge(turned_ready, 1)
                link(dve.tensor_copy(q_t[:], turned[:, 1]))
                for h in range(HH):
                    link(dve.tensor_scalar(f_t[:, h, :], turned[:, 0, h, :], core.rest[:, h:h + 1],
                                           core.bound[:, h:h + 1], ALU.mult, ALU.add))
                    link(dve.tensor_scalar(k_t[:, h, :], f_t[:, h, :], -1.0, 1.0, ALU.mult, ALU.add))
                dve.sem_inc(step, 1)
                link.done[0] += 1
                with dve.Fori(0, B // 2) as it:
                    for i in range(2):
                        b = it * 2 + i
                        dve.wait_ge(state_loaded[i], (it + 1) * 32)
                        dve.tensor_tensor(kv[i][:], v[i][:], k_t[:, :, bass.ds(b, 1)].to_broadcast([P, HH, P]),
                                          ALU.mult).then_inc(kv_ready, 1)
                        dve.tensor_tensor(state[i][:], state[i][:], f_t[:, :, bass.ds(b, 1)].to_broadcast([P, HH, P]),
                                          ALU.mult).then_inc(faded, 1)
                        dve.wait_ge(faded, b + 1)
                        dve.wait_ge(kv_ready, b + 1)
                        dve.tensor_tensor(state[i][:], state[i][:], kv[i][:], ALU.add).then_inc(ready, 1)
                dve.wait_ge(back_ready, 1)
                heads = [t[:].rearrange("b (h d) -> b h d", h=HH) for t in (o, square)]
                link(dve.tensor_copy(o[:], back[:]))
                link(dve.tensor_tensor(square[:], o[:], o[:], ALU.mult))
                link(dve.tensor_reduce(stat[:, 0, :], heads[1], AX.X, ALU.add))
                dve.tensor_scalar(stat[:, 1, :], stat[:, 0, :], 1.0 / HD, EPS, ALU.mult, ALU.add).then_inc(mean_ready, 1)
                dve.wait_ge(root_ready, 1)
                link(dve.reciprocal(stat[:, 2, :], stat[:, 1, :]))
                link(dve.tensor_tensor(heads[0], heads[0], stat[:, 2, :].unsqueeze(2).to_broadcast([B, HH, HD]),
                                       ALU.mult))
                dve.wait_ge(small_loaded, 32)
                link(dve.tensor_tensor(o[:], o[:], gains[:], ALU.mult))
                dve.tensor_tensor(o[:], o[:], z[:], ALU.mult).then_inc(done, 1)

            @block.scalar
            def _(act):
                act.sem_inc(taken, 2)
                with act.Fori(0, B // 2) as it:
                    for i in range(2):
                        b = it * 2 + i
                        act.wait_ge(out_ready, b + 1)
                        act.activation(o_t[:, :, bass.ds(b, 1)], out[i][:, :, bass.ds(b, 1)], ACT.Copy
                                       ).then_inc(taken, 1)
                act.wait_ge(mean_ready, 1)
                act.activation(stat[:, 1, :], stat[:, 1, :], ACT.Sqrt).then_inc(root_ready, 1)


def decoder_step(nc, x_prompt, x_sample, mem_prompt, cache_fox_k, cache_fox_v, cache_fox_logf, page_table, state_hgrn,
                 cache_mem_k, cache_mem_v, norm_g, w_in, b_fgate, hg_norm_g, lb_param, mem_norm_g, w_mk, w_mv, w_pa,
                 w_pb, w_pm, w_o, final_norm_g, y_prompt, y_sample, fox_k_prompt, fox_v_prompt, fox_logf_prompt,
                 state_prompt, mem_k_prompt, mem_v_prompt, fox_k_sample, fox_v_sample, fox_logf_sample, state_sample):
    def dram(name, shape):
        return nc.dram_tensor(name, shape, F32, kind="Internal").ap()

    rows = NT * P + P
    turned, plain = dram("turned", (len(TURNED), W, T)), dram("plain", (len(PN) - 1 + NGATE, rows, W))
    sample, neg_c = dram("sample", (NGROUP, 2 * B, W)), dram("neg_c", (FH, T))
    s_raw, s_sigmoid, s_silu = (dram(n, (NGROUP * B, W)) for n in ("s_raw", "s_sigmoid", "s_silu"))
    gated, mixed = dram("gated", (rows, 3 * W)), dram("mixed", (rows, D))
    gates = plain[PN["gate"]:PN["gate"] + NGATE]

    fox_k, fox_v = (t[0, 0].rearrange("t h d -> t (h d)") for t in (fox_k_prompt, fox_v_prompt))
    mem_k, mem_v = (t[0, 0].rearrange("t h d -> t (h d)") for t in (mem_k_prompt, mem_v_prompt))
    fox_k_s, fox_v_s = (t[0].rearrange("b o h d -> (b o) (h d)") for t in (fox_k_sample, fox_v_sample))
    logf_s = fox_logf_sample[0].rearrange("b o h -> (b o) h")
    k_pages, v_pages = (t[0].rearrange("n t h d -> n t (h d)") for t in (cache_fox_k, cache_fox_v))
    mem_k_pages, mem_v_pages = (t[0].rearrange("b (g t) h d -> (b g) t (h d)", t=PAGE)
                                for t in (cache_mem_k, cache_mem_v))
    x, x_s = x_prompt[0], x_sample.rearrange("b o d -> (b o) d")
    hg_gain = hg_norm_g[0]

    def of(group, spilled):
        at = (TURNED + PLAIN).index(group) * B
        return spilled[at:at + B, :]

    with ExitStack() as ctx:
        core = Core(nc, ctx)
        constants(nc, core)
        with nc.cleanup_on_exit():
            with ExitStack() as inner:
                mem_hi, mem_lo = (inner.enter_context(nc.sbuf_tensor(n, [P, KT, NM], F32R)) for n in ("mem_hi", "mem_lo"))
                normalise_rows(nc, core, "tokens", mem_prompt[0], mem_norm_g[0], mem_hi, mem_lo, NM // P, P, 2)
                project_memory(nc, core, mem_hi, mem_lo, [w_mk[0], w_mv[0]], [mem_k, mem_v])
            with ExitStack() as inner:
                x_hi, x_lo = (inner.enter_context(nc.sbuf_tensor(n, [P, KT, T], F32R)) for n in ("x_hi", "x_lo"))
                xs = inner.enter_context(nc.sbuf_tensor("xs_both", [P, KT, SAMPLE_COLUMNS], F32R))
                xs_hi, xs_lo = xs[:, :, 0:B], xs[:, :, B:2 * B]
                normalise_rows(nc, core, "x", x, norm_g[0], x_hi, x_lo, NT, P, 4)
                clear(nc, core, xs)
                normalise_rows(nc, core, "xs", x_s, norm_g[0], xs_hi, xs_lo, 1, B, 1)
                forget_gates(nc, core, x_hi, x_lo, xs_hi, xs_lo, w_in[0][:, COL["ff"]:COL["ff"] + FH], b_fgate[0],
                             fox_logf_prompt[0, 0], logf_s, neg_c)
                project_inputs(nc, core, x_hi, x_lo, xs, w_in[0], turned, plain, fox_k, fox_v, sample)
        with nc.cleanup_on_exit():
            unpack_sample(nc, core, sample, s_raw, s_sigmoid, s_silu, fox_k_s, fox_v_s, gates, gated)
            attend_cache(nc, core, "mem_cache", HH, NM // PAGE, mem_k_pages, mem_v_pages, of("mq", s_raw),
                         of("mz", s_silu), gated[T:T + B, 2 * W:3 * W])
            attend_prompt(nc, core, turned[PT["fq"]], fox_k, fox_v, plain[PN["fz"]][0:T, :], neg_c, gated[0:T, 0:W])
        lower_bound(nc, core, lb_param)
        recur_sample(nc, core, of("hf", s_sigmoid), of("hq", s_silu), of("hi", s_raw), of("hz", s_silu),
                     state_hgrn[0], hg_gain, gated[T:T + B, W:2 * W], state_sample[0])
        recur_prompt(nc, core, turned[PT["hq"]], turned[PT["hf"]], plain[PN["hi"]][0:T, :], plain[PN["hz"]][0:T, :],
                     hg_gain, gated[0:T, W:2 * W], state_prompt[0, 0],
                     ("paged", FH, T // PAGE, k_pages, v_pages, of("fq", s_raw), of("fz", s_silu), gated[T:T + B, 0:W],
                      page_table, cache_fox_logf[0], of("fk", s_raw), of("fv", s_raw), logf_s))
        attend_memory(nc, core, turned[PT["mq"]], mem_k, mem_v, plain[PN["mz"]][0:T, :], gated[0:T, 2 * W:3 * W])
        merge_branches(nc, core, gated, gates, [w_pa[0], w_pb[0], w_pm[0]], mixed)
        finish_rows(nc, core, mixed, w_o[0], x, x_s, final_norm_g, y_prompt[0],
                    y_sample.rearrange("b o d -> (b o) d"))


_INS = ["x_prompt", "x_sample", "mem_prompt", "cache_fox_k", "cache_fox_v", "cache_fox_logf", "page_table",
        "state_hgrn", "cache_mem_k", "cache_mem_v", "norm_g", "w_in", "b_fgate", "hg_norm_g", "lb_param", "mem_norm_g",
        "w_mk", "w_mv", "w_pa", "w_pb", "w_pm", "w_o", "final_norm_g"]
_OUTS = [(1, 2048, 1024), (8, 1, 1024), (1, 1, 2048, 8, 64), (1, 1, 2048, 8, 64), (1, 1, 2048, 8),
         (1, 1, 4, 128, 128), (1, 1, 256, 4, 128), (1, 1, 256, 4, 128), (1, 8, 1, 8, 64), (1, 8, 1, 8, 64),
         (1, 8, 1, 8), (1, 8, 4, 128, 128)]


def kernel(**inputs):
    import numpy as _np
    import concourse.bacc as _bacc
    from concourse import mybir as _mybir
    from concourse.bass_utils import run_bass_kernel_spmd as _run

    nc = _bacc.Bacc("TRN2", target_bir_lowering=False, num_devices=1)
    arrays, args = {}, []
    for name in _INS:
        a = _np.ascontiguousarray(inputs[name])
        arrays[f"in_{name}_dram"] = a
        args.append(nc.dram_tensor(f"in_{name}_dram", a.shape, _mybir.dt.from_np(a.dtype), kind="ExternalInput").ap())
    for i, shape in enumerate(_OUTS):
        args.append(nc.dram_tensor(f"out_{i}_dram", shape, _mybir.dt.float32, kind="ExternalOutput").ap())
    decoder_step(nc, *args)
    r = _run(nc, [arrays], core_ids=[0])
    return tuple(r.results[0][f"out_{i}_dram"] for i in range(len(_OUTS)))
```
